# Optimizing a Trainium2 kernel written in Bass

```python
import math
import jax
import jax.numpy as jnp
from jax import lax
import numpy as np

D_MODEL = 1024
BATCH = 1
SEQ = 128
DEPTH = 2
DEC_BATCH = 1
DEC_SEQ = 512
PAST_LEN = 128

GRID_W = 64
HEAD_DIM = 64
BLOCK = 128
N_AB = (DEPTH + 1) // 2
N_C = DEPTH // 2
A_HEADS = 8
A_KV_HEADS = 2
A_GROUP = A_HEADS // A_KV_HEADS
WINDOW = 128
A_COLS = (A_HEADS + 2 * A_KV_HEADS) * HEAD_DIM
B_HEADS = 8
B_WIDTH = B_HEADS * HEAD_DIM
DECAY_LORA = 64
AAA_LORA = 64
GATE_LORA = 128
B_COLS = 3 * B_WIDTH + 2 * DECAY_LORA + 2 * AAA_LORA + GATE_LORA
AB_COLS = A_COLS + B_COLS
C_HEADS = 8
C_VDIM = 2 * HEAD_DIM
C_COLS = 3 * C_HEADS * C_VDIM
D_FF = 2816
N_MOD = 9
ROPE_THETA = 10000.0
NORM_EPS = 1e-6
GN_EPS = 64e-5
SUBLN_EPS = 1e-5

kernel_name = "hybrid_diffusion_trunk_step"

def _split(x, sizes):
    idx = np.cumsum(sizes)[:-1].tolist()
    return jnp.split(x, idx, axis=-1)

def _rmsnorm(x, g):
    xf = x.astype(jnp.float32)
    y = xf * lax.rsqrt(jnp.mean(xf * xf, axis=-1, keepdims=True) + NORM_EPS)
    return (y * g.astype(jnp.float32)).astype(x.dtype)

def _swiglu(h, w1, w3, w2):
    return (jax.nn.silu(h @ w1) * (h @ w3)) @ w2

def _axial_rope(n_tok):
    n_rows = n_tok // GRID_W
    row = jnp.repeat(jnp.arange(n_rows, dtype=jnp.float32), GRID_W)
    col = jnp.tile(jnp.arange(GRID_W, dtype=jnp.float32), n_rows)
    n_freq = HEAD_DIM // 4
    inv = jnp.power(ROPE_THETA, -jnp.arange(n_freq, dtype=jnp.float32) / n_freq)
    ang_r = (row[:, None] * inv)[:, None, :]
    ang_c = (col[:, None] * inv)[:, None, :]
    return (jnp.cos(ang_r), jnp.sin(ang_r), jnp.cos(ang_c), jnp.sin(ang_c))

def _rotate(x, cos, sin):
    x1, x2 = jnp.split(x, 2, axis=-1)
    return jnp.concatenate([x1 * cos - x2 * sin, x2 * cos + x1 * sin], axis=-1)

def _apply_axial_rope(x, rope):
    cos_r, sin_r, cos_c, sin_c = rope
    x_row, x_col = jnp.split(x.astype(jnp.float32), 2, axis=-1)
    return jnp.concatenate([_rotate(x_row, cos_r, sin_r), _rotate(x_col, cos_c, sin_c)], axis=-1).astype(x.dtype)

def _rope_pairs(x, rope):
    b, t, h, _ = x.shape
    return _apply_axial_rope(x.reshape(b, t, 2 * h, HEAD_DIM), rope).reshape(b, t, h, 2 * HEAD_DIM)

def _gqa_blocks(q, k_ctx, v_ctx, sink, k_lat=None, v_lat=None):
    bn, t = q.shape[0], q.shape[1]
    n_ctx = k_ctx.shape[1]
    nb = t // BLOCK
    scale = HEAD_DIM ** -0.5
    qb = q.reshape(bn, nb, BLOCK, A_KV_HEADS, A_GROUP, HEAD_DIM).swapaxes(0, 1)
    sink_s = jnp.broadcast_to(sink.astype(jnp.float32).reshape(1, A_KV_HEADS, A_GROUP, 1, 1),
                              (bn, A_KV_HEADS, A_GROUP, BLOCK, 1))
    windowed = k_lat is not None
    if windowed:
        pad = ((0, 0), (BLOCK, BLOCK), (0, 0), (0, 0))
        kp, vp = jnp.pad(k_lat, pad), jnp.pad(v_lat, pad)
        rel = jnp.arange(3 * BLOCK)[None, :] - BLOCK - jnp.arange(BLOCK)[:, None]
        band = jnp.abs(rel) <= WINDOW

    def one_block(args):
        qi, i = args
        s_ctx = jnp.einsum("bqkgd,blkd->bkgql", qi, k_ctx).astype(jnp.float32) * scale
        parts = [s_ctx, sink_s]
        if windowed:
            start = i * BLOCK
            kw = lax.dynamic_slice_in_dim(kp, start, 3 * BLOCK, axis=1)
            vw = lax.dynamic_slice_in_dim(vp, start, 3 * BLOCK, axis=1)
            kpos = start - BLOCK + jnp.arange(3 * BLOCK)
            valid = band & ((kpos >= 0) & (kpos < t))[None, :]
            s_win = jnp.einsum("bqkgd,blkd->bkgql", qi, kw).astype(jnp.float32) * scale
            parts = [jnp.where(valid, s_win, -jnp.inf)] + parts
        p = jax.nn.softmax(jnp.concatenate(parts, axis=-1), axis=-1)
        if windowed:
            p_win = p[..., :3 * BLOCK].astype(vw.dtype)
            p_ctx = p[..., 3 * BLOCK:3 * BLOCK + n_ctx].astype(v_ctx.dtype)
            return (jnp.einsum("bkgql,blkd->bqkgd", p_win, vw)
                    + jnp.einsum("bkgql,blkd->bqkgd", p_ctx, v_ctx))
        return jnp.einsum("bkgql,blkd->bqkgd", p[..., :n_ctx].astype(v_ctx.dtype), v_ctx)

    out = lax.map(one_block, (qb, jnp.arange(nb)))
    return out.swapaxes(0, 1).reshape(bn, t, A_HEADS * HEAD_DIM)

def _token_shift(p, mu_prev, mu_next):
    prev = jnp.pad(p, ((0, 0), (1, 0), (0, 0)))[:, :-1]
    nxt = jnp.pad(p, ((0, 0), (0, 1), (0, 0)))[:, 1:]
    return p + mu_prev * (prev - p) + mu_next * (nxt - p)

def _wkv_scan(r, w, k, v, kk, a, s0, reverse):
    xs = tuple(z.astype(jnp.float32).transpose(1, 0, 2, 3) for z in (r, w, k, v, kk, a))

    def step(s, inp):
        r_t, w_t, k_t, v_t, kk_t, a_t = inp
        sa = jnp.einsum("bhij,bhj->bhi", s, kk_t)
        s = (s * w_t[:, :, None, :] - sa[..., None] * (kk_t * a_t)[:, :, None, :]
             + v_t[..., None] * k_t[:, :, None, :])
        return s, jnp.einsum("bhij,bhj->bhi", s, r_t)

    s_fin, ys = lax.scan(step, s0.astype(jnp.float32), xs, reverse=reverse)
    return ys.transpose(1, 0, 2, 3), s_fin

def _rwkv_mixer(pb, s0, j, W):
    bn, t, _ = pb.shape
    r, k, v, wf, wb, af, ab, gd = _split(
        pb, (B_WIDTH, B_WIDTH, B_WIDTH, DECAY_LORA, DECAY_LORA, AAA_LORA, AAA_LORA, GATE_LORA))
    hs = lambda z: z.astype(jnp.float32).reshape(bn, t, B_HEADS, HEAD_DIM)
    kk = hs(k * W["b_k_k"][j])
    kk = kk / jnp.maximum(jnp.sqrt(jnp.sum(kk * kk, axis=-1, keepdims=True)), 1e-12)
    rh, vh = hs(r), hs(v)
    ys, bonus, finals = [], [], []
    for d, (w_dn, a_dn) in enumerate(((wf, af), (wb, ab))):
        w_log = -jax.nn.softplus(-(W["b_w0"][j, d] + jnp.tanh(w_dn) @ W["b_w2"][j, d])) - 0.5
        decay = jnp.exp(-jnp.exp(w_log.astype(jnp.float32)))
        a = jax.nn.sigmoid(W["b_a0"][j, d] + a_dn @ W["b_a2"][j, d])
        k_d = hs(k * (1 + (a - 1) * W["b_k_a"][j]))
        y_d, s_d = _wkv_scan(rh, hs(decay), k_d, vh, kk, hs(a), s0[:, d], reverse=(d == 1))
        ys.append(y_d)
        bonus.append(jnp.sum(rh * k_d * W["b_r_k"][j].astype(jnp.float32), axis=-1, keepdims=True) * vh)
        finals.append(s_d)
    y = ys[0] + ys[1]
    mu = jnp.mean(y, axis=-1, keepdims=True)
    var = jnp.mean(jnp.square(y - mu), axis=-1, keepdims=True)
    yn = ((y - mu) * lax.rsqrt(var + GN_EPS)).reshape(bn, t, B_WIDTH) * W["b_gn_w"][j] + W["b_gn_b"][j]
    yn = yn + (bonus[0] + bonus[1]).reshape(bn, t, B_WIDTH)
    g = jax.nn.sigmoid(gd) @ W["b_g2"][j]
    return (yn * g).astype(pb.dtype), jnp.stack(finals, axis=1)

def _mixer_ab(h, j, W, rope, cache):
    bn, t, _ = h.shape
    p = h @ W["w_in_ab"][j]
    qa, ka, va = _split(p[..., :A_COLS], (A_HEADS * HEAD_DIM, A_KV_HEADS * HEAD_DIM, A_KV_HEADS * HEAD_DIM))
    qa = qa.reshape(bn, t, A_HEADS, HEAD_DIM)
    ka = ka.reshape(bn, t, A_KV_HEADS, HEAD_DIM)
    va = va.reshape(bn, t, A_KV_HEADS, HEAD_DIM)
    pb = _token_shift(p[..., A_COLS:], W["b_mu_prev"][j], W["b_mu_next"][j])
    sink = W["a_sink"][j]
    if cache is None:
        oa = _gqa_blocks(qa, ka, va, sink)
        s0 = jnp.zeros((bn, 2, B_HEADS, HEAD_DIM, HEAD_DIM), jnp.float32)
    else:
        k_ctx, v_ctx, s0 = cache
        oa = _gqa_blocks(_apply_axial_rope(qa, rope), k_ctx, v_ctx, sink,
                         _apply_axial_rope(ka, rope), va)
    ob, s_fin = _rwkv_mixer(pb, s0, j, W)
    out = jnp.concatenate([oa, ob], axis=-1) @ W["w_out_ab"][j]
    return out, (ka, va, s_fin)

def _diff_attn(q, k, v, lam):
    bn, t = q.shape[0], q.shape[1]
    nb = t // BLOCK
    scale = HEAD_DIM ** -0.5
    qb = q.reshape(bn, nb, BLOCK, C_HEADS, 2, HEAD_DIM).swapaxes(0, 1)
    k2 = k.reshape(bn, k.shape[1], C_HEADS, 2, HEAD_DIM)

    def one_block(qi):
        s = jnp.einsum("bqhmd,bnhmd->bhmqn", qi, k2).astype(jnp.float32) * scale
        p = jax.nn.softmax(s, axis=-1)
        amap = p[:, :, 0] - lam * p[:, :, 1]
        return jnp.einsum("bhqn,bnhe->bqhe", amap.astype(v.dtype), v)

    o = lax.map(one_block, qb)
    return o.swapaxes(0, 1).reshape(bn, t, C_HEADS, C_VDIM)

def _mixer_c(h, j, l, W, rope, cache):
    bn, t, _ = h.shape
    q, k, v = jnp.split(h @ W["w_in_c"][j], 3, axis=-1)
    shp = (bn, t, C_HEADS, 2 * HEAD_DIM)
    q, k, v = q.reshape(shp), k.reshape(shp), v.reshape(shp)
    lam_init = 0.8 - 0.6 * math.exp(-0.3 * l)
    lam = (jnp.exp(jnp.sum(W["c_lq1"][j] * W["c_lk1"][j]).astype(jnp.float32))
           - jnp.exp(jnp.sum(W["c_lq2"][j] * W["c_lk2"][j]).astype(jnp.float32)) + lam_init)
    if cache is None:
        o = _diff_attn(q, k, v, lam)
    else:
        k_ctx, v_ctx = cache
        keys = jnp.concatenate([k_ctx, _rope_pairs(k, rope)], axis=1)
        vals = jnp.concatenate([v_ctx, v], axis=1)
        o = _diff_attn(_rope_pairs(q, rope), keys, vals, lam)
    of = o.astype(jnp.float32)
    of = of * lax.rsqrt(jnp.mean(of * of, axis=-1, keepdims=True) + SUBLN_EPS) * W["c_subln"][j] * (1.0 - lam_init)
    out = of.astype(h.dtype).reshape(bn, t, C_HEADS * C_VDIM) @ W["w_out_c"][j]
    return out, (k, v)

def _forward(x, cond, caches, W, latent):
    t = x.shape[1]
    rope = _axial_rope(t) if latent else None
    ak, av, bs, ck, cv = [], [], [], [], []
    for l in range(DEPTH):
        mod = (jax.nn.silu(cond) @ W["mod_w"][l] + W["mod_b"][l]).reshape(-1, 1, N_MOD * D_MODEL)
        sh1, sc1, g1, sh2, sc2, g2, sh3, sc3, g3 = jnp.split(mod, N_MOD, axis=-1)
        h = _rmsnorm(x, W["norms"][l, 0]) * (1 + sc1) + sh1
        x = x + 0.5 * g1 * _swiglu(h, W["ffn_w1"][l, 0], W["ffn_w3"][l, 0], W["ffn_w2"][l, 0])
        h = _rmsnorm(x, W["norms"][l, 1]) * (1 + sc2) + sh2
        j = l // 2
        if l % 2 == 0:
            cache = (caches["a_k"][:, j], caches["a_v"][:, j], caches["b_s"][:, j]) if latent else None
            m, st = _mixer_ab(h, j, W, rope, cache)
            if not latent:
                ak.append(st[0]); av.append(st[1]); bs.append(st[2])
        else:
            cache = (caches["c_k"][:, j], caches["c_v"][:, j]) if latent else None
            m, st = _mixer_c(h, j, l, W, rope, cache)
            if not latent:
                ck.append(st[0]); cv.append(st[1])
        x = x + g2 * m.astype(x.dtype)
        h = _rmsnorm(x, W["norms"][l, 2]) * (1 + sc3) + sh3
        x = x + 0.5 * g3 * _swiglu(h, W["ffn_w1"][l, 1], W["ffn_w3"][l, 1], W["ffn_w2"][l, 1])
    return _rmsnorm(x, W["final_norm"]), (ak, av, bs, ck, cv)

def setup_inputs(seed: int = 0) -> dict:
    key = jax.random.key(seed)
    ks = iter(jax.random.split(key, 48))
    nrm = lambda shape, s=1.0: s * jax.random.normal(next(ks), shape, jnp.float32)
    uni = lambda shape, lo, hi: jax.random.uniform(next(ks), shape, jnp.float32, lo, hi)
    D = D_MODEL
    return {
        "x_prompt": nrm((BATCH, SEQ, D)),
        "x_sample": nrm((DEC_BATCH, DEC_SEQ, D)),
        "c": nrm((DEC_BATCH, D)),
        "c_ctx": nrm((D,)),
        "cache_a_k": nrm((DEC_BATCH, N_AB, PAST_LEN, A_KV_HEADS, HEAD_DIM)),
        "cache_a_v": nrm((DEC_BATCH, N_AB, PAST_LEN, A_KV_HEADS, HEAD_DIM)),
        "state_b_wkv": nrm((DEC_BATCH, N_AB, 2, B_HEADS, HEAD_DIM, HEAD_DIM), 0.5),
        "cache_c_k": nrm((DEC_BATCH, N_C, PAST_LEN, C_HEADS, 2 * HEAD_DIM)),
        "cache_c_v": nrm((DEC_BATCH, N_C, PAST_LEN, C_HEADS, C_VDIM)),
        "norms": 1.0 + nrm((DEPTH, 3, D), 0.02),
        "mod_w": nrm((DEPTH, D, N_MOD * D), 0.02),
        "mod_b": nrm((DEPTH, N_MOD * D), 0.02),
        "ffn_w1": nrm((DEPTH, 2, D, D_FF), D ** -0.5),
        "ffn_w3": nrm((DEPTH, 2, D, D_FF), D ** -0.5),
        "ffn_w2": nrm((DEPTH, 2, D_FF, D), D_FF ** -0.5),
        "w_in_ab": nrm((N_AB, D, AB_COLS), D ** -0.5),
        "w_out_ab": nrm((N_AB, A_HEADS * HEAD_DIM + B_WIDTH, D), (A_HEADS * HEAD_DIM + B_WIDTH) ** -0.5),
        "a_sink": nrm((N_AB, A_HEADS), 0.5),
        "b_mu_prev": uni((N_AB, B_COLS), 0.0, 0.5),
        "b_mu_next": uni((N_AB, B_COLS), 0.0, 0.5),
        "b_w0": uni((N_AB, 2, B_WIDTH), -5.0, 0.0),
        "b_w2": nrm((N_AB, 2, DECAY_LORA, B_WIDTH), 0.1),
        "b_a0": nrm((N_AB, 2, B_WIDTH), 0.5),
        "b_a2": nrm((N_AB, 2, AAA_LORA, B_WIDTH), 0.1),
        "b_k_k": 0.85 + nrm((N_AB, B_WIDTH), 0.05),
        "b_k_a": 1.0 + nrm((N_AB, B_WIDTH), 0.05),
        "b_r_k": nrm((N_AB, B_HEADS, HEAD_DIM), 0.1),
        "b_g2": nrm((N_AB, GATE_LORA, B_WIDTH), GATE_LORA ** -0.5),
        "b_gn_w": 1.0 + nrm((N_AB, B_WIDTH), 0.02),
        "b_gn_b": nrm((N_AB, B_WIDTH), 0.02),
        "w_in_c": nrm((N_C, D, C_COLS), D ** -0.5),
        "w_out_c": nrm((N_C, C_HEADS * C_VDIM, D), (C_HEADS * C_VDIM) ** -0.5),
        "c_lq1": nrm((N_C, HEAD_DIM), 0.1),
        "c_lk1": nrm((N_C, HEAD_DIM), 0.1),
        "c_lq2": nrm((N_C, HEAD_DIM), 0.1),
        "c_lk2": nrm((N_C, HEAD_DIM), 0.1),
        "c_subln": 1.0 + nrm((N_C, C_VDIM), 0.02),
        "final_norm": 1.0 + nrm((D,), 0.02),
    }

def reference(x_prompt, x_sample, c, c_ctx, cache_a_k, cache_a_v, state_b_wkv, cache_c_k, cache_c_v,
              norms, mod_w, mod_b, ffn_w1, ffn_w3, ffn_w2,
              w_in_ab, w_out_ab, a_sink, b_mu_prev, b_mu_next, b_w0, b_w2, b_a0, b_a2,
              b_k_k, b_k_a, b_r_k, b_g2, b_gn_w, b_gn_b,
              w_in_c, w_out_c, c_lq1, c_lk1, c_lq2, c_lk2, c_subln, final_norm):
    W = dict(norms=norms, mod_w=mod_w, mod_b=mod_b, ffn_w1=ffn_w1, ffn_w3=ffn_w3, ffn_w2=ffn_w2,
             w_in_ab=w_in_ab, w_out_ab=w_out_ab, a_sink=a_sink, b_mu_prev=b_mu_prev, b_mu_next=b_mu_next,
             b_w0=b_w0, b_w2=b_w2, b_a0=b_a0, b_a2=b_a2, b_k_k=b_k_k, b_k_a=b_k_a, b_r_k=b_r_k,
             b_g2=b_g2, b_gn_w=b_gn_w, b_gn_b=b_gn_b, w_in_c=w_in_c, w_out_c=w_out_c,
             c_lq1=c_lq1, c_lk1=c_lk1, c_lq2=c_lq2, c_lk2=c_lk2, c_subln=c_subln, final_norm=final_norm)
    y_prompt, (ak, av, bs, ck, cv) = _forward(x_prompt, c_ctx, None, W, latent=False)
    caches = dict(a_k=cache_a_k, a_v=cache_a_v, b_s=state_b_wkv, c_k=cache_c_k, c_v=cache_c_v)
    y_sample, _ = _forward(x_sample, c, caches, W, latent=True)
    new_a_k = jnp.stack(ak, axis=1)
    new_a_v = jnp.stack(av, axis=1)
    new_b_wkv = jnp.stack(bs, axis=1)
    new_c_k = jnp.stack(ck, axis=1)
    new_c_v = jnp.stack(cv, axis=1)
    return (y_prompt, y_sample, new_a_k, new_a_v, new_b_wkv, new_c_k, new_c_v)


_drawn_inputs = setup_inputs


def setup_inputs(seed=0):
    import zlib

    import numpy as np

    out = dict(_drawn_inputs(seed))
    spreads = {}
    factors = {'cache_a_k': 3.468,
     'cache_a_v': 2.984,
     'state_b_wkv': 6.023,
     'a_sink': 8.0,
     'b_gn_w': 8.0,
     'b_gn_b': 8.0,
     'c_lq1': 4.166,
     'c_lk1': 4.303,
     'c_lq2': 3.82,
     'c_subln': 8.0,
     'final_norm': 2.712}
    for name, (base, spread) in spreads.items():
        noise = np.random.default_rng([zlib.crc32(name.encode()), seed]).standard_normal(out[name].shape)
        drawn = base * np.exp(spread * noise) if base else spread * noise
        out[name] = jnp.asarray(drawn.astype(out[name].dtype))
    for name, factor in factors.items():
        out[name] = (out[name] * factor).astype(out[name].dtype)
    return out
```

```python
from contextlib import ExitStack
import math

import numpy as np

import concourse.bass as bass
from concourse import mybir

F32 = mybir.dt.float32
F32R = mybir.dt.float32r
ALU = mybir.AluOpType
ACT = mybir.ActivationFunctionType
AX = mybir.AxisListType

P = 128
D = 1024
DT = D // P
LAT, CTX = 512, 128
TOK = LAT + CTX
HALF = TOK // 2
NB = LAT // P
NCH = TOK // P
DEPTH = 2
FF = 2816
FT = FF // P
BLOCKS = [(0, 8), (8, 8), (16, 6)]
NMOD = 9
HD = 64
AH, CH = 8, 8
BW = 512
BT = BW // P
AB_TILES = 21
C_TILES = 24
RING = 4
W = P
SCALE = HD ** -0.5
DECAY = math.exp(-0.5)
SEGS = ((0, LAT, 0), (LAT, TOK, 1))

AB_COLUMN = [0, 1, 2, 3] + list(range(6, 21)) + [4, 5]
T_R, T_K, T_V, T_W, T_A, T_G, T_KA, T_VA = 4, 8, 12, 16, 17, 18, 19, 20

C_NORM, C_FINAL, C_MUP, C_MUN, C_W0, C_A0, C_KK, C_KA, C_RK = 0, 48, 56, 77, 98, 106, 114, 118, 122
C_GNW, C_GNB, C_SUB, C_COND, C_MODB = 128, 132, 136, 137, 153
C_END = 384


class Steps:

    def __init__(self, sem, names, offset=0):
        self.s, self.names, self.index, self.next = sem, names, {n: i for i, n in enumerate(names)}, 0
        self.offset = offset
        assert len(self.index) == len(names)

    def sem(self, name):
        assert self.names[self.next % len(self.names)] == name, (name, self.names[self.next % len(self.names)])
        self.next += 1
        return self.s

    def value(self, name, turn=0):
        return turn * len(self.names) + (self.offset + self.index[name] + 1)

    def before(self, turn):
        return turn * len(self.names) + self.offset


def tables():
    i = np.arange(P)
    eye = np.eye(P, dtype=np.float32)
    blk = (i[:, None] // HD == i[None, :] // HD).astype(np.float32)
    base = np.concatenate([eye, np.full((P, P), 1 / D, np.float32), np.full((P, P), 1 / P, np.float32), blk], 1)

    n_freq = HD // 4
    inv = np.power(np.float32(10000.0), -np.arange(n_freq, dtype=np.float32) / n_freq).astype(np.float32)
    t = np.arange(LAT)
    f = i % HD
    pos = np.where((f < HD // 2)[:, None], (t // 64)[None, :], (t % 64)[None, :]).astype(np.float32)
    ang = (pos * inv[f % n_freq][:, None]).astype(np.float32)
    second = (f % 32) >= n_freq
    rot = np.zeros((P, P), np.float32)
    for m in range(P):
        rot[m - n_freq if second[m] else m + n_freq, m] = 1.0 if second[m] else -1.0
    dup = [np.zeros((P, P), np.float32) for _ in range(2)]
    for g in range(2):
        dup[g][g * HD + i % HD, i] = 1.0
    rdup = [np.zeros((P, P), np.float32) for _ in range(2)]
    for g in range(2):
        rdup[g] = dup[g] @ rot
    q, k = i[:, None], i[None, :]
    low = np.float32(-1e30)
    none, prev, nxt = np.zeros((P, P)), np.where(k >= q, 0, low), np.where(k <= q, 0, low)
    band = np.concatenate([none, prev, none, nxt, none, none, nxt], 1).astype(np.float32)
    attn = np.concatenate([dup[0], dup[1], rdup[0], rdup[1], rot, np.cos(ang), np.sin(ang), band], 1)

    s, t2 = i[:, None], i[None, :]
    fwd = [(s < t2), (s <= t2)] * 2
    bwd = [(s > t2), (s >= t2)] * 2
    late, early = [], []
    for lev in range(7):
        b = 1 << lev
        blkc = np.repeat(np.arange(HD // b), b)[None, :]
        same = (s // (2 * b)) == blkc
        late.append(same & (s % (2 * b) >= b))
        early.append(same & (s % (2 * b) < b))
    reset = np.ones((P, TOK), np.float32)
    reset[:, ::P] = 0.0
    eye2 = np.concatenate([np.eye(HD), np.eye(HD)], 0)
    rwkv = np.concatenate([np.concatenate(x, 1).astype(np.float32) for x in (fwd, bwd, late, early)] + [reset, eye2], 1)
    return base.astype(np.float32), attn.astype(np.float32), rwkv.astype(np.float32)


BASE_W, ATTN_W, RWKV_W = 512, 2560, 2624


def build(nc, T):
    ctx = ExitStack()
    with ctx:
        def sb(name, shape, dt=F32):
            return ctx.enter_context(nc.sbuf_tensor(name, shape, dt))

        def sem(name):
            return ctx.enter_context(nc.semaphore(name))

        def sb_two(name, shape, first, second):
            at = (nc.sbuf_base + 31) // 32 * 32
            a = sb(name, shape, first)
            return a, nc.alloc_sbuf_tensor_at(name + "_as_" + ("f32r" if second == F32R else "f32"), shape, second, offset=at)

        x = sb("x", [P, DT, TOK])
        h_hi, h_hi_f = sb_two("h_hi", [P, DT, TOK], F32R, F32)
        h_lo, h_lo_f = sb_two("h_lo", [P, DT, TOK], F32R, F32)
        big, hidden = sb_two("big", [P, 24, TOK], F32, F32R)
        raw = sb("raw", [P, RING, DT, W])
        w_hi, w_hi_f = sb_two("w_hi", [P, RING, DT, W], F32R, F32)
        w_lo, w_lo_f = sb_two("w_lo", [P, RING, DT, W], F32R, F32)
        work = sb("work", [P, 6400])
        mod = sb("mod", [P, DEPTH * NMOD * DT, 2])
        cols = sb("cols", [P, C_END])
        base = sb("base", [P, BASE_W])
        attn = sb("attn", [P, ATTN_W])
        eps = sb("eps", [P, 12])
        small = sb("small", [P, 32])
        pp = [ctx.enter_context(nc.psum_tensor(f"pair{i}", [P, 2, 512], F32)) for i in range(4)]

        ident, mean_d, mean_p, blk = (base[:, i * P:(i + 1) * P] for i in range(4))
        dup = [attn[:, g * P:(g + 1) * P] for g in range(2)]
        rdup = [attn[:, (2 + g) * P:(3 + g) * P] for g in range(2)]
        rot = attn[:, 512:640]
        cos, sin = attn[:, 640:1152], attn[:, 1152:1664]
        band = attn[:, 1664:2560]
        g_hi = hidden[:, 0:8, :]
        g_lo = hidden[:, 8:16, :]
        mod_ring = work[:, 0:RING * DT * W].rearrange("p (s k w) -> p s k w", s=RING, k=DT)
        silu_t = work[:, 4096:4736].rearrange("p (a b) -> p a b", a=2)
        prod_t = work[:, 4736:5376].rearrange("p (a b) -> p a b", a=2)
        rt_t = work[:, 5376:6016]
        def col(i, n=1):
            return cols[:, i:i + n]

        def mod_at(l, c):
            return (l * NMOD + c) * DT

        def halves(ap):
            return ap.rearrange("p (a b) -> p a b", a=2)

        def f32(ap):
            return ap.bitcast(F32)

        raw_full = [sem(f"raw_full{i}") for i in range(RING)]
        hi_full = sem("hi_full")
        lo_full = sem("lo_full")
        slab_used = sem("slab_used")
        pair_free = sem("pair_free")
        silu_done = sem("silu_done")
        ghi_done = sem("ghi_done")
        g_ready = sem("g_ready")
        mraw_full = [sem(f"mraw_full{i}") for i in range(RING)]
        m_used = sem("m_used")
        m_taken = sem("m_taken")
        s_load = sem("s_load")
        s_zero = sem("s_zero")
        s_tr = sem("s_tr")
        s_ev = sem("s_ev")
        s_cond = sem("s_cond")
        s_vec = sem("s_vec")
        s_out = sem("s_out")

        NORMS = 2 * 3 + 1
        NM = [sem(f"norm_{n}") for n in ("sq", "sum", "root", "recip", "scaled", "hi", "lo")]
        n_sq, n_sum, n_root, n_recip, n_scaled, n_hi, n_lo = NM

        stages = []
        for l in range(DEPTH):
            for f in range(2):
                if f == 1:
                    stages.append(("in", l, 0, 0, AB_TILES if l % 2 == 0 else C_TILES))
                    stages.append(("out", l, 0, 0, DT))
                for b, (_, cnt) in enumerate(BLOCKS):
                    stages.append(("up", l, f, b, 2 * cnt))
                    stages.append(("down", l, f, b, DT))
        start, n = {}, 0
        for st in stages:
            start[st[:4]] = n
            n += st[4]
        total = n
        upd, hid, u, hh = {}, {}, 0, 0
        for st in stages:
            upd[st[:4]], hid[st[:4]] = u, hh
            u += DT if st[0] in ("down", "out") else 0
            hh += st[4] // 2 if st[0] == "up" else 0
        norm_before = {}
        norm_no = {}
        k = 0
        for l in range(DEPTH):
            for s, key in enumerate([("up", l, 0, 0), ("in", l, 0, 0), ("up", l, 1, 0)]):
                norm_before[key] = k
                norm_no[k] = (l, s, upd[key])
                k += 1
        norm_no[k] = (DEPTH, 0, u)

        R = big[:, :, :].rearrange("p t n -> p (t n)")
        rows = [R[:, i * P:(i + 1) * P] for i in range(3)]
        x_rows = h_hi_f[:, :, :].rearrange("p t n -> p (t n)").rearrange("p (t n) -> p t n", t=5)
        norm_t = big[:, 16:24, :]
        praw = [work[:, 4096 + 644 * q:4096 + 644 * (q + 1)] for q in range(2)]
        c0 = small[:, 0:AB_TILES]
        kam = small[:, 24:28]
        ab_shift, ab_pad = sem("ab_shift"), sem("ab_pad")
        o_hi, o_lo = sem("o_hi"), sem("o_lo")
        y_tr, y_ev = sem("y_tr"), sem("y_ev")

        def halves2(ap, t):
            return ap[:, t, :].rearrange("p (a b) -> p a b", a=2)

        def LOOKAHEAD(i):
            return i + 1 < len(stages) and stages[i + 1][0] != "out"

        def FRESH(i):
            return i == 0 or stages[i][0] == "out"

        norm_at = {norm_before[q]: start[q] for q in norm_before}
        norm_at[NORMS - 1] = total

        def loop_and_last(eng, turns, turn):
            if turns > 1:
                with eng.Fori(0, turns - 1) as i:
                    turn(i, False)
            turn(turns - 1, True)

        cols3 = cols[:, :].unsqueeze(2)
        kam3 = kam.unsqueeze(2)

        hh = h_hi_f[:, :, :].rearrange("p t n -> p (t n)")
        hl = h_lo_f[:, :, :].rearrange("p t n -> p (t n)")
        wh = w_hi_f[:, :, :, :].rearrange("p s k w -> p (s k w)")
        wl = w_lo_f[:, :, :, :].rearrange("p s k w -> p (s k w)")
        rw = raw[:, :, :, :].rearrange("p s k w -> p (s k w)")

        a_keys = hh[:, 0:1280].rearrange("p (g n) -> p g n", g=2)
        a_pkeys = hh[:, 1280:1536].rearrange("p (g n) -> p g n", g=2)
        a_vtok = hh[:, 1536:2176].rearrange("p (t n) -> p t n", n=P)
        a_vpast, a_kpast = hh[:, 2176:2304], hh[:, 2304:2432]
        a_kpast_t, a_kout = hh[:, 2432:2560], hh[:, 2560:2688]
        a_sink = hh[:, 2688:2696]
        a_q, a_qp = hh[:, 2700:3212], hh[:, 3212:3340]
        a_t1, a_t2 = hh[:, 3340:3852], hh[:, 3852:4364]
        a_max, a_neg, a_es, a_den, a_rden = (hh[:, 4400 + 8 * i:4405 + 8 * i] for i in range(5))
        a_sk = hh[:, 4440:4442]
        a_s = hl[:, 0:2560].rearrange("p (b n) -> p b n", b=5)
        a_e = hl[:, 2560:5120].rearrange("p (b n) -> p b n", b=5)
        a_pt = wh[:, 0:2048]
        WIN = [(max(0, b - 1), min(NB, b + 2)) for b in range(NB)]
        ENDS = [P + (k1 - k0) * P for k0, k1 in WIN]
        PIECES = [(b, i) for b in range(NB) for i in range(ENDS[b] // P)] + [(NB, 0)]

        a_load, a_pe, a_act, a_dve, a_out = (sem(f"a_{n}") for n in ("load", "pe", "act", "dve", "out"))
        APE0 = Steps(a_pe, ["past_t", "v_t", "dup", "dup2"])
        AAC0 = Steps(a_act, ["past_t", "v_t", "dup2"])
        ADV0 = Steps(a_dve, ["mul0", "keys0", "mul1", "keys1"])
        APE = Steps(a_pe, ["rot", "sc0", "tr0", "pv0", "sc1", "tr1", "pv1"], 4)
        AAC = Steps(a_act, ["qp", "exp0", "pt0", "o0", "exp1", "pt1", "o1"], 3)
        ADV = Steps(a_dve, ["rope1", "rope"] + [f"{n}{h}" for h in range(2) for n in ("s", "mx", "ng", "dn", "rd", "pn")], 4)
        IN_AB = start["in", 0, 0, 0]
        IN_C = start["in", 1, 0, 0]

        def sp_attn_ab(sp):
            sp.wait_ge(slab_used, IN_AB + AB_TILES + RING)
            sp.dma_start(a_vpast, T["cache_a_v"][0, 0].rearrange("t g d -> t (g d)")).then_inc(a_load, 16)
            sp.dma_start(a_kpast, T["cache_a_k"][0, 0].rearrange("t g d -> t (g d)")).then_inc(a_load, 16)
            sp.dma_start(a_sink, T["a_sink"].to_broadcast([P, AH])).then_inc(a_load, 16)
            sp.wait_ge(a_act, AAC0.value("v_t"))
            sp.dma_start(T["new_a_k"][0, 0].rearrange("t g d -> t (g d)"), a_kout).then_inc(a_out, 16)
            sp.dma_start(T["new_a_v"][0, 0].rearrange("t g d -> t (g d)"), a_vtok[:, 4, :]).then_inc(a_out, 16)

        def pe_attn_ab(pe):
            pe.wait_ge(a_load, 48)
            pe.wait_ge(ab_shift, 3 * AB_TILES)
            nc.tensor.transpose(pp[0][:, 0, 0:P], a_kpast, ident)
            nc.tensor.transpose(pp[0][:, 0, P:2 * P], big[:, T_KA, LAT:TOK], ident).then_inc(APE0.sem("past_t"), 1)
            for t in range(NCH):
                ins = nc.tensor.transpose(pp[1][:, t // 4, (t % 4) * P:(t % 4 + 1) * P], big[:, T_VA, t * P:(t + 1) * P], ident)
            ins.then_inc(APE0.sem("v_t"), 1)
            for g in range(2):
                nc.tensor.matmul(pp[2][:, g, :], dup[g], big[:, T_KA, 0:LAT], start=True, stop=True)
                ins = nc.tensor.matmul(pp[3][:, g, :], rdup[g], big[:, T_KA, 0:LAT], start=True, stop=True)
            ins.then_inc(APE0.sem("dup"), 1)
            pe.wait_ge(a_act, AAC0.value("past_t"))
            for g in range(2):
                nc.tensor.matmul(pp[0][:, g, 0:P], dup[g], a_kpast_t, start=True, stop=True)
                ins = nc.tensor.matmul(pp[0][:, g, P:2 * P], dup[g], big[:, T_KA, LAT:TOK], start=True, stop=True)
            ins.then_inc(APE0.sem("dup2"), 1)

            for g in range(2):
                with pe.Fori(0, 2) as jj:
                    it = jj + 2 * g
                    pe.wait_ge(a_act, AAC.before(it))
                    pe.wait_ge(a_dve, ADV.before(it))
                    nc.tensor.matmul(pp[3][:, 0, :], rot, big[:, it, 0:LAT], start=True, stop=True).then_inc(APE.sem("rot"), 1)
                    for h in range(2):
                        r = slice(h * HD, h * HD + HD)
                        if h == 0:
                            pe.wait_ge(a_dve, ADV.value("rope", it))
                            pe.wait_ge(a_act, AAC.value("qp", it))
                        else:
                            pe.wait_ge(a_act, AAC.value("pt0", it))
                        for b in range(NB):
                            ps = pp[b // 2][:, b % 2, :]
                            q = a_q[r, b * P:(b + 1) * P]
                            k0, k1 = WIN[b]
                            nc.tensor.matmul(ps[:, 0:P], q, a_keys[r, g, 0:P], start=True, stop=True)
                            nc.tensor.matmul(ps[:, P:ENDS[b]], q, a_keys[r, g, P + k0 * P:P + k1 * P], start=True, stop=True)
                        nc.tensor.matmul(pp[2][:, 0, 0:P], a_qp[r, :], a_pkeys[r, g, :], start=True, stop=True
                                         ).then_inc(APE.sem(f"sc{h}"), 1)
                        pe.wait_ge(a_dve, ADV.value(f"pn{h}", it))
                        for s, (b, i) in enumerate(PIECES):
                            ins = nc.tensor.transpose(pp[s // 8][:, s // 4 % 2, s % 4 * P:s % 4 * P + P],
                                                      a_e[:, b, i * P:(i + 1) * P], ident)
                        ins.then_inc(APE.sem(f"tr{h}"), 1)
                        pe.wait_ge(a_act, AAC.value(f"pt{h}", it))
                        for s, (b, i) in enumerate(PIECES):
                            last = s + 1 == len(PIECES) or PIECES[s + 1][0] != b
                            if b == NB:
                                v = a_vtok[:, NB, g * HD:(g + 1) * HD]
                            elif i == 0:
                                v = a_vpast[:, g * HD:(g + 1) * HD]
                            else:
                                v = a_vtok[:, WIN[b][0] + i - 1, g * HD:(g + 1) * HD]
                            out = pp[3][r, b // NB, (b % NB) * P:(b % NB + 1) * P]
                            ins = nc.tensor.matmul(out, v, a_pt[:, s * P:(s + 1) * P], start=(i == 0), stop=last)
                        ins.then_inc(APE.sem(f"pv{h}"), 1)

        def act_attn_ab(act):
            act.wait_ge(a_pe, APE0.value("past_t"))
            nc.scalar.activation(hh[:, 2432:2688], pp[0][:, 0, 0:2 * P], ACT.Copy).then_inc(AAC0.sem("past_t"), 1)
            act.wait_ge(a_pe, APE0.value("v_t"))
            nc.scalar.activation(hh[:, 1536:2048], pp[1][:, 0, :], ACT.Copy)
            nc.scalar.activation(hh[:, 2048:2176], pp[1][:, 1, 0:P], ACT.Copy).then_inc(AAC0.sem("v_t"), 1)
            act.wait_ge(a_pe, APE0.value("dup2"))
            nc.scalar.activation(a_keys[:, :, 0:P], pp[0][:, :, 0:P], ACT.Copy)
            nc.scalar.activation(a_pkeys, pp[0][:, :, P:2 * P], ACT.Copy).then_inc(AAC0.sem("dup2"), 1)
            nc.scalar.preload_act_table(ACT.Exp)
            with act.Fori(0, 4) as it:
                act.wait_ge(a_act, AAC.before(it))
                nc.scalar.activation(a_qp, big[:, it, LAT:TOK], ACT.Copy).then_inc(AAC.sem("qp"), 1)
                for h in range(2):
                    act.wait_ge(a_dve, ADV.value(f"ng{h}", it))
                    nc.scalar.activation(a_es, a_neg, ACT.Exp, bias=a_sk[:, h:h + 1])
                    for b in range(5):
                        n = ENDS[b] if b < NB else P
                        ins = nc.scalar.activation(a_e[:, b, 0:n], a_s[:, b, 0:n], ACT.Exp, bias=a_neg[:, b:b + 1],
                                                   accum_out=a_den[:, b:b + 1])
                    ins.then_inc(AAC.sem(f"exp{h}"), 1)
                    act.wait_ge(a_pe, APE.value(f"tr{h}", it))
                    nc.scalar.activation(halves(a_pt[:, 0:1024]), pp[0][:, :, :], ACT.Copy)
                    nc.scalar.activation(a_pt[:, 1024:1536], pp[1][:, 0, :], ACT.Copy)
                    nc.scalar.activation(a_pt[:, 1536:1920], pp[1][:, 1, 0:384], ACT.Copy).then_inc(AAC.sem(f"pt{h}"), 1)
                    act.wait_ge(a_pe, APE.value(f"pv{h}", it))
                    r = slice(h * HD, h * HD + HD)
                    nc.scalar.activation(big[r, it, 0:LAT], pp[3][r, 0, :], ACT.Copy)
                    nc.scalar.activation(big[r, it, LAT:TOK], pp[3][r, 1, 0:P], ACT.Copy).then_inc(AAC.sem(f"o{h}"), 1)

        def dve_attn_ab(dve):
            dve.wait_ge(a_pe, APE0.value("dup"))
            for g in range(2):
                if g:
                    dve.wait_ge(a_dve, ADV0.value("keys0"))
                nc.vector.tensor_tensor(a_t1, pp[2][:, g, :], cos, ALU.mult)
                nc.vector.tensor_tensor(a_t2, pp[3][:, g, :], sin, ALU.mult).then_inc(ADV0.sem(f"mul{g}"), 1)
                dve.wait_ge(a_dve, ADV0.value(f"mul{g}"))
                nc.vector.tensor_tensor(a_keys[:, g, P:TOK], a_t1, a_t2, ALU.add).then_inc(ADV0.sem(f"keys{g}"), 1)
            with dve.Fori(0, 4) as it:
                dve.wait_ge(a_pe, APE.value("rot", it))
                nc.vector.tensor_copy(a_sk, a_sink.rearrange("p (a b) -> p a b", b=2)[:, it, :])
                nc.vector.tensor_tensor(a_t1, big[:, it, 0:LAT], cos, ALU.mult)
                nc.vector.tensor_tensor(a_t2, pp[3][:, 0, :], sin, ALU.mult).then_inc(ADV.sem("rope1"), 1)
                dve.wait_ge(a_dve, ADV.value("rope1", it))
                nc.vector.tensor_tensor(a_q, a_t1, a_t2, ALU.add).then_inc(ADV.sem("rope"), 1)
                for h in range(2):
                    dve.wait_ge(a_pe, APE.value(f"sc{h}", it))
                    for b in range(NB):
                        m = band[:, 0:ENDS[b]] if b else band[:, 512:512 + ENDS[b]]
                        nc.vector.scalar_tensor_tensor(out=a_s[:, b, 0:ENDS[b]], in0=pp[b // 2][:, b % 2, 0:ENDS[b]], scalar=SCALE,
                                                       in1=m, op0=ALU.mult, op1=ALU.add)
                    nc.vector.tensor_scalar(a_s[:, NB, 0:P], pp[2][:, 0, 0:P], SCALE, None, ALU.mult
                                            ).then_inc(ADV.sem(f"s{h}"), 1)
                    dve.wait_ge(a_dve, ADV.value(f"s{h}", it))
                    for b in range(5):
                        ins = nc.vector.tensor_reduce(a_max[:, b:b + 1], a_s[:, b, 0:(ENDS[b] if b < NB else P)], AX.X, ALU.max)
                    ins.then_inc(ADV.sem(f"mx{h}"), 1)
                    dve.wait_ge(a_dve, ADV.value(f"mx{h}", it))
                    nc.vector.tensor_scalar(a_neg, a_max, a_sk[:, h:h + 1], -1.0, ALU.max, ALU.mult
                                            ).then_inc(ADV.sem(f"ng{h}"), 1)
                    dve.wait_ge(a_act, AAC.value(f"exp{h}", it))
                    nc.vector.tensor_tensor(a_den, a_den, a_es, ALU.add).then_inc(ADV.sem(f"dn{h}"), 1)
                    dve.wait_ge(a_dve, ADV.value(f"dn{h}", it))
                    nc.vector.reciprocal(a_rden, a_den).then_inc(ADV.sem(f"rd{h}"), 1)
                    dve.wait_ge(a_dve, ADV.value(f"rd{h}", it))
                    for b in range(5):
                        n = ENDS[b] if b < NB else P
                        ins = nc.vector.tensor_scalar(a_e[:, b, 0:n], a_e[:, b, 0:n], a_rden[:, b:b + 1], None, ALU.mult)
                    ins.then_inc(ADV.sem(f"pn{h}"), 1)

        r_ar = hh[:, 0:1280].rearrange("p (c two n) -> p c two n", c=NCH, two=2)
        r_beta, r_kappa, r_kkn, r_y = (hh[:, 1280 + 640 * i:1920 + 640 * i] for i in range(4))
        r_vtok = hh[:, 3840:4480].rearrange("p (c n) -> p c n", c=NCH)
        r_rhop = hh[:, 4480:4992]
        r_ktok = hl[:, 0:640].rearrange("p (c n) -> p c n", c=NCH)
        r_btok = hl[:, 640:1280].rearrange("p (c n) -> p c n", c=NCH)
        r_av = hl[:, 1280:2560].rearrange("p (u n) -> p u n", n=P)
        r_nwu = hl[:, 2560:3840].rearrange("p (u n) -> p u n", n=P)
        r_v, r_tb = hl[:, 3840:4480], hl[:, 4480:5120]
        r_sig, r_cum, r_a, r_kd, r_e1, r_e2 = (wh[:, 640 * i:640 * (i + 1)] for i in range(6))
        r_ft2, r_ft1 = wh[:, 3840:4096].rearrange("p (c n) -> p c n", n=P), hh[:, 4992:5120]
        r_ft = [r_ft2[:, 0, :], r_ft2[:, 1, :], r_ft1]
        r_p = wl[:, 0:640].rearrange("p (u n) -> p u n", n=HD)
        r_n = wl[:, 640:1280].rearrange("p (u n) -> p u n", n=HD)
        r_g = wl[:, 1280:1600].rearrange("p (c n) -> p c n", n=HD)
        r_z = wl[:, 1600:1920].rearrange("p (c n) -> p c n", n=HD)
        r_ht, r_d1, r_dd = (wl[:, 1920 + 8 * i:1925 + 8 * i] for i in range(3))
        r_w2, r_a2, r_g2 = (wl[:, 1952 + P * i:1952 + P * (i + 1)] for i in range(3))
        r_so = wl[0:HD, 2336:2592].rearrange("p (d n) -> p d n", d=2)
        r_kds, r_bonus = wl[:, 2592:3232], wl[:, 3232:3872]
        r_mask = [rw[:, 512 * i:512 * (i + 1)] for i in range(2)]
        r_late = rw[:, 1024:1472].rearrange("p (l n) -> p l n", n=HD)
        r_early = rw[:, 1472:1920].rearrange("p (l n) -> p l n", n=HD)
        r_reset, r_eye2 = rw[:, 1920:2560], rw[:, 2560:2624]
        r_s0t = rw[:, 2624:3136].rearrange("p (q n) -> p q n", n=HD)
        r_gate = rw[:, 3136:3776]
        r_s0 = work[0:HD, 0:1024].rearrange("p (q n) -> p q n", n=P)
        r_u4 = work[:, 0:5120].rearrange("p (u m n) -> p u m n", m=4, n=P)
        r_am = work[:, 5120:6400].rearrange("p (u n) -> p u n", n=P)
        r_t = R[:, 12160:13440].rearrange("p (u n) -> p u n", n=P)
        r_tt = R[:, 13440:14720].rearrange("p (u n) -> p u n", n=P)
        NU = 2 * NCH
        NL = 7

        def bank(i):
            return pp[i // 2][:, i % 2, :]

        def level_cols(ap, lev, half):
            return ap.rearrange("p u (k two b) -> p u k two b", two=2, b=1 << lev)[:, :, :, half, :]

        def sides(d):
            return (0, 1, r_late, r_early) if d == 0 else (1, 0, r_early, r_late)

        def lv_bank(k, g, n):
            u0, u1 = GROUPS[g]
            return bank(LBANK[k][g])[:, 0:(u1 - u0) * n].rearrange("p (u n) -> p u n", n=n)

        def chunks(d):
            return (0, 1, 2, 3) if d == 0 else (3, 2, 1, 0)

        b_load, b_lora, b_pe, b_act, b_dve, b_out = (sem(f"b_{n}") for n in ("load", "lora", "pe", "act", "dve", "out"))
        GROUPS = [(0, 4), (4, 7), (7, 10)]
        GS = range(len(GROUPS))
        LV = [("P", 1, g) for g in GS]
        for lev in range(1, NL - 1):
            LV += [("Q", lev, g) for g in GS]
            for g in GS:
                LV += [("X", lev, g)] + ([("P", lev + 1, g)] if lev < NL - 2 else [])
        LV += [(k, NL - 1, g) for k in "NR" for g in GS]
        LD = [({"P": "pn", "N": "pn", "Q": "t", "R": "t"}[k], lev, g) for k, lev, g in LV if k != "X"]
        LX = [("x", lev, g) for k, lev, g in LV if k == "X"]
        LBANK = {"P": (0, 1, 2), "N": (0, 1, 2), "Q": (3, 4, 5), "R": (3, 4, 5), "X": (6, 7, 6)}
        named = lambda steps, d: [f"{k}{lev}{g}_{d}" for k, lev, g in steps]
        BPE = Steps(b_pe, ["vT", "kkss"] + [f"{n}_{d}" for d in range(2) for n in
                    ["z", "tr"] + [f"pr{u}" for u in range(NU)] + ["A", "RV"]
                    + [f"{k}{lev}{g}" for k, lev, g in LV] + ["WU", "FG", "S0", "S1", "S2", "Y", "So"]] + ["bs", "gate", "mu", "var"], 1)
        BAC = Steps(b_act, ["vcopy", "kksq", "kkroot", "vtok", "sig_0", "ex_0", "tok_0", "rv_0"] + named(LX, 0) + ["wu_0", "y0", "so_0",
                            "sig_1", "ex_1", "tok_1", "rv_1"] + named(LX, 1) + ["wu_1", "so_1", "gt", "ysq", "sd"], 1)
        BDV = Steps(b_dve, ["kkmul", "kkmax", "kkrec", "kkn"] + [f"{n}_{d}" for d in range(2) for n in
                    ["cum", "ht", "q", "m", "kd1", "kd", "arr", "beta"] + [f"U{u}" for u in range(NU)] + ["Am", "id", "T0"]
                    + [f"{k}{lev}{g}" for k, lev, g in LD] + ["FG", "Z0", "Z1", "Z2"]] + ["y1", "bn", "bonus", "yc", "rs", "yn", "yg", "yb", "yo"], 1)

        def sp_rwkv(sp):
            sp.wait_ge(lo_full, IN_AB + AB_TILES + RING)
            sp.wait_ge(a_act, AAC.before(4))
            sp.dma_start(rw[:, 0:RWKV_W], T["t_rwkv"]).then_inc(b_load, 16)
            for d in range(2):
                sp.dma_start(r_s0[:, 4 * d:4 * d + 4, :].rearrange("p q (h n) -> p (q h) n", h=2),
                             T["state_b_wkv"][0, 0, d].rearrange("h i j -> i h j")).then_inc(b_load, 16)
            w2 = T["b_w2"][0].rearrange("d l (t w) -> (d l) t w", w=P)
            a2 = T["b_a2"][0].rearrange("d l (t w) -> (d l) t w", w=P)
            g2 = T["b_g2"][0].rearrange("l (t w) -> l t w", w=P)
            with sp.Fori(0, BT) as it:
                sp.wait_ge(b_pe, BPE.before(it))
                sp.wait_ge(b_out, 32 * it + 32)
                sp.dma_start(r_w2, w2[:, it, :]).then_inc(b_lora, 16)
                sp.dma_start(r_a2, a2[:, it, :]).then_inc(b_lora, 16)
                sp.dma_start(r_g2, g2[:, it, :]).then_inc(b_lora, 16)
                for d in range(2):
                    sp.wait_ge(b_act, BAC.value(f"so_{d}", it))
                    dst = T["new_b_wkv"][0, 0, d].rearrange("(t h) i j -> i t h j", h=2)[:, it, :, :]
                    sp.dma_start(dst, r_so[:, d, :].rearrange("p (h n) -> p h n", h=2)).then_inc(b_out, 16)
            sp.wait_ge(b_out, 32 * BT + 32)
            sp.wait_ge(b_dve, BDV.before(BT))

        def pe_rwkv(pe):
            pe.wait_ge(b_load, 48)
            pe.wait_ge(a_act, AAC.before(4))
            for q in range(2 * BT):
                ins = nc.tensor.transpose(bank(0)[:, q * HD:(q + 1) * HD], r_s0[:, q, :], ident[0:HD, 0:HD])
            ins.then_inc(b_pe, 1)
            heads = [slice(h * HD, h * HD + HD) for h in range(2)]
            with pe.Fori(0, BT) as it:
                def V(steps, name):
                    return steps.value(name, it)

                pe.wait_ge(b_act, V(BAC, "vcopy"))
                for c in range(NCH):
                    ins = nc.tensor.transpose(bank(c // 4)[:, c % 4 * P:c % 4 * P + P], r_v[:, c * P:(c + 1) * P], ident)
                ins.then_inc(BPE.sem("vT"), 1)
                pe.wait_ge(b_act, V(BAC, "kksq"))
                for c in range(2):
                    ins = nc.tensor.matmul(bank(2 + c)[:, 0:HALF], blk, r_tb[:, c * HALF:(c + 1) * HALF], start=True, stop=True)
                ins.then_inc(BPE.sem("kkss"), 1)
                for d in range(2):
                    dr = heads[d]
                    if d == 0:
                        pe.wait_ge(b_lora, 48 * it + 48)
                    for c in range(2):
                        nc.tensor.matmul(bank(4 + c)[:, 0:HALF], r_w2[dr, :], big[dr, T_W, c * HALF:(c + 1) * HALF],
                                         start=True, stop=True)
                        ins = nc.tensor.matmul(bank(6 + c)[:, 0:HALF], r_a2[dr, :], big[dr, T_A, c * HALF:(c + 1) * HALF],
                                               start=True, stop=True)
                    ins.then_inc(BPE.sem(f"z_{d}"), 1)
                    pe.wait_ge(b_dve, V(BDV, f"beta_{d}"))
                    for s in range(3 * NCH):
                        c = s % NCH
                        src = (r_ar[:, c, 0, :], r_beta[:, c * P:(c + 1) * P], r_kappa[:, c * P:(c + 1) * P])[s // NCH]
                        ins = nc.tensor.transpose(bank(s // 4)[:, s % 4 * P:s % 4 * P + P], src, ident)
                    ins.then_inc(BPE.sem(f"tr_{d}"), 1)
                    for u in range(NU):
                        c, r = u % NCH, heads[u // NCH]
                        if u >= 4:
                            pe.wait_ge(b_dve, V(BDV, f"U{u - 4}_{d}"))
                        ps = bank(4 + u % 4)
                        tk = slice(c * P, (c + 1) * P)
                        ar = r_ar[r, c, :, :]
                        nc.tensor.matmul(ps[:, 0:2 * P], r_beta[r, tk], ar, start=True, stop=True)
                        nc.tensor.matmul(ps[:, 2 * P:4 * P], r_kappa[r, tk], ar, start=True, stop=True
                                         ).then_inc(BPE.sem(f"pr{u}_{d}"), 1)
                    pe.wait_ge(b_act, V(BAC, f"tok_{d}"))
                    for u in range(NU):
                        c, r = u % NCH, heads[u // NCH]
                        ins = nc.tensor.matmul(bank(2 * (u // NCH) + c // 4)[:, c % 4 * P:c % 4 * P + P], r_ar[r, c, 0, :],
                                               r_beta[r, c * P:(c + 1) * P], start=True, stop=True)
                    ins.then_inc(BPE.sem(f"A_{d}"), 1)
                    pe.wait_ge(b_dve, V(BDV, f"U{NU - 1}_{d}"))
                    for u in range(NU):
                        c, r = u % NCH, heads[u // NCH]
                        ins = nc.tensor.matmul(bank(6 + u // 8)[:, u % 8 * HD:u % 8 * HD + HD], r_u4[:, u, 2, :],
                                               r_vtok[:, c, r], start=True, stop=True)
                    ins.then_inc(BPE.sem(f"RV_{d}"), 1)
                    hp, hn, _, _ = sides(d)
                    for k, lev, g in LV:
                        step = f"{k}{lev}{g}_{d}"
                        if k == "P":
                            pe.wait_ge(b_dve, V(BDV, f"T0_{d}" if lev == 1 else f"t{lev - 1}{g}_{d}"))
                        elif k == "X":
                            if lev == 1 and g == 0:
                                pe.wait_ge(b_act, V(BAC, f"rv_{d}"))
                            if g == 2:
                                pe.wait_ge(b_act, V(BAC, f"x{lev}0_{d}"))
                            pe.wait_ge(b_dve, V(BDV, f"t{lev}{g}_{d}"))
                        elif k == "N":
                            pe.wait_ge(b_act, V(BAC, f"x{lev - 1}{g}_{d}"))
                        else:
                            if k == "Q" and lev > 1:
                                pe.wait_ge(b_act, V(BAC, f"x{lev - 1}{g}_{d}"))
                            pe.wait_ge(b_dve, V(BDV, f"pn{lev}{g}_{d}"))
                        for u in range(*GROUPS[g]):
                            out = lv_bank(k, g, P if k in "PX" else HD)[:, u - GROUPS[g][0], :]
                            if k == "X":
                                ins = nc.tensor.transpose(out, r_t[:, u, :], ident)
                                continue
                            w, m = {"P": (r_u4[:, u, 0, :], r_t[:, u, :]), "Q": (r_tt[:, u, :], r_p[:, u, :]),
                                    "N": (r_am[:, u, :], level_cols(r_tt, lev, hn)[:, u]),
                                    "R": (r_t[:, u, :], r_n[:, u, :])}[k]
                            ins = nc.tensor.matmul(out, w, m, start=True, stop=True)
                        ins.then_inc(BPE.sem(step), 1)
                    pe.wait_ge(b_dve, V(BDV, f"t{NL - 1}2_{d}"))
                    for u in range(NU):
                        ins = nc.tensor.matmul(bank(u // 4)[:, u % 4 * P:u % 4 * P + P], r_tt[:, u, :], r_av[:, u, :],
                                               start=True, stop=True)
                    ins.then_inc(BPE.sem(f"WU_{d}"), 1)
                    pe.wait_ge(b_act, V(BAC, f"wu_{d}"))
                    order = chunks(d)
                    for h in range(2):
                        r = heads[h]
                        for i, c in enumerate(order[:3]):
                            nc.tensor.matmul(bank(3)[r, i * HD:(i + 1) * HD], r_nwu[:, NCH * h + c, 0:HD], r_btok[:, c, r],
                                             start=True, stop=True)
                        for c in range(NB):
                            nc.tensor.matmul(bank(5)[r, c * P:(c + 1) * P], r_nwu[:, NCH * h + c, 0:HD], r_u4[:, NCH * h + c, 1, :],
                                             start=True, stop=True)
                        for c in range(NCH):
                            nc.tensor.matmul(bank(4)[r, c * HD:(c + 1) * HD], r_ktok[:, c, r], r_vtok[:, c, r],
                                             start=True, stop=False)
                            ins = nc.tensor.matmul(bank(4)[r, c * HD:(c + 1) * HD], r_btok[:, c, r],
                                                   r_nwu[:, NCH * h + c, HD:P], start=False, stop=True)
                    ins.then_inc(BPE.sem(f"FG_{d}"), 1)
                    for i in range(3):
                        pe.wait_ge(b_dve, V(BDV, f"Z{i - 1}_{d}" if i else f"FG_{d}"))
                        nc.tensor.matmul(bank(7)[:, i * HD:(i + 1) * HD], r_ft[i], r_z[:, order[i], :], start=True, stop=True
                                         ).then_inc(BPE.sem(f"S{i}_{d}"), 1)
                    pe.wait_ge(b_dve, V(BDV, f"Z2_{d}"))
                    for h in range(2):
                        r = heads[h]
                        for c in range(NCH):
                            u = NCH * h + c
                            out = bank(c // 4)[r, c % 4 * P:c % 4 * P + P]
                            nc.tensor.matmul(out, r_vtok[:, c, r], r_u4[:, u, 3, :], start=True, stop=False)
                            ins = nc.tensor.matmul(out, r_nwu[:, u, HD:P], r_u4[:, u, 1, :], start=False, stop=(c == NB))
                            if c < NB:
                                ins = nc.tensor.matmul(out, r_z[r, c, :], r_rhop[r, c * P:(c + 1) * P], start=False, stop=True)
                    ins.then_inc(BPE.sem(f"Y_{d}"), 1)
                    nc.tensor.transpose(bank(2)[0:HD, 0:P], r_g[:, NB, :], ident).then_inc(BPE.sem(f"So_{d}"), 1)
                pe.wait_ge(b_dve, V(BDV, "bn"))
                pe.wait_ge(b_act, V(BAC, "so_1"))
                for c in range(2):
                    ins = nc.tensor.matmul(bank(2 + c)[:, 0:HALF], blk, r_e2[:, c * HALF:(c + 1) * HALF], start=True, stop=True)
                ins.then_inc(BPE.sem("bs"), 1)
                for c in range(2):
                    ins = nc.tensor.matmul(bank(4 + c)[:, 0:HALF], r_g2, big[:, T_G, c * HALF:(c + 1) * HALF], start=True, stop=True)
                ins.then_inc(BPE.sem("gate"), 1)
                for c in range(2):
                    ins = nc.tensor.matmul(bank(6 + c)[:, 0:HALF], blk, r_y[:, c * HALF:(c + 1) * HALF], start=True, stop=True)
                ins.then_inc(BPE.sem("mu"), 1)
                pe.wait_ge(b_act, V(BAC, "ysq"))
                for c in range(2):
                    ins = nc.tensor.matmul(bank(c)[:, 0:HALF], blk, r_sig[:, c * HALF:(c + 1) * HALF], start=True, stop=True)
                ins.then_inc(BPE.sem("var"), 1)

        def act_rwkv(act):
            act.wait_ge(ab_shift, 3 * AB_TILES)
            nc.scalar.activation(big[:, T_W, :], big[:, T_W, :], ACT.Tanh)
            nc.scalar.activation(big[:, T_G, :], big[:, T_G, :], ACT.Sigmoid)
            act.wait_ge(b_pe, 1)
            nc.scalar.activation(r_s0t, bank(0).rearrange("p (q n) -> p q n", n=HD), ACT.Copy).then_inc(b_act, 1)
            with act.Fori(0, BT) as it:
                def V(steps, name):
                    return steps.value(name, it)

                act.wait_ge(b_act, BAC.before(it))
                act.wait_ge(b_dve, BDV.value("kkmul", it))
                nc.scalar.activation(r_v, big[:, it + T_V, :], ACT.Copy).then_inc(BAC.sem("vcopy"), 1)
                nc.scalar.activation(r_tb, r_kkn, ACT.Square).then_inc(BAC.sem("kksq"), 1)
                act.wait_ge(b_pe, V(BPE, "kkss"))
                nc.scalar.activation(halves(r_e1), pp[1][:, :, 0:HALF], ACT.Sqrt).then_inc(BAC.sem("kkroot"), 1)
                nc.scalar.activation(r_vtok[:, 0:4, :], bank(0).rearrange("p (c n) -> p c n", n=P), ACT.Copy)
                nc.scalar.activation(r_vtok[:, 4, :], bank(1)[:, 0:P], ACT.Copy).then_inc(BAC.sem("vtok"), 1)
                for d in range(2):
                    act.wait_ge(b_pe, V(BPE, f"z_{d}"))
                    nc.scalar.activation(halves(r_sig), pp[2][:, :, 0:HALF], ACT.Sigmoid, bias=cols3[:, it + (C_W0 + BT * d), :])
                    nc.scalar.activation(halves(r_a), pp[3][:, :, 0:HALF], ACT.Sigmoid, bias=cols3[:, it + (C_A0 + BT * d), :]
                                         ).then_inc(BAC.sem(f"sig_{d}"), 1)
                    act.wait_ge(b_dve, V(BDV, f"m_{d}"))
                    q, m = (r_cum.rearrange("p (c n) -> p c n", n=P), r_sig.rearrange("p (c n) -> p c n", n=P))
                    e1 = r_e1.rearrange("p (c n) -> p c n", n=P)
                    for out, src, sg in (((r_ar[:, :, 0, :], m, -1), (r_ar[:, :, 1, :], q, -1), (e1, q, 1)) if d == 0 else
                                         ((r_ar[:, :, 0, :], q, 1), (r_ar[:, :, 1, :], m, 1), (e1, m, -1))):
                        nc.scalar.activation(out, src, ACT.Exp, scale=sg * DECAY)
                    nc.scalar.activation(r_d1, r_ht, ACT.Exp, scale=-DECAY).then_inc(BAC.sem(f"ex_{d}"), 1)
                    act.wait_ge(b_pe, V(BPE, f"tr_{d}"))
                    av = r_av.rearrange("p (h c) n -> p c h n", h=2)
                    c3 = lambda a, n: a.rearrange("p (c n) -> p c n", n=n)
                    nc.scalar.activation(av[:, 0:4, :, 0:HD], bank(0).rearrange("p (c h n) -> p c h n", h=2, n=HD), ACT.Copy)
                    nc.scalar.activation(av[:, 4, :, 0:HD], c3(bank(1)[:, 0:P], HD), ACT.Copy)
                    nc.scalar.activation(r_btok[:, 0:3, :], c3(bank(1)[:, P:512], P), ACT.Copy)
                    nc.scalar.activation(r_btok[:, 3:5, :], c3(bank(2)[:, 0:256], P), ACT.Copy)
                    nc.scalar.activation(r_ktok[:, 0:2, :], c3(bank(2)[:, 256:512], P), ACT.Copy)
                    nc.scalar.activation(r_ktok[:, 2:5, :], c3(bank(3)[:, 0:384], P), ACT.Copy).then_inc(BAC.sem(f"tok_{d}"), 1)
                    act.wait_ge(b_pe, V(BPE, f"RV_{d}"))
                    nc.scalar.activation(r_av[:, 0:8, HD:P], c3(bank(6), HD), ACT.Copy)
                    nc.scalar.activation(r_av[:, 8:10, HD:P], c3(bank(7)[:, 0:P], HD), ACT.Copy).then_inc(BAC.sem(f"rv_{d}"), 1)
                    for _, lev, g in LX:
                        act.wait_ge(b_pe, V(BPE, f"X{lev}{g}_{d}"))
                        nc.scalar.activation(r_tt[:, slice(*GROUPS[g]), :], lv_bank("X", g, P), ACT.Copy
                                             ).then_inc(BAC.sem(f"x{lev}{g}_{d}"), 1)
                    act.wait_ge(b_pe, V(BPE, f"WU_{d}"))
                    nc.scalar.activation(r_nwu[:, 0:4, :], c3(bank(0), P), ACT.Copy, scale=-1.0)
                    nc.scalar.activation(r_nwu[:, 4:8, :], c3(bank(1), P), ACT.Copy, scale=-1.0)
                    nc.scalar.activation(r_nwu[:, 8:10, :], c3(bank(2)[:, 0:256], P), ACT.Copy, scale=-1.0
                                         ).then_inc(BAC.sem(f"wu_{d}"), 1)
                    if d == 0:
                        act.wait_ge(b_pe, V(BPE, "Y_0"))
                        nc.scalar.activation(r_y[:, 0:LAT], bank(0), ACT.Copy)
                        nc.scalar.activation(r_y[:, LAT:TOK], bank(1)[:, 0:P], ACT.Copy).then_inc(BAC.sem("y0"), 1)
                    act.wait_ge(b_pe, V(BPE, f"So_{d}"))
                    nc.scalar.activation(r_so[:, d, :], bank(2)[0:HD, 0:P], ACT.Copy).then_inc(BAC.sem(f"so_{d}"), 1)
                act.wait_ge(b_pe, V(BPE, "gate"))
                nc.scalar.activation(halves(r_gate), pp[2][:, :, 0:HALF], ACT.Copy).then_inc(BAC.sem("gt"), 1)
                act.wait_ge(b_dve, V(BDV, "yc"))
                nc.scalar.activation(r_sig, r_cum, ACT.Square).then_inc(BAC.sem("ysq"), 1)
                act.wait_ge(b_pe, V(BPE, "var"))
                nc.scalar.activation(halves(r_e1), pp[0][:, :, 0:HALF], ACT.Sqrt, scale=1.0 / HD, bias=eps[:, 1:2]
                                     ).then_inc(BAC.sem("sd"), 1)

        def dve_rwkv(dve):
            dve.wait_ge(b_act, 1)
            dve.wait_ge(b_load, 48)
            dve.wait_ge(a_out, 32)
            v = nc.vector
            v.memset(r_ft2, 0.0)
            v.memset(r_ft1, 0.0).then_inc(b_dve, 1)
            dve.wait_ge(b_dve, 1)
            with dve.Fori(0, BT) as it:
                def V(steps, name):
                    return steps.value(name, it)


                def own(name):
                    dve.wait_ge(b_dve, V(BDV, name))

                dve.wait_ge(b_act, BAC.before(it))
                v.tensor_scalar(r_kkn, big[:, it + T_K, :], cols3[:, it + C_KK, :], None, ALU.mult).then_inc(BDV.sem("kkmul"), 1)
                dve.wait_ge(b_act, V(BAC, "kkroot"))
                v.tensor_scalar(r_e1, r_e1, 1e-12, None, ALU.max).then_inc(BDV.sem("kkmax"), 1)
                own("kkmax")
                v.reciprocal(r_e1, r_e1).then_inc(BDV.sem("kkrec"), 1)
                own("kkrec")
                v.tensor_tensor(r_kkn, r_kkn, r_e1, ALU.mult).then_inc(BDV.sem("kkn"), 1)
                for d in range(2):
                    n = lambda a, d=d: f"{a}_{d}"
                    dve.wait_ge(b_act, V(BAC, n("sig")))
                    v.tensor_tensor_scan(r_cum, r_reset, r_sig, 0.0, ALU.mult, ALU.add).then_inc(BDV.sem(n("cum")), 1)
                    own(n("cum"))
                    cum3 = r_cum.rearrange("p (c n) -> p c n", n=P)
                    v.tensor_scalar(r_ht, cum3[:, :, P - 1], 0.5, None, ALU.mult).then_inc(BDV.sem(n("ht")), 1)
                    own(n("ht"))
                    v.tensor_tensor(cum3, cum3, r_ht.unsqueeze(2).to_broadcast([P, NCH, P]), ALU.subtract
                                    ).then_inc(BDV.sem(n("q")), 1)
                    own(n("q"))
                    v.tensor_tensor(r_sig, r_cum, r_sig, ALU.subtract).then_inc(BDV.sem(n("m")), 1)
                    v.tensor_scalar(r_e2, r_a, cols3[:, it + C_KA, :], kam3[:, it, :], ALU.mult, ALU.add
                                    ).then_inc(BDV.sem(n("kd1")), 1)
                    own(n("kd1"))
                    kd = r_kd if d else r_kds
                    v.tensor_tensor(kd, r_e2, big[:, it + T_K, :], ALU.mult).then_inc(BDV.sem(n("kd")), 1)
                    own(n("kd"))
                    dve.wait_ge(b_act, V(BAC, n("ex")))
                    al, rh = r_ar[:, :, 0, :], r_ar[:, :, 1, :]
                    b3 = lambda a: a.rearrange("p (c n) -> p c n", n=P)
                    v.tensor_tensor(al, al, b3(r_kkn), ALU.mult)
                    v.tensor_tensor(rh, rh, b3(big[:, it + T_R, :]), ALU.mult)
                    v.tensor_tensor(r_kappa, kd, r_e1, ALU.mult)
                    if d:
                        v.tensor_tensor(r_kds, r_kds, kd, ALU.add)
                    lo, hi = (0, 1) if d == 0 else (1, 0)
                    v.tensor_tensor(r_dd[:, lo:lo + 3], r_d1[:, lo:lo + 3], r_d1[:, hi:hi + 3], ALU.mult)
                    v.tensor_copy(r_dd[:, NB:NCH], r_d1[:, NB:NCH])
                    v.tensor_copy(r_dd[:, 3 * (1 - d):3 * (1 - d) + 1], r_d1[:, 0:1])
                    v.tensor_tensor(r_a, r_kkn, r_a, ALU.mult).then_inc(BDV.sem(n("arr")), 1)
                    own(n("arr"))
                    v.tensor_tensor(r_beta, r_a, r_e1, ALU.mult).then_inc(BDV.sem(n("beta")), 1)
                    for u in range(NU):
                        dve.wait_ge(b_pe, V(BPE, n(f"pr{u}")))
                        v.tensor_tensor(r_u4[:, u, :, :].rearrange("p m n -> p (m n)"), bank(4 + u % 4), r_mask[d], ALU.mult
                                        ).then_inc(BDV.sem(n(f"U{u}")), 1)
                    dve.wait_ge(b_pe, V(BPE, n("A")))
                    ma = r_mask[1 - d][:, 0:P].unsqueeze(1)
                    for q, (a, b) in enumerate(((0, 4), (4, 5), (5, 9), (9, 10))):
                        ins = v.tensor_tensor(r_am[:, a:b, :], bank(q)[:, 0:(b - a) * P].rearrange("p (u n) -> p u n", n=P),
                                              ma.to_broadcast([P, b - a, P]), ALU.mult)
                    ins.then_inc(BDV.sem(n("Am")), 1)
                    v.tensor_copy(r_t, ident.unsqueeze(1).to_broadcast([P, NU, P]))
                    v.tensor_copy(r_tt, ident.unsqueeze(1).to_broadcast([P, NU, P]))
                    own(n("Am"))
                    hp, hn, mp, mn = sides(d)
                    wide = lambda m, lev, k: m[:, lev, :].unsqueeze(1).to_broadcast([P, k, HD])
                    at = r_u4[:, :, 0, :]
                    v.tensor_tensor(r_p, level_cols(r_am, 0, hp)[:, :, :, 0], wide(mp, 0, NU), ALU.mult)
                    v.tensor_tensor(r_n, at.rearrange("p u (k two) -> p u k two", two=2)[:, :, :, hn], wide(mn, 0, NU),
                                    ALU.mult).then_inc(BDV.sem(n("id")), 1)
                    own(n("id"))
                    tc, ttc = level_cols(r_t, 0, hp)[:, :, :, 0], level_cols(r_tt, 0, hn)[:, :, :, 0]
                    v.tensor_tensor(tc, tc, r_p, ALU.subtract)
                    v.tensor_tensor(ttc, ttc, r_n, ALU.subtract).then_inc(BDV.sem(n("T0")), 1)
                    for k, lev, g in LV:
                        if k == "X":
                            continue
                        us = slice(*GROUPS[g])
                        nu = us.stop - us.start
                        dve.wait_ge(b_pe, V(BPE, n(f"{k}{lev}{g}")))
                        if k == "P":
                            dst = r_p[:, us, :].rearrange("p u (k b) -> p u k b", b=1 << lev)
                            m = mp[:, lev, :].rearrange("p (k b) -> p k b", b=1 << lev).unsqueeze(1)
                            v.tensor_tensor(dst, level_cols(lv_bank(k, g, P), lev, hp), m.to_broadcast([P, nu, HD >> lev, 1 << lev]),
                                            ALU.mult).then_inc(BDV.sem(n(f"pn{lev}{g}")), 1)
                        elif k == "N":
                            v.tensor_tensor(r_n[:, us, :], lv_bank(k, g, HD), wide(mn, lev, nu), ALU.mult
                                            ).then_inc(BDV.sem(n(f"pn{lev}{g}")), 1)
                        else:
                            src = lv_bank(k, g, HD).rearrange("p u (k b) -> p u k b", b=1 << lev)
                            dst = level_cols(r_t[:, us, :], lev, hp) if k == "Q" else level_cols(r_tt[:, us, :], lev, hn)
                            v.tensor_tensor(dst, dst, src, ALU.subtract).then_inc(BDV.sem(n(f"t{lev}{g}")), 1)
                    dve.wait_ge(b_pe, V(BPE, n("FG")))
                    order = chunks(d)
                    for r in (slice(0, HD), slice(HD, P)):
                        v.tensor_tensor(r_ft2[r, :, r], bank(3)[r, 0:2 * HD].rearrange("p (c n) -> p c n", n=HD),
                                        r_eye2[r].unsqueeze(1).to_broadcast([HD, 2, HD]), ALU.add)
                        v.tensor_tensor(r_ft1[r, r], bank(3)[r, 2 * HD:3 * HD], r_eye2[r], ALU.add)
                    v.tensor_tensor(r_g, bank(4)[:, 0:NCH * HD].rearrange("p (c n) -> p c n", n=HD),
                                    r_dd.unsqueeze(2).to_broadcast([P, NCH, HD]), ALU.mult)
                    v.tensor_tensor(r_rhop.rearrange("p (c n) -> p c n", n=P), bank(5).rearrange("p (c n) -> p c n", n=P),
                                    r_ar[:, 0:NB, 1, :], ALU.add)
                    f = order[0]
                    v.tensor_scalar(r_z[:, f, :], r_s0t[:, it + BT * d, :], r_d1[:, f:f + 1], None, ALU.mult
                                    ).then_inc(BDV.sem(n("FG")), 1)
                    for i in range(3):
                        c, nx = order[i], order[i + 1]
                        dve.wait_ge(b_pe, V(BPE, n(f"S{i}")))
                        if i == 0:
                            own(n("FG"))
                        v.scalar_tensor_tensor(out=r_z[:, nx, :], in0=bank(7)[:, i * HD:(i + 1) * HD], scalar=r_dd[:, c:c + 1],
                                               in1=r_g[:, c, :], op0=ALU.mult, op1=ALU.add).then_inc(BDV.sem(n(f"Z{i}")), 1)
                dve.wait_ge(b_pe, V(BPE, "Y_1"))
                dve.wait_ge(b_act, V(BAC, "y0"))
                v.tensor_tensor(r_y[:, 0:LAT], r_y[:, 0:LAT], bank(0), ALU.add)
                v.tensor_tensor(r_y[:, LAT:TOK], r_y[:, LAT:TOK], bank(1)[:, 0:P], ALU.add).then_inc(BDV.sem("y1"), 1)
                v.scalar_tensor_tensor(out=r_e2, in0=big[:, it + T_R, :], scalar=cols3[:, it + C_RK, :], in1=r_kds,
                                       op0=ALU.mult, op1=ALU.mult).then_inc(BDV.sem("bn"), 1)
                dve.wait_ge(b_pe, V(BPE, "bs"))
                v.tensor_tensor(halves(r_bonus), pp[1][:, :, 0:HALF], halves(r_v), ALU.mult).then_inc(BDV.sem("bonus"), 1)
                dve.wait_ge(b_pe, V(BPE, "mu"))
                v.scalar_tensor_tensor(out=halves(r_cum), in0=pp[3][:, :, 0:HALF], scalar=-1.0 / HD, in1=halves(r_y),
                                       op0=ALU.mult, op1=ALU.add).then_inc(BDV.sem("yc"), 1)
                dve.wait_ge(b_act, V(BAC, "sd"))
                v.reciprocal(r_e1, r_e1).then_inc(BDV.sem("rs"), 1)
                own("rs")
                v.tensor_tensor(r_cum, r_cum, r_e1, ALU.mult).then_inc(BDV.sem("yn"), 1)
                own("yn")
                v.tensor_scalar(r_cum, r_cum, cols3[:, it + C_GNW, :], cols3[:, it + C_GNB, :], ALU.mult, ALU.add
                                ).then_inc(BDV.sem("yg"), 1)
                own("yg")
                v.tensor_tensor(r_cum, r_cum, r_bonus, ALU.add).then_inc(BDV.sem("yb"), 1)
                own("yb")
                v.tensor_tensor(big[:, it + T_R, :], r_cum, r_gate, ALU.mult).then_inc(BDV.sem("yo"), 1)

        LAM_INIT = 0.8 - 0.6 * math.exp(-0.3)
        c_keys, c_q, c_qp = hh[:, 0:640], hh[:, 640:1152], hh[:, 1152:1280]
        c_v = hh[:, 1280:1920]
        c_vtok = hh[:, 1920:2560].rearrange("p (c n) -> p c n", n=P)
        c_kout, c_vpast, c_kpast = hh[:, 2560:2688], hh[:, 2688:2816], hh[:, 2816:2944]
        c_t1 = hh[:, 2944:3968].rearrange("p (a n) -> p a n", a=2)
        c_t2 = hh[:, 3968:4992].rearrange("p (a n) -> p a n", a=2)
        NQ = NB + 1
        c_mxa, c_mxb, c_mx, c_neg, c_da, c_db, c_den, c_rd = (
            hh[:, 4992 + 2 * NQ * i:4992 + 2 * NQ * (i + 1)].rearrange("p (b m) -> p b m", m=2) for i in range(8))
        c_e = hl[:, 0:2560].rearrange("p (q m n) -> p q m n", q=2, m=2)
        c_a = hl[:, 2560:3840].rearrange("p (q n) -> p q n", q=2)
        c_t = hl[:, 3840:4480]
        c_at = wh[:, 0:2560].rearrange("p (i n) -> p i n", i=5)
        c_atp = wh[:, 2560:2688]
        c_o, c_sq = wh[:, 2688:3328], wh[:, 3328:3968]
        c_rs = wl[:, 0:640]
        c_lq = wl[:, 640:896].rearrange("p (a n) -> p a n", n=HD)
        c_lp = wl[:, 896:1024].rearrange("p (a n) -> p a n", n=HD)
        c_ls, c_le = wl[:, 1024:1026], wl[:, 1026:1028]
        c_kp = wl[:, 1032:1160]
        c_l1 = wl[:, 1160:1160 + NQ]
        nlam, csub = small[:, 28:29], small[:, 29:30]

        c_load, c_lam, c_pe, c_act, c_dve, c_out = (sem(f"c_{n}") for n in ("load", "lam", "pe", "act", "dve", "out"))
        ORDER = [("s", 0), ("s", 1), ("t", 0), ("s", 2), ("t", 1), ("s", 3), ("t", 2), ("s", 4), ("t", 3), ("t", 4)]
        CPE = Steps(c_pe, ["rot", "kt", "vt"] + [("sc" if a == "s" else "tr") + str(b) for a, b in ORDER] + ["pv", "ms"], 0)
        CAC = Steps(c_act, ["cp", "kt", "vt"] + [("ex" if a == "s" else "at") + str(b) for a, b in ORDER] + ["o", "sq", "rt"], 1)
        CDV = Steps(c_dve, ["r1", "r2"] + [n + str(b) for a, b in ORDER for n in
                    (("mx", "m2", "ng") if a == "s" else ("dn", "rd", "lm", "tm", "A"))] + ["rc", "fin"], 4)

        def c_main(b):
            return pp[2 * (b % 2)]

        def c_rest(b, m):
            return pp[2 * (b % 2) + 1][:, m, 0:P]

        def c_turn(b, i):
            return pp[2 * (b % 2) + 1][:, i // 3, (i % 3 + 1) * P:(i % 3 + 2) * P]

        def sp_attn_c(sp):
            sp.wait_ge(slab_used, IN_C + C_TILES + RING)
            for i, name in enumerate(("c_lq1", "c_lq2", "c_lk1", "c_lk2")):
                sp.dma_start(c_lq[:, i, :], T[name].to_broadcast([P, HD])).then_inc(c_lam, 16)
            kc = T["cache_c_k"][0, 0]
            vc = T["cache_c_v"][0, 0]
            with sp.Fori(0, CH) as h:
                sp.wait_ge(c_act, CAC.before(h))
                sp.wait_ge(c_out, 32 * h + 32)
                sp.dma_start(c_kpast, kc[:, h, :]).then_inc(c_load, 16)
                sp.dma_start(c_vpast, vc[:, h, :]).then_inc(c_load, 16)
                sp.wait_ge(c_act, CAC.value("vt", h))
                sp.dma_start(T["new_c_k"][0, 0][:, h, :], c_kout).then_inc(c_out, 16)
                sp.dma_start(T["new_c_v"][0, 0][:, h, :], c_vtok[:, 4, :]).then_inc(c_out, 16)

        def pe_attn_c(pe):
            pe.wait_ge(pair_free, IN_C + C_TILES + RING)
            with pe.Fori(0, CH) as h:
                def V(steps, name):
                    return steps.value(name, h)

                pe.wait_ge(c_act, CAC.before(h))
                pe.wait_ge(c_dve, CDV.before(h))
                nc.tensor.matmul(pp[0][:, 0, :], rot, big[:, h, 0:LAT], start=True, stop=True)
                nc.tensor.matmul(pp[0][:, 1, :], rot, big[:, h + CH, 0:LAT], start=True, stop=True).then_inc(CPE.sem("rot"), 1)
                pe.wait_ge(c_act, V(CAC, "cp"))
                pe.wait_ge(c_load, 32 * h + 32)
                nc.tensor.transpose(pp[1][:, 0, 0:P], c_kpast, ident)
                nc.tensor.transpose(pp[1][:, 0, P:2 * P], c_kp, ident).then_inc(CPE.sem("kt"), 1)
                for c in range(NCH):
                    ins = nc.tensor.transpose(pp[2][:, c // 4, c % 4 * P:c % 4 * P + P], c_v[:, c * P:(c + 1) * P], ident)
                ins.then_inc(CPE.sem("vt"), 1)
                for kind, b in ORDER:
                    if kind == "s":
                        if b == 0:
                            pe.wait_ge(c_dve, V(CDV, "r2"))
                            pe.wait_ge(c_act, V(CAC, "vt"))
                        elif b >= 2:
                            pe.wait_ge(c_act, V(CAC, f"at{b - 2}"))
                        for m in range(2):
                            r = slice(m * HD, m * HD + HD)
                            if b < NB:
                                q = c_q[r, b * P:(b + 1) * P]
                                nc.tensor.matmul(c_main(b)[:, m, :], q, c_keys[r, 0:512], start=True, stop=True)
                                ins = nc.tensor.matmul(c_rest(b, m), q, c_keys[r, 512:640], start=True, stop=True)
                            else:
                                ins = nc.tensor.matmul(c_rest(b, m), c_qp[r, :], c_kp[r, :],
                                                       start=True, stop=True)
                        ins.then_inc(CPE.sem(f"sc{b}"), 1)
                    else:
                        pe.wait_ge(c_dve, V(CDV, f"A{b}"))
                        for i in range(5 if b < NB else 1):
                            ins = nc.tensor.transpose(c_turn(b, i), c_a[:, b % 2, i * P:(i + 1) * P], ident)
                        ins.then_inc(CPE.sem(f"tr{b}"), 1)
                pe.wait_ge(c_act, V(CAC, "at4"))
                for i in range(5):
                    nc.tensor.matmul(pp[0][:, 0, :], c_vtok[:, i - 1, :] if i else c_vpast, c_at[:, i, :],
                                     start=(i == 0), stop=(i == 4))
                nc.tensor.matmul(pp[0][:, 1, 0:P], c_vtok[:, 4, :], c_atp, start=True, stop=True).then_inc(CPE.sem("pv"), 1)
                pe.wait_ge(c_act, V(CAC, "sq"))
                for c in range(2):
                    ins = nc.tensor.matmul(pp[2][:, c, 0:HALF], mean_p, c_sq[:, c * HALF:(c + 1) * HALF], start=True, stop=True)
                ins.then_inc(CPE.sem("ms"), 1)

        def act_attn_c(act):
            act.wait_ge(c_dve, 2)
            act.wait_ge(pair_free, IN_C + C_TILES + RING)
            nc.scalar.activation(c_le, c_ls, ACT.Exp).then_inc(c_act, 1)
            with act.Fori(0, CH) as h:
                def V(steps, name):
                    return steps.value(name, h)

                act.wait_ge(c_dve, CDV.before(h))
                nc.scalar.activation(c_qp, big[:, h, LAT:TOK], ACT.Copy)
                nc.scalar.activation(c_kp, big[:, h + CH, LAT:TOK], ACT.Copy)
                nc.scalar.activation(c_v, big[:, h + 2 * CH, :], ACT.Copy).then_inc(CAC.sem("cp"), 1)
                act.wait_ge(c_pe, V(CPE, "kt"))
                nc.scalar.activation(c_keys[:, 0:P], pp[1][:, 0, 0:P], ACT.Copy)
                nc.scalar.activation(c_kout, pp[1][:, 0, P:2 * P], ACT.Copy).then_inc(CAC.sem("kt"), 1)
                act.wait_ge(c_pe, V(CPE, "vt"))
                nc.scalar.activation(c_vtok[:, 0:4, :], pp[2][:, 0, :].rearrange("p (c n) -> p c n", n=P), ACT.Copy)
                nc.scalar.activation(c_vtok[:, 4, :], pp[2][:, 1, 0:P], ACT.Copy).then_inc(CAC.sem("vt"), 1)
                for kind, b in ORDER:
                    if kind == "s":
                        act.wait_ge(c_dve, V(CDV, f"ng{b}"))
                        for m in range(2):
                            bias = c_neg[:, b, m:m + 1]
                            if b < NB:
                                nc.scalar.activation(c_e[:, b % 2, m, 0:512], c_main(b)[:, m, :], ACT.Exp, bias=bias, scale=SCALE,
                                                     accum_out=c_da[:, b, m:m + 1])
                                ins = nc.scalar.activation(c_e[:, b % 2, m, 512:640], c_rest(b, m), ACT.Exp,
                                                           bias=bias, scale=SCALE, accum_out=c_db[:, b, m:m + 1])
                            else:
                                ins = nc.scalar.activation(c_e[:, b % 2, m, 0:P], c_rest(b, m), ACT.Exp,
                                                           bias=bias, scale=SCALE, accum_out=c_den[:, b, m:m + 1])
                        ins.then_inc(CAC.sem(f"ex{b}"), 1)
                    else:
                        act.wait_ge(c_pe, V(CPE, f"tr{b}"))
                        if b < NB:
                            ps = pp[2 * (b % 2) + 1]
                            nc.scalar.activation(c_at[:, 0:3, b * P:(b + 1) * P], ps[:, 0, P:4 * P].rearrange(
                                "p (i n) -> p i n", n=P), ACT.Copy)
                            nc.scalar.activation(c_at[:, 3:5, b * P:(b + 1) * P], ps[:, 1, P:3 * P].rearrange(
                                "p (i n) -> p i n", n=P), ACT.Copy).then_inc(CAC.sem(f"at{b}"), 1)
                        else:
                            nc.scalar.activation(c_atp, c_turn(b, 0), ACT.Copy).then_inc(CAC.sem("at4"), 1)
                act.wait_ge(c_pe, V(CPE, "pv"))
                nc.scalar.activation(c_o[:, 0:LAT], pp[0][:, 0, :], ACT.Copy)
                nc.scalar.activation(c_o[:, LAT:TOK], pp[0][:, 1, 0:P], ACT.Copy).then_inc(CAC.sem("o"), 1)
                act.wait_ge(c_act, V(CAC, "o"))
                nc.scalar.activation(c_sq, c_o, ACT.Square).then_inc(CAC.sem("sq"), 1)
                act.wait_ge(c_pe, V(CPE, "ms"))
                nc.scalar.activation(halves(c_rs), pp[2][:, :, 0:HALF], ACT.Sqrt, bias=eps[:, 2:3]).then_inc(CAC.sem("rt"), 1)

        def dve_attn_c(dve):
            v = nc.vector
            dve.wait_ge(c_lam, 64)
            v.tensor_tensor(c_lp, c_lq[:, 0:2, :], c_lq[:, 2:4, :], ALU.mult).then_inc(c_dve, 1)
            dve.wait_ge(c_dve, 1)
            v.tensor_reduce(c_ls, c_lp, AX.X, ALU.add).then_inc(c_dve, 1)
            dve.wait_ge(c_act, 1)
            v.tensor_scalar(nlam, c_le[:, 1:2], -LAM_INIT, None, ALU.add)
            v.tensor_scalar(csub, col(C_SUB), 1.0 - LAM_INIT, None, ALU.mult).then_inc(c_dve, 1)
            dve.wait_ge(c_dve, 3)
            v.tensor_tensor(nlam, nlam, c_le[:, 0:1], ALU.subtract).then_inc(c_dve, 1)
            with dve.Fori(0, CH) as h:
                def V(steps, name):
                    return steps.value(name, h)


                def own(name):
                    dve.wait_ge(c_dve, V(CDV, name))

                dve.wait_ge(c_dve, CDV.before(h))
                v.tensor_tensor(c_t1[:, 0, :], big[:, h, 0:LAT], cos, ALU.mult)
                v.tensor_tensor(c_t1[:, 1, :], big[:, h + CH, 0:LAT], cos, ALU.mult)
                dve.wait_ge(c_pe, V(CPE, "rot"))
                v.tensor_tensor(c_t2, pp[0][:, :, :], sin.unsqueeze(1).to_broadcast([P, 2, LAT]), ALU.mult
                                ).then_inc(CDV.sem("r1"), 1)
                own("r1")
                v.tensor_tensor(c_q, c_t1[:, 0, :], c_t2[:, 0, :], ALU.add)
                v.tensor_tensor(c_keys[:, P:TOK], c_t1[:, 1, :], c_t2[:, 1, :], ALU.add).then_inc(CDV.sem("r2"), 1)
                for kind, b in ORDER:
                    if kind == "s":
                        dve.wait_ge(c_pe, V(CPE, f"sc{b}"))
                        if b < NB:
                            v.tensor_reduce(c_mxa[:, b, :], c_main(b)[:, :, :], AX.X, ALU.max)
                        v.tensor_reduce(c_mxb[:, b, :], pp[2 * (b % 2) + 1][:, :, 0:P], AX.X, ALU.max
                                        ).then_inc(CDV.sem(f"mx{b}"), 1)
                        own(f"mx{b}")
                        v.tensor_tensor(c_mx[:, b, :], (c_mxa if b < NB else c_mxb)[:, b, :], c_mxb[:, b, :], ALU.max
                                        ).then_inc(CDV.sem(f"m2{b}"), 1)
                        own(f"m2{b}")
                        v.tensor_scalar(c_neg[:, b, :], c_mx[:, b, :], -SCALE, None, ALU.mult).then_inc(CDV.sem(f"ng{b}"), 1)
                    else:
                        n = TOK if b < NB else P
                        dve.wait_ge(c_act, V(CAC, f"ex{b}"))
                        if b < NB:
                            v.tensor_tensor(c_den[:, b, :], c_da[:, b, :], c_db[:, b, :], ALU.add).then_inc(CDV.sem(f"dn{b}"), 1)
                            own(f"dn{b}")
                        else:
                            v.tensor_copy(c_da[:, b, :], c_den[:, b, :]).then_inc(CDV.sem(f"dn{b}"), 1)
                        v.reciprocal(c_rd[:, b, :], c_den[:, b, :]).then_inc(CDV.sem(f"rd{b}"), 1)
                        own(f"rd{b}")
                        v.tensor_tensor(c_l1[:, b:b + 1], c_rd[:, b, 1:2], nlam, ALU.mult).then_inc(CDV.sem(f"lm{b}"), 1)
                        own(f"lm{b}")
                        v.tensor_scalar(c_t[:, 0:n], c_e[:, b % 2, 1, 0:n], c_l1[:, b:b + 1], None, ALU.mult
                                        ).then_inc(CDV.sem(f"tm{b}"), 1)
                        own(f"tm{b}")
                        v.scalar_tensor_tensor(out=c_a[:, b % 2, 0:n], in0=c_e[:, b % 2, 0, 0:n], scalar=c_rd[:, b, 0:1],
                                               in1=c_t[:, 0:n], op0=ALU.mult, op1=ALU.add).then_inc(CDV.sem(f"A{b}"), 1)
                dve.wait_ge(c_act, V(CAC, "rt"))
                v.reciprocal(c_rs, c_rs).then_inc(CDV.sem("rc"), 1)
                own("rc")
                v.scalar_tensor_tensor(out=big[:, h, :], in0=c_o, scalar=csub, in1=c_rs, op0=ALU.mult, op1=ALU.mult
                                       ).then_inc(CDV.sem("fin"), 1)

        MIXED = {0: [(b_dve, BDV.before(BT)), (a_act, AAC.before(4))], 1: [(c_dve, CDV.before(CH)), (c_out, 32 * CH + 32)]}

        loads = []
        loads.append((base[:, :], T["t_base"]))
        loads.append((x_rows[:, 0:4, :], T["x_sample"][0].rearrange("(t p) n -> p t n", p=P)))
        loads.append((x_rows[:, 4, :], T["x_prompt"][0]))
        r0, r1, r2 = rows
        v = lambda a: a.rearrange("(r c) -> r c", c=P)
        loads.append((r0[C_NORM:C_NORM + 48, :], T["norms"].rearrange("l s (r c) -> (l s r) c", c=P)))
        loads.append((r0[C_FINAL:C_FINAL + 8, :], v(T["final_norm"])))
        loads.append((r0[C_MUP + 4:C_MUP + 19, :], v(T["b_mu_prev"][0])))
        loads.append((r0[C_MUN + 4:C_MUN + 19, :], v(T["b_mu_next"][0])))
        loads.append((r0[C_W0:C_W0 + 8, :], T["b_w0"][0].rearrange("d (r c) -> (d r) c", c=P)))
        loads.append((r0[C_A0:C_A0 + 8, :], T["b_a0"][0].rearrange("d (r c) -> (d r) c", c=P)))
        loads.append((r0[C_KK:C_KK + 4, :], v(T["b_k_k"][0])))
        loads.append((r0[C_KA:C_KA + 4, :], v(T["b_k_a"][0])))
        loads.append((r0[C_RK:C_RK + 4, :], T["b_r_k"][0].rearrange("(r two) c -> r (two c)", two=2)))
        o = -P
        loads.append((r1[C_GNW + o:C_GNW + o + 4, :], v(T["b_gn_w"][0])))
        loads.append((r1[C_GNB + o:C_GNB + o + 4, :], v(T["b_gn_b"][0])))
        loads.append((r1[C_SUB + o:C_SUB + o + 1, :], T["c_subln"]))
        loads.append((r1[C_COND + o:C_COND + o + 8, :], v(T["c"][0])))
        loads.append((r1[C_COND + o + 8:C_COND + o + 16, :], v(T["c_ctx"])))
        mb = T["mod_b"].rearrange("l (r c) -> (l r) c", c=P)
        loads.append((r1[C_MODB + o:C_MODB + o + 16, :], mb[P:P + 16, :]))
        loads.append((r2, mb[0:P, :]))
        loads.append((attn[:, :], T["t_attn"]))
        LOADS = len(loads)

        block = ctx.enter_context(nc.Block())

        @block.sync
        def _(sp):
            def weights(key, cnt):
                kind, l, f, b = key
                n0 = start[key]

                def slab(i, j, src):
                    sp.wait_ge(lo_full, 4 * i + (j + 1))
                    sp.dma_start(raw[:, j % RING, :, :], src).then_inc(raw_full[j % RING], 16)

                if kind == "up":
                    w1 = T["ffn_w1"][l, f].rearrange("(k p) (t w) -> p k t w", p=P, w=W)
                    w3 = T["ffn_w3"][l, f].rearrange("(k p) (t w) -> p k t w", p=P, w=W)
                    t0 = BLOCKS[b][0]
                    with sp.Fori(0, cnt // 4) as i:
                        for j in range(4):
                            src = (w1 if j % 2 == 0 else w3)[:, :, 2 * i + (t0 + j // 2), :]
                            slab(i, n0 + j, src)
                elif kind == "down":
                    r0 = min(BLOCKS[b][0], FT - DT) * P
                    w2 = T["ffn_w2"][l, f][r0:r0 + D, :].rearrange("(k p) (t w) -> p k t w", p=P, w=W)
                    with sp.Fori(0, cnt // 4) as i:
                        for j in range(4):
                            slab(i, n0 + j, w2[:, :, 4 * i + j, :])
                else:
                    src = {("in", 0): "w_in_ab", ("in", 1): "w_in_c", ("out", 0): "w_out_ab", ("out", 1): "w_out_c"}
                    v = T[src[kind, l % 2]][l // 2].rearrange("(k p) (t w) -> p k t w", p=P, w=W)
                    for j in range(cnt):
                        c = AB_COLUMN[j] if (kind, l % 2) == ("in", 0) else j
                        slab(0, n0 + j, v[:, :, c, :])

            sp.wait_ge(s_zero, 2)
            for dst, src in loads:
                sp.dma_start(dst, src).then_inc(s_load, 16)
            mw = T["mod_w"].rearrange("l (k p) (t w) -> l p k t w", p=P, w=W)
            for l in range(DEPTH):
                with sp.Fori(0, NMOD * DT // 8) as i:
                    for j in range(8):
                        sp.wait_ge(m_used, 8 * i + (l * NMOD * DT + j + 1))
                        sp.dma_start(mod_ring[:, j % RING, :, :], mw[l][:, :, 8 * i + j, :]).then_inc(
                            mraw_full[j % RING], 16)
            for i in range(len(stages)):
                kind, l = stages[i][:2]
                if kind == "out":
                    if l % 2 == 0:
                        sp_attn_ab(sp)
                        sp_rwkv(sp)
                    else:
                        sp_attn_c(sp)
                weights(stages[i][:4], stages[i][4])
            n_out = 0
            for t in range(NCH):
                sp.wait_ge(y_ev, t + 1)
                dst = T["y_sample"][0, t * P:(t + 1) * P, :] if t < NB else T["y_prompt"][0]
                sp.dma_start(dst, x_rows[:, t, :]).then_inc(s_out, 16)
            sp.wait_ge(s_out, 16 * NCH)
            sp.wait_ge(a_out, 32)
            sp.wait_ge(b_out, 32 * BT + 32)
            sp.wait_ge(c_out, 32 * CH + 32)
        @block.scalar
        def _(act):
            def split_hi(i, j):
                act.wait_ge(raw_full[j % RING], 16 * i + (16 * (j // RING) + 16))
                act.wait_ge(slab_used, 4 * i + (j + 1))
                nc.scalar.activation(w_hi[:, j % RING, :, :], raw[:, j % RING, :, :], ACT.Copy).then_inc(hi_full, 1)

            act.wait_ge(s_load, 16 * LOADS)
            for t in range(NCH):
                act.wait_ge(s_tr, t + 1)
                dst = x[:, :, t * P:(t + 1) * P].rearrange("p (a b) c -> p a b c", a=2)
                nc.scalar.activation(dst, pp[t % 4][:, :, :].rearrange("p a (b c) -> p a b c", c=P), ACT.Copy).then_inc(s_ev, 1)
            act.wait_ge(s_tr, NCH + 1)
            nc.scalar.activation(cols[:, :], pp[1][:, 0, 0:C_END], ACT.Copy).then_inc(s_ev, 1)
            act.wait_ge(s_ev, NCH + 1)
            nc.scalar.activation(col(C_COND, 16), col(C_COND, 16), ACT.Silu).then_inc(s_cond, 1)

            def norm(k):
                l, s, u = norm_no[k]
                for t in range(DT):
                    if k:
                        act.wait_ge(pair_free, norm_at[k] + RING - DT + t + 1)
                    nc.scalar.activation(norm_t[:, t, :], x[:, t, :], ACT.Square).then_inc(n_sq, 1)
                act.wait_ge(n_sum, k + 1)
                nc.scalar.activation(halves(rt_t), pp[norm_at[k] % 4][:, :, 0:HALF], ACT.Sqrt, bias=eps[:, 0:1]).then_inc(n_root, 1)
                if k == NORMS - 1:
                    return
                sh = mod_at(l, 3 * s)
                for t in range(DT):
                    act.wait_ge(n_scaled, DT * k + t + 1)
                    for a, b, g in SEGS:
                        ins = nc.scalar.activation(h_hi[:, t, a:b], norm_t[:, t, a:b], ACT.Identity,
                                                   bias=mod[:, sh + t, g:g + 1])
                    ins.then_inc(n_hi, 1)

            def stage(i):
                kind, l, f, b, cnt = stages[i]
                key = stages[i][:4]
                n0 = start[key]
                ahead = LOOKAHEAD(i)
                if key in norm_before:
                    norm(norm_before[key])
                if FRESH(i):
                    split_hi(0, n0)
                    split_hi(0, n0 + 1)
                if kind == "up":
                    h0 = hid[key]
                    nc.scalar.preload_act_table(ACT.Silu)

                    def turn(i, last):
                        for e in range(2):
                            if not (last and e == 1 and not ahead):
                                for j in (2 * e + 2, 2 * e + 3):
                                    split_hi(i, n0 + j)
                            act.wait_ge(slab_used, 4 * i + (n0 + 2 * e + 1 + RING))
                            act.wait_ge(pair_free, 4 * i + (n0 + 2 * e + RING))
                            nc.scalar.activation(silu_t, pp[(n0 + 2 * e) % 4][:, :, 0:HALF], ACT.Silu).then_inc(silu_done, 1)
                            act.wait_ge(pair_free, 4 * i + (n0 + 2 * e + 2 + RING))
                            nc.scalar.activation(halves2(g_hi, 2 * i + e), prod_t, ACT.Copy).then_inc(ghi_done, 1)

                    loop_and_last(act, cnt // 4, turn)
                elif kind in ("down", "out"):
                    for j in range(cnt):
                        if j + 2 < cnt or ahead:
                            split_hi(0, n0 + j + 2)
                elif l % 2 == 0:
                    for j in range(cnt):
                        if j + 2 < cnt or ahead:
                            split_hi(0, n0 + j + 2)
                        act.wait_ge(slab_used, n0 + j + 1 + RING)
                        if j >= 2:
                            act.wait_ge(ab_shift, 3 * (j - 1))
                        else:
                            act.wait_ge(ab_pad, 1)
                        ps = pp[(n0 + j) % 4]
                        dst = praw[j % 2]
                        nc.scalar.activation(dst[:, 1:321], ps[:, 0, 0:HALF], ACT.Copy)
                        nc.scalar.activation(dst[:, 321:513], ps[:, 1, 0:LAT - HALF], ACT.Copy)
                        nc.scalar.activation(dst[:, 515:643], ps[:, 1, LAT - HALF:HALF], ACT.Copy).then_inc(pair_free, 1)
                else:
                    for j in range(cnt):
                        if j + 2 < cnt or ahead:
                            split_hi(0, n0 + j + 2)
                        act.wait_ge(slab_used, n0 + j + 1 + RING)
                        nc.scalar.activation(halves(big[:, j, :]), pp[(n0 + j) % 4][:, :, 0:HALF], ACT.Copy).then_inc(pair_free, 1)

            def split_out(m):
                for t in range(DT):
                    for q, value in MIXED[m]:
                        act.wait_ge(q, value)
                    nc.scalar.activation(h_hi[:, t, :], big[:, t, :], ACT.Copy).then_inc(o_hi, 1)

            for i in range(len(stages)):
                if stages[i][0] == "out":
                    (act_attn_ab if stages[i][1] % 2 == 0 else act_attn_c)(act)
                    if stages[i][1] % 2 == 0:
                        act_rwkv(act)
                    split_out(stages[i][1])
                stage(i)
            norm(NORMS - 1)
            for t in range(NCH):
                act.wait_ge(y_tr, t + 1)
                nc.scalar.activation(x_rows[:, t, :].rearrange("p (a b) -> p a b", a=2), pp[t % 4][:, :, :],
                                     ACT.Copy).then_inc(y_ev, 1)

        @block.vector
        def _(dve):
            def split_lo(i, j):
                dve.wait_ge(hi_full, 4 * i + (j + 1))
                nc.vector.tensor_tensor(w_lo[:, j % RING, :, :], raw[:, j % RING, :, :], f32(w_hi[:, j % RING, :, :]),
                                        ALU.subtract).then_inc(lo_full, 1)

            nc.vector.memset(R[:, 0:3 * P], 0.0).then_inc(s_zero, 1)
            nc.vector.memset(eps[:, 0:1], 1e-6)
            nc.vector.memset(eps[:, 1:2], 64e-5)
            nc.vector.memset(eps[:, 2:3], 1e-5).then_inc(s_zero, 1)
            for i, (q, c) in enumerate(((lo_full, 4), (slab_used, 4), (pair_free, 4), (m_used, 4), (m_taken, 2), (g_ready, 1), (b_out, 32), (c_out, 32))):
                nc.vector.memset(eps[:, 3 + i:4 + i], 0.0).then_inc(q, c)
            for g in range(2 * DEPTH * NMOD * DT // 8):
                dve.wait_ge(m_used, 4 * g + 8)
                nc.vector.tensor_copy(mod[:, 4 * g:4 * g + 4, :], pp[2 + g % 2][:, 0, 0:8].rearrange("p (a b) -> p a b", b=2)
                                      ).then_inc(m_taken, 1)
            ALLG = 2 * DEPTH * NMOD * DT // 8
            dve.wait_ge(m_taken, ALLG + 2)
            dve.wait_ge(s_ev, NCH + 1)
            c = [0]

            def vec(ins):
                ins.then_inc(s_vec, 1)
                c[0] += 1

            vec(nc.vector.tensor_tensor(mod[:, 0:P, :], mod[:, 0:P, :], col(256, P).unsqueeze(2).to_broadcast([P, P, 2]), ALU.add))
            vec(nc.vector.tensor_tensor(mod[:, P:P + 16, :], mod[:, P:P + 16, :],
                                        col(C_MODB, 16).unsqueeze(2).to_broadcast([P, 16, 2]), ALU.add))
            vec(nc.vector.tensor_tensor(c0, col(C_MUP, AB_TILES), col(C_MUN, AB_TILES), ALU.add))
            vec(nc.vector.tensor_scalar(kam, col(C_KA, 4), -1.0, 1.0, ALU.mult, ALU.add))
            dve.wait_ge(s_vec, c[0])
            vec(nc.vector.tensor_scalar(c0, c0, -1.0, 1.0, ALU.mult, ALU.add))
            for l in range(DEPTH):
                for s in range(3):
                    sc = mod[:, mod_at(l, 3 * s + 1):mod_at(l, 3 * s + 1) + DT, :]
                    g_in = col(C_NORM + (3 * l + s) * DT, DT).unsqueeze(2).to_broadcast([P, DT, 2])
                    vec(nc.vector.scalar_tensor_tensor(out=sc, in0=sc, scalar=1.0, in1=g_in, op0=ALU.add, op1=ALU.mult))
                    if s != 1:
                        gt = mod[:, mod_at(l, 3 * s + 2):mod_at(l, 3 * s + 2) + DT, :]
                        vec(nc.vector.tensor_scalar(gt, gt, 0.5, None, ALU.mult))
            dve.wait_ge(s_vec, c[0])

            def norm(k):
                l, s, u = norm_no[k]
                dve.wait_ge(n_root, k + 1)
                nc.vector.reciprocal(rt_t, rt_t).then_inc(n_recip, 1)
                dve.wait_ge(n_recip, k + 1)
                last = k == NORMS - 1
                for t in range(DT):
                    for a, b, g in SEGS:
                        sc = col(C_FINAL + t) if last else mod[:, mod_at(l, 3 * s + 1) + t, g:g + 1]
                        ins = nc.vector.scalar_tensor_tensor(out=norm_t[:, t, a:b], in0=x[:, t, a:b], scalar=sc,
                                                             in1=rt_t[:, a:b], op0=ALU.mult, op1=ALU.mult)
                    ins.then_inc(n_scaled, 1)
                if last:
                    return
                sh = mod_at(l, 3 * s)
                for t in range(DT):
                    dve.wait_ge(n_hi, DT * k + t + 1)
                    for a, b, g in SEGS:
                        ins = nc.vector.scalar_tensor_tensor(out=h_lo[:, t, a:b], in0=norm_t[:, t, a:b],
                                                             scalar=mod[:, sh + t, g:g + 1], in1=f32(h_hi[:, t, a:b]),
                                                             op0=ALU.add, op1=ALU.subtract)
                    ins.then_inc(n_lo, 1)

            def stage(i):
                kind, l, f, b, cnt = stages[i]
                key = stages[i][:4]
                n0 = start[key]
                ahead = LOOKAHEAD(i)
                if key in norm_before:
                    norm(norm_before[key])
                if FRESH(i):
                    split_lo(0, n0)
                    split_lo(0, n0 + 1)
                if kind == "up":
                    h0 = hid[key]

                    def turn(i, last):
                        for e in range(2):
                            if not (last and e == 1 and not ahead):
                                for j in (2 * e + 2, 2 * e + 3):
                                    split_lo(i, n0 + j)
                            dve.wait_ge(slab_used, 4 * i + (n0 + 2 * e + 2 + RING))
                            dve.wait_ge(silu_done, 2 * i + (h0 + e + 1))
                            dve.wait_ge(g_ready, 2 * i + (h0 + e + 1))
                            nc.vector.tensor_tensor(prod_t, silu_t, pp[(n0 + 2 * e + 1) % 4][:, :, 0:HALF],
                                                    ALU.mult).then_inc(pair_free, 2)
                            dve.wait_ge(ghi_done, 2 * i + (h0 + e + 1))
                            nc.vector.tensor_tensor(halves2(g_lo, 2 * i + e), prod_t, f32(halves2(g_hi, 2 * i + e)),
                                                    ALU.subtract).then_inc(g_ready, 1)

                    loop_and_last(dve, cnt // 4, turn)
                elif kind in ("down", "out"):
                    gate = mod_at(l, 5 if kind == "out" else (2 if f == 0 else 8))
                    for j in range(cnt):
                        if j + 2 < cnt or ahead:
                            split_lo(0, n0 + j + 2)
                        dve.wait_ge(slab_used, n0 + j + 1 + RING)
                        if j == 0:
                            dve.wait_ge(pair_free, n0 + RING)
                        ps = pp[(n0 + j) % 4]
                        for (a, b2), src, g in (((0, HALF), ps[:, 0, 0:HALF], 0),
                                                ((HALF, LAT), ps[:, 1, 0:LAT - HALF], 0),
                                                ((LAT, TOK), ps[:, 1, LAT - HALF:HALF], 1)):
                            ins = nc.vector.scalar_tensor_tensor(out=x[:, j, a:b2], in0=src,
                                                                 scalar=mod[:, gate + j, g:g + 1], in1=x[:, j, a:b2],
                                                                 op0=ALU.mult, op1=ALU.add)
                        ins.then_inc(pair_free, 1)
                elif l % 2 == 0:
                    for q in range(2):
                        for z in (0, 513, 643):
                            w = 2 if z == 513 else 1
                            ins = nc.vector.memset(praw[q][:, z:z + w], 0.0)
                    ins.then_inc(ab_pad, 1)
                    for j in range(cnt):
                        if j + 2 < cnt or ahead:
                            split_lo(0, n0 + j + 2)
                        dve.wait_ge(pair_free, n0 + j + 1 + RING)
                        src = praw[j % 2]
                        for op in range(3):
                            if op:
                                dve.wait_ge(ab_shift, 3 * j + op)
                            for a, b2, o in ((0, LAT, 1), (LAT, TOK, 3)):
                                dst = big[:, j, a:b2]
                                if op == 0:
                                    ins = nc.vector.tensor_scalar(dst, src[:, a + o:b2 + o], c0[:, j:j + 1], None, ALU.mult)
                                else:
                                    d = -1 if op == 1 else 1
                                    mu = col((C_MUP if op == 1 else C_MUN) + j)
                                    ins = nc.vector.scalar_tensor_tensor(out=dst, in0=src[:, a + o + d:b2 + o + d], scalar=mu,
                                                                         in1=dst, op0=ALU.mult, op1=ALU.add)
                            ins.then_inc(ab_shift, 1)
                else:
                    for j in range(cnt):
                        if j + 2 < cnt or ahead:
                            split_lo(0, n0 + j + 2)

            def split_out(m):
                for t in range(DT):
                    dve.wait_ge(o_hi, DT * m + t + 1)
                    nc.vector.tensor_tensor(h_lo[:, t, :], big[:, t, :], f32(h_hi[:, t, :]), ALU.subtract).then_inc(o_lo, 1)

            for i in range(len(stages)):
                if stages[i][0] == "out":
                    (dve_attn_ab if stages[i][1] % 2 == 0 else dve_attn_c)(dve)
                    if stages[i][1] % 2 == 0:
                        dve_rwkv(dve)
                    split_out(stages[i][1])
                stage(i)
            norm(NORMS - 1)

        @block.tensor
        def _(pe):
            pe.wait_ge(s_load, 16 * LOADS)
            for t in range(NCH):
                if t == 4:
                    pe.wait_ge(s_ev, 1)
                for d in range(DT):
                    ins = nc.tensor.transpose(pp[t % 4][:, d // 4, (d % 4) * P:(d % 4 + 1) * P],
                                              x_rows[:, t, d * P:(d + 1) * P], ident)
                ins.then_inc(s_tr, 1)
            pe.wait_ge(s_ev, 2)
            for r in range(3):
                ins = nc.tensor.transpose(pp[1][:, 0, r * P:(r + 1) * P], rows[r], ident)
            ins.then_inc(s_tr, 1)
            pe.wait_ge(s_cond, 1)
            pe.wait_ge(s_ev, NCH + 1)
            cond = col(C_COND, 16).rearrange("p (g k) -> p k g", g=2)
            with pe.Fori(0, DEPTH * NMOD * DT // 8) as i:
                for j in range(8):
                    pe.wait_ge(mraw_full[j % RING], 32 * i + (16 * (j // RING) + 16))
                    if j % 4 == 0:
                        pe.wait_ge(m_taken, 2 * i + (j // 4 + 1))
                    for k in range(DT):
                        ins = nc.tensor.matmul(pp[2 + j // 4][:, 0, 2 * (j % 4):2 * (j % 4) + 2], mod_ring[:, j % RING, k, :],
                                               cond[:, k, :], start=(k == 0), stop=(k == DT - 1))
                    ins.then_inc(m_used, 1)

            def norm(k):
                pair = pp[norm_at[k] % 4]
                if k == 0:
                    pe.wait_ge(m_taken, 2 * DEPTH * NMOD * DT // 8 + 2)
                else:
                    pe.wait_ge(pair_free, norm_at[k] + 1)
                for t in range(DT):
                    pe.wait_ge(n_sq, DT * k + t + 1)
                    for c in range(2):
                        ins = nc.tensor.matmul(pair[:, c, 0:HALF], mean_d, norm_t[:, t, c * HALF:(c + 1) * HALF],
                                               start=(t == 0), stop=(t == DT - 1))
                ins.then_inc(n_sum, 1)

            def slab(i, j, kts, k0, xh, xl, wait_tile):
                pe.wait_ge(lo_full, 4 * i + (j + 1 + RING))
                pe.wait_ge(pair_free, 4 * i + (j + 1))
                ps = pp[j % 4]
                for k in range(kts):
                    if wait_tile:
                        wait_tile(k)
                    hi, lo = w_hi[:, j % RING, k + k0, :], w_lo[:, j % RING, k + k0, :]
                    for w, v in ((hi, xh), (hi, xl), (lo, xh)):
                        for c in range(2):
                            ins = nc.tensor.matmul(ps[:, c, 0:HALF], w, v[:, k, c * HALF:(c + 1) * HALF],
                                                   start=(k == 0 and w is hi and v is xh),
                                                   stop=(k == kts - 1 and w is lo))
                ins.then_inc(slab_used, 1)

            def stage(i):
                kind, l, f, b, cnt = stages[i]
                key = stages[i][:4]
                n0 = start[key]
                if key in norm_before:
                    norm(norm_before[key])
                k0, kts = 0, DT
                if kind == "down":
                    kts = BLOCKS[b][1]
                    k0 = BLOCKS[b][0] - min(BLOCKS[b][0], FT - DT)
                    xh, xl = g_hi, g_lo
                    tile_ready = lambda k: pe.wait_ge(g_ready, hid[key] - kts + k + 2)
                elif kind == "out":
                    xh, xl = h_hi, h_lo
                    tile_ready = lambda k: pe.wait_ge(o_lo, DT * l + k + 1)
                else:
                    xh, xl = h_hi, h_lo
                    kk = norm_before.get(key)
                    tile_ready = None if kk is None else (lambda k: pe.wait_ge(n_lo, DT * kk + k + 1))
                with pe.Fori(0, cnt // 4) as i2:
                    for j in range(4):
                        slab(i2, n0 + j, kts, k0, xh, xl, tile_ready if j == 0 else None)
                for j in range(cnt // 4 * 4, cnt):
                    slab(0, n0 + j, kts, k0, xh, xl, None)

            for i in range(len(stages)):
                if stages[i][0] == "out":
                    (pe_attn_ab if stages[i][1] % 2 == 0 else pe_attn_c)(pe)
                    if stages[i][1] % 2 == 0:
                        pe_rwkv(pe)
                stage(i)
            norm(NORMS - 1)
            for t in range(NCH):
                if t == 0:
                    pe.wait_ge(n_scaled, DT * NORMS)
                if t == 4:
                    pe.wait_ge(y_ev, 1)
                for d in range(DT):
                    ins = nc.tensor.transpose(pp[t % 4][:, d // 4, (d % 4) * P:(d % 4 + 1) * P],
                                              norm_t[:, d, t * P:(t + 1) * P], ident)
                ins.then_inc(y_tr, 1)


_INS = ["x_prompt", "x_sample", "c", "c_ctx", "cache_a_k", "cache_a_v", "state_b_wkv", "cache_c_k", "cache_c_v", "norms",
        "mod_w", "mod_b", "ffn_w1", "ffn_w3", "ffn_w2", "w_in_ab", "w_out_ab", "a_sink", "b_mu_prev", "b_mu_next", "b_w0",
        "b_w2", "b_a0", "b_a2", "b_k_k", "b_k_a", "b_r_k", "b_g2", "b_gn_w", "b_gn_b", "w_in_c", "w_out_c", "c_lq1",
        "c_lk1", "c_lq2", "c_lk2", "c_subln", "final_norm"]
_OUTS = [("y_prompt", (1, CTX, D)), ("y_sample", (1, LAT, D)), ("new_a_k", (1, 1, CTX, 2, HD)),
         ("new_a_v", (1, 1, CTX, 2, HD)), ("new_b_wkv", (1, 1, 2, 8, HD, HD)), ("new_c_k", (1, 1, CTX, CH, P)),
         ("new_c_v", (1, 1, CTX, CH, P))]


def kernel(**inputs):
    import concourse.bacc as _bacc
    from concourse.bass_utils import run_bass_kernel_spmd as _run

    nc = _bacc.Bacc("TRN2", target_bir_lowering=False, num_devices=1)
    arrays, T = {}, {}
    for name in _INS:
        arrays[name] = np.ascontiguousarray(inputs[name])
    for name, a in zip(("t_base", "t_attn", "t_rwkv"), tables()):
        arrays[name] = np.ascontiguousarray(a)
    for name, a in arrays.items():
        T[name] = nc.dram_tensor(name, a.shape, mybir.dt.from_np(a.dtype), kind="ExternalInput").ap()
    for name, shape in _OUTS:
        T[name] = nc.dram_tensor(name, shape, F32, kind="ExternalOutput").ap()
    build(nc, T)
    r = _run(nc, [arrays], core_ids=[0])
    return tuple(r.results[0][name] for name, _ in _OUTS)
```

```python
from contextlib import ExitStack
import math

import numpy as np

import concourse.bass as bass
from concourse import mybir

F32 = mybir.dt.float32
F32R = mybir.dt.float32r
ALU = mybir.AluOpType
ACT = mybir.ActivationFunctionType
AX = mybir.AxisListType

P = 128
D = 1024
DT = D // P
LAT, CTX = 512, 128
TOK = LAT + CTX
HALF = TOK // 2
NB = LAT // P
NCH = TOK // P
DEPTH = 2
FF = 2816
FT = FF // P
BLOCKS = [(0, 8), (8, 8), (16, 6)]
NMOD = 9
HD = 64
AH, CH = 8, 8
BW = 512
BT = BW // P
AB_TILES = 21
C_TILES = 24
RING = 4
W = P
SCALE = HD ** -0.5
DECAY = math.exp(-0.5)
SEGS = ((0, LAT, 0), (LAT, TOK, 1))

AB_COLUMN = [0, 1, 2, 3] + list(range(6, 21)) + [4, 5]
T_R, T_K, T_V, T_W, T_A, T_G, T_KA, T_VA = 4, 8, 12, 16, 17, 18, 19, 20

C_NORM, C_FINAL, C_MUP, C_MUN, C_W0, C_A0, C_KK, C_KA, C_RK = 0, 48, 56, 77, 98, 106, 114, 118, 122
C_GNW, C_GNB, C_SUB, C_COND, C_MODB = 128, 132, 136, 137, 153
C_END = 384


class Steps:

    def __init__(self, sem, names, offset=0):
        self.s, self.names, self.index, self.next = sem, names, {n: i for i, n in enumerate(names)}, 0
        self.offset = offset
        assert len(self.index) == len(names)

    def sem(self, name):
        assert self.names[self.next % len(self.names)] == name, (name, self.names[self.next % len(self.names)])
        self.next += 1
        return self.s

    def value(self, name, turn=0):
        return turn * len(self.names) + (self.offset + self.index[name] + 1)

    def before(self, turn):
        return turn * len(self.names) + self.offset


def tables():
    i = np.arange(P)
    eye = np.eye(P, dtype=np.float32)
    blk = (i[:, None] // HD == i[None, :] // HD).astype(np.float32)
    base = np.concatenate([eye, np.full((P, P), 1 / D, np.float32), np.full((P, P), 1 / P, np.float32), blk], 1)

    n_freq = HD // 4
    inv = np.power(np.float32(10000.0), -np.arange(n_freq, dtype=np.float32) / n_freq).astype(np.float32)
    t = np.arange(LAT)
    f = i % HD
    pos = np.where((f < HD // 2)[:, None], (t // 64)[None, :], (t % 64)[None, :]).astype(np.float32)
    ang = (pos * inv[f % n_freq][:, None]).astype(np.float32)
    second = (f % 32) >= n_freq
    rot = np.zeros((P, P), np.float32)
    for m in range(P):
        rot[m - n_freq if second[m] else m + n_freq, m] = 1.0 if second[m] else -1.0
    dup = [np.zeros((P, P), np.float32) for _ in range(2)]
    for g in range(2):
        dup[g][g * HD + i % HD, i] = 1.0
    rdup = [np.zeros((P, P), np.float32) for _ in range(2)]
    for g in range(2):
        rdup[g] = dup[g] @ rot
    q, k = i[:, None], i[None, :]
    low = np.float32(-1e30)
    none, prev, nxt = np.zeros((P, P)), np.where(k >= q, 0, low), np.where(k <= q, 0, low)
    band = np.concatenate([none, prev, none, nxt, none, none, nxt], 1).astype(np.float32)
    attn = np.concatenate([dup[0], dup[1], rdup[0], rdup[1], rot, np.cos(ang), np.sin(ang), band], 1)

    s, t2 = i[:, None], i[None, :]
    fwd = [(s < t2), (s <= t2)] * 2
    bwd = [(s > t2), (s >= t2)] * 2
    late, early = [], []
    for lev in range(7):
        b = 1 << lev
        blkc = np.repeat(np.arange(HD // b), b)[None, :]
        same = (s // (2 * b)) == blkc
        late.append(same & (s % (2 * b) >= b))
        early.append(same & (s % (2 * b) < b))
    reset = np.ones((P, TOK), np.float32)
    reset[:, ::P] = 0.0
    eye2 = np.concatenate([np.eye(HD), np.eye(HD)], 0)
    rwkv = np.concatenate([np.concatenate(x, 1).astype(np.float32) for x in (fwd, bwd, late, early)] + [reset, eye2], 1)
    return base.astype(np.float32), attn.astype(np.float32), rwkv.astype(np.float32)


BASE_W, ATTN_W, RWKV_W = 512, 2560, 2624


def build(nc, T):
    ctx = ExitStack()
    with ctx:
        def sb(name, shape, dt=F32):
            return ctx.enter_context(nc.sbuf_tensor(name, shape, dt))

        def sem(name):
            return ctx.enter_context(nc.semaphore(name))

        def sb_two(name, shape, first, second):
            at = (nc.sbuf_base + 31) // 32 * 32
            a = sb(name, shape, first)
            return a, nc.alloc_sbuf_tensor_at(name + "_as_" + ("f32r" if second == F32R else "f32"), shape, second, offset=at)

        x = sb("x", [P, DT, TOK])
        h_hi, h_hi_f = sb_two("h_hi", [P, DT, TOK], F32R, F32)
        h_lo, h_lo_f = sb_two("h_lo", [P, DT, TOK], F32R, F32)
        big, hidden = sb_two("big", [P, 24, TOK], F32, F32R)
        raw = sb("raw", [P, RING, DT, W])
        w_hi, w_hi_f = sb_two("w_hi", [P, RING, DT, W], F32R, F32)
        w_lo, w_lo_f = sb_two("w_lo", [P, RING, DT, W], F32R, F32)
        work = sb("work", [P, 6400])
        mod = sb("mod", [P, DEPTH * NMOD * DT, 2])
        cols = sb("cols", [P, C_END])
        base = sb("base", [P, BASE_W])
        attn = sb("attn", [P, ATTN_W])
        eps = sb("eps", [P, 16])
        small = sb("small", [P, 32])
        pp = [ctx.enter_context(nc.psum_tensor(f"pair{i}", [P, 2, 512], F32)) for i in range(4)]

        ident, mean_d, mean_p, blk = (base[:, i * P:(i + 1) * P] for i in range(4))
        dup = [attn[:, g * P:(g + 1) * P] for g in range(2)]
        rdup = [attn[:, (2 + g) * P:(3 + g) * P] for g in range(2)]
        rot = attn[:, 512:640]
        cos, sin = attn[:, 640:1152], attn[:, 1152:1664]
        band = attn[:, 1664:2560]
        g_hi = hidden[:, 0:8, :]
        g_lo = hidden[:, 8:16, :]
        mod_ring = work[:, 0:RING * DT * W].rearrange("p (s k w) -> p s k w", s=RING, k=DT)
        silu_t = work[:, 4096:4736].rearrange("p (a b) -> p a b", a=2)
        prod_t = work[:, 4736:5376].rearrange("p (a b) -> p a b", a=2)
        rt_t = work[:, 5376:6016]
        def col(i, n=1):
            return cols[:, i:i + n]

        def mod_at(l, c):
            return (l * NMOD + c) * DT

        def halves(ap):
            return ap.rearrange("p (a b) -> p a b", a=2)

        def f32(ap):
            return ap.bitcast(F32)

        raw_full = [sem(f"raw_full{i}") for i in range(RING)]
        hi_full = sem("hi_full")
        lo_full = sem("lo_full")
        slab_used = sem("slab_used")
        pair_free = sem("pair_free")
        silu_done = sem("silu_done")
        ghi_done = sem("ghi_done")
        g_ready = sem("g_ready")
        mraw_full = [sem(f"mraw_full{i}") for i in range(RING)]
        m_used = sem("m_used")
        m_taken = sem("m_taken")
        sec_full = [sem(f"sec_full{i}") for i in range(2)]
        sec_acc = sem("sec_acc")
        mod_fin = sem("mod_fin")
        s_load = sem("s_load")
        s_zero = sem("s_zero")
        s_tr = sem("s_tr")
        s_ev = sem("s_ev")
        s_cond = sem("s_cond")
        s_vec = sem("s_vec")
        s_out = sem("s_out")

        NORMS = 2 * 3 + 1
        NM = [sem(f"norm_{n}") for n in ("sq", "sum", "root", "recip", "scaled", "hi", "lo")]
        n_sq, n_sum, n_root, n_recip, n_scaled, n_hi, n_lo = NM

        stages = []
        for l in range(DEPTH):
            for f in range(2):
                if f == 1:
                    stages.append(("in", l, 0, 0, AB_TILES if l % 2 == 0 else C_TILES))
                    stages.append(("out", l, 0, 0, DT))
                for b, (_, cnt) in enumerate(BLOCKS):
                    stages.append(("up", l, f, b, 2 * cnt))
                    stages.append(("down", l, f, b, DT))
        start, n = {}, 0
        for st in stages:
            start[st[:4]] = n
            n += st[4]
        total = n
        upd, hid, u, hh = {}, {}, 0, 0
        for st in stages:
            upd[st[:4]], hid[st[:4]] = u, hh
            u += DT if st[0] in ("down", "out") else 0
            hh += st[4] // 2 if st[0] == "up" else 0
        norm_before = {}
        norm_no = {}
        k = 0
        for l in range(DEPTH):
            for s, key in enumerate([("up", l, 0, 0), ("in", l, 0, 0), ("up", l, 1, 0)]):
                norm_before[key] = k
                norm_no[k] = (l, s, upd[key])
                k += 1
        norm_no[k] = (DEPTH, 0, u)

        R = big[:, :, :].rearrange("p t n -> p (t n)")
        rows = [R[:, i * P:(i + 1) * P] for i in range(3)]
        x_rows = h_hi_f[:, :, :].rearrange("p t n -> p (t n)").rearrange("p (t n) -> p t n", t=5)
        norm_t = big[:, 16:24, :]
        praw = [work[:, 4096 + 644 * q:4096 + 644 * (q + 1)] for q in range(2)]
        c0 = small[:, 0:AB_TILES]
        kam = small[:, 24:28]
        ab_shift, ab_pad = sem("ab_shift"), sem("ab_pad")
        o_hi, o_lo = sem("o_hi"), sem("o_lo")
        y_tr, y_ev = sem("y_tr"), sem("y_ev")

        def halves2(ap, t):
            return ap[:, t, :].rearrange("p (a b) -> p a b", a=2)

        def LOOKAHEAD(i):
            return i + 1 < len(stages) and stages[i + 1][0] != "out"

        def FRESH(i):
            return i == 0 or stages[i][0] == "out"

        norm_at = {norm_before[q]: start[q] for q in norm_before}
        norm_at[NORMS - 1] = total

        FIRST = 3
        SECTIONS = {}
        for fi, (l, f) in enumerate(((0, 0), (0, 1), (1, 0))):
            for st, (kind, b) in enumerate((("up", 0), ("down", 0), ("up", 1), ("down", 1), ("up", 2))):
                SECTIONS[kind, l, f, b] = 5 * fi + st
        sec_ring = work[:, 0:2 * D].rearrange("p (s n) -> p s n", s=2)
        sec_sum = big[:, 16:24, :].rearrange("p t n -> p (t n)")[:, 0:4 * D].rearrange("p (a g n) -> p a g n", a=2, g=2)
        ones = eps[:, 15:16]

        def sum_steps(q, k, g=0):
            return 2 * k + (18 * q + g + 2)

        def sections_at(key, j):
            kind, l, f, b = key
            up = SECTIONS.get(("up", l, f, b))
            own = SECTIONS.get(key)
            return ([up] if j == min(b, 1) and up is not None else []) + ([own] if j == DT - 1 and own is not None else [])

        def loop_and_last(eng, turns, turn):
            if turns > 1:
                with eng.Fori(0, turns - 1) as i:
                    turn(i, False)
            turn(turns - 1, True)

        cols3 = cols[:, :].unsqueeze(2)
        kam3 = kam.unsqueeze(2)

        hh = h_hi_f[:, :, :].rearrange("p t n -> p (t n)")
        hl = h_lo_f[:, :, :].rearrange("p t n -> p (t n)")
        wh = w_hi_f[:, :, :, :].rearrange("p s k w -> p (s k w)")
        wl = w_lo_f[:, :, :, :].rearrange("p s k w -> p (s k w)")
        rw = raw[:, :, :, :].rearrange("p s k w -> p (s k w)")

        a_keys = hh[:, 0:1280].rearrange("p (g n) -> p g n", g=2)
        a_pkeys = hh[:, 1280:1536].rearrange("p (g n) -> p g n", g=2)
        a_vtok = hh[:, 1536:2176].rearrange("p (t n) -> p t n", n=P)
        a_vpast, a_kpast = hh[:, 2176:2304], hh[:, 2304:2432]
        a_kpast_t, a_kout = hh[:, 2432:2560], hh[:, 2560:2688]
        a_sink = hh[:, 2688:2696]
        a_q, a_qp = hh[:, 2700:3212], hh[:, 3212:3340]
        a_t1, a_t2 = hh[:, 3340:3852], hh[:, 3852:4364]
        a_max, a_neg, a_es, a_den, a_rden = (hh[:, 4400 + 8 * i:4405 + 8 * i] for i in range(5))
        a_sk = hh[:, 4440:4442]
        a_s = hl[:, 0:2560].rearrange("p (b n) -> p b n", b=5)
        a_e = hl[:, 2560:5120].rearrange("p (b n) -> p b n", b=5)
        a_pt = wh[:, 0:2048]
        WIN = [(max(0, b - 1), min(NB, b + 2)) for b in range(NB)]
        ENDS = [P + (k1 - k0) * P for k0, k1 in WIN]
        PIECES = [(b, i) for b in range(NB) for i in range(ENDS[b] // P)] + [(NB, 0)]

        a_load, a_pe, a_act, a_dve, a_out = (sem(f"a_{n}") for n in ("load", "pe", "act", "dve", "out"))
        APE0 = Steps(a_pe, ["past_t", "v_t", "dup", "dup2"])
        AAC0 = Steps(a_act, ["past_t", "v_t", "dup2"])
        ADV0 = Steps(a_dve, ["mul0", "keys0", "mul1", "keys1"])
        APE = Steps(a_pe, ["rot", "sc0", "tr0", "pv0", "sc1", "tr1", "pv1"], 4)
        AAC = Steps(a_act, ["qp", "exp0", "pt0", "o0", "exp1", "pt1", "o1"], 3)
        ADV = Steps(a_dve, ["rope1", "rope"] + [f"{n}{h}" for h in range(2) for n in ("s", "mx", "ng", "dn", "rd", "pn")], 4)
        IN_AB = start["in", 0, 0, 0]
        IN_C = start["in", 1, 0, 0]

        def sp_attn_ab(sp):
            sp.wait_ge(slab_used, IN_AB + AB_TILES + RING)
            sp.dma_start(a_vpast, T["cache_a_v"][0, 0].rearrange("t g d -> t (g d)")).then_inc(a_load, 16)
            sp.dma_start(a_kpast, T["cache_a_k"][0, 0].rearrange("t g d -> t (g d)")).then_inc(a_load, 16)
            sp.dma_start(a_sink, T["a_sink"].to_broadcast([P, AH])).then_inc(a_load, 16)
            sp.wait_ge(a_act, AAC0.value("v_t"))
            sp.dma_start(T["new_a_k"][0, 0].rearrange("t g d -> t (g d)"), a_kout).then_inc(a_out, 16)
            sp.dma_start(T["new_a_v"][0, 0].rearrange("t g d -> t (g d)"), a_vtok[:, 4, :]).then_inc(a_out, 16)

        def pe_attn_ab(pe):
            pe.wait_ge(a_load, 48)
            pe.wait_ge(ab_shift, 3 * AB_TILES)
            nc.tensor.transpose(pp[0][:, 0, 0:P], a_kpast, ident)
            nc.tensor.transpose(pp[0][:, 0, P:2 * P], big[:, T_KA, LAT:TOK], ident).then_inc(APE0.sem("past_t"), 1)
            for t in range(NCH):
                ins = nc.tensor.transpose(pp[1][:, t // 4, (t % 4) * P:(t % 4 + 1) * P], big[:, T_VA, t * P:(t + 1) * P], ident)
            ins.then_inc(APE0.sem("v_t"), 1)
            for g in range(2):
                nc.tensor.matmul(pp[2][:, g, :], dup[g], big[:, T_KA, 0:LAT], start=True, stop=True)
                ins = nc.tensor.matmul(pp[3][:, g, :], rdup[g], big[:, T_KA, 0:LAT], start=True, stop=True)
            ins.then_inc(APE0.sem("dup"), 1)
            pe.wait_ge(a_act, AAC0.value("past_t"))
            for g in range(2):
                nc.tensor.matmul(pp[0][:, g, 0:P], dup[g], a_kpast_t, start=True, stop=True)
                ins = nc.tensor.matmul(pp[0][:, g, P:2 * P], dup[g], big[:, T_KA, LAT:TOK], start=True, stop=True)
            ins.then_inc(APE0.sem("dup2"), 1)

            for g in range(2):
                with pe.Fori(0, 2) as jj:
                    it = jj + 2 * g
                    pe.wait_ge(a_act, AAC.before(it))
                    pe.wait_ge(a_dve, ADV.before(it))
                    nc.tensor.matmul(pp[3][:, 0, :], rot, big[:, it, 0:LAT], start=True, stop=True).then_inc(APE.sem("rot"), 1)
                    for h in range(2):
                        r = slice(h * HD, h * HD + HD)
                        if h == 0:
                            pe.wait_ge(a_dve, ADV.value("rope", it))
                            pe.wait_ge(a_act, AAC.value("qp", it))
                        else:
                            pe.wait_ge(a_act, AAC.value("pt0", it))
                        for b in range(NB):
                            ps = pp[b // 2][:, b % 2, :]
                            q = a_q[r, b * P:(b + 1) * P]
                            k0, k1 = WIN[b]
                            nc.tensor.matmul(ps[:, 0:P], q, a_keys[r, g, 0:P], start=True, stop=True)
                            nc.tensor.matmul(ps[:, P:ENDS[b]], q, a_keys[r, g, P + k0 * P:P + k1 * P], start=True, stop=True)
                        nc.tensor.matmul(pp[2][:, 0, 0:P], a_qp[r, :], a_pkeys[r, g, :], start=True, stop=True
                                         ).then_inc(APE.sem(f"sc{h}"), 1)
                        pe.wait_ge(a_dve, ADV.value(f"pn{h}", it))
                        for s, (b, i) in enumerate(PIECES):
                            ins = nc.tensor.transpose(pp[s // 8][:, s // 4 % 2, s % 4 * P:s % 4 * P + P],
                                                      a_e[:, b, i * P:(i + 1) * P], ident)
                        ins.then_inc(APE.sem(f"tr{h}"), 1)
                        pe.wait_ge(a_act, AAC.value(f"pt{h}", it))
                        for s, (b, i) in enumerate(PIECES):
                            last = s + 1 == len(PIECES) or PIECES[s + 1][0] != b
                            if b == NB:
                                v = a_vtok[:, NB, g * HD:(g + 1) * HD]
                            elif i == 0:
                                v = a_vpast[:, g * HD:(g + 1) * HD]
                            else:
                                v = a_vtok[:, WIN[b][0] + i - 1, g * HD:(g + 1) * HD]
                            out = pp[3][r, b // NB, (b % NB) * P:(b % NB + 1) * P]
                            ins = nc.tensor.matmul(out, v, a_pt[:, s * P:(s + 1) * P], start=(i == 0), stop=last)
                        ins.then_inc(APE.sem(f"pv{h}"), 1)

        def act_attn_ab(act):
            act.wait_ge(a_pe, APE0.value("past_t"))
            nc.scalar.activation(hh[:, 2432:2688], pp[0][:, 0, 0:2 * P], ACT.Copy).then_inc(AAC0.sem("past_t"), 1)
            act.wait_ge(a_pe, APE0.value("v_t"))
            nc.scalar.activation(hh[:, 1536:2048], pp[1][:, 0, :], ACT.Copy)
            nc.scalar.activation(hh[:, 2048:2176], pp[1][:, 1, 0:P], ACT.Copy).then_inc(AAC0.sem("v_t"), 1)
            act.wait_ge(a_pe, APE0.value("dup2"))
            nc.scalar.activation(a_keys[:, :, 0:P], pp[0][:, :, 0:P], ACT.Copy)
            nc.scalar.activation(a_pkeys, pp[0][:, :, P:2 * P], ACT.Copy).then_inc(AAC0.sem("dup2"), 1)
            nc.scalar.preload_act_table(ACT.Exp)
            with act.Fori(0, 4) as it:
                act.wait_ge(a_act, AAC.before(it))
                nc.scalar.activation(a_qp, big[:, it, LAT:TOK], ACT.Copy).then_inc(AAC.sem("qp"), 1)
                for h in range(2):
                    act.wait_ge(a_dve, ADV.value(f"ng{h}", it))
                    nc.scalar.activation(a_es, a_neg, ACT.Exp, bias=a_sk[:, h:h + 1])
                    for b in range(5):
                        n = ENDS[b] if b < NB else P
                        ins = nc.scalar.activation(a_e[:, b, 0:n], a_s[:, b, 0:n], ACT.Exp, bias=a_neg[:, b:b + 1],
                                                   accum_out=a_den[:, b:b + 1])
                    ins.then_inc(AAC.sem(f"exp{h}"), 1)
                    act.wait_ge(a_pe, APE.value(f"tr{h}", it))
                    nc.scalar.activation(halves(a_pt[:, 0:1024]), pp[0][:, :, :], ACT.Copy)
                    nc.scalar.activation(a_pt[:, 1024:1536], pp[1][:, 0, :], ACT.Copy)
                    nc.scalar.activation(a_pt[:, 1536:1920], pp[1][:, 1, 0:384], ACT.Copy).then_inc(AAC.sem(f"pt{h}"), 1)
                    act.wait_ge(a_pe, APE.value(f"pv{h}", it))
                    r = slice(h * HD, h * HD + HD)
                    nc.scalar.activation(big[r, it, 0:LAT], pp[3][r, 0, :], ACT.Copy)
                    nc.scalar.activation(big[r, it, LAT:TOK], pp[3][r, 1, 0:P], ACT.Copy).then_inc(AAC.sem(f"o{h}"), 1)

        def dve_attn_ab(dve):
            dve.wait_ge(a_pe, APE0.value("dup"))
            for g in range(2):
                if g:
                    dve.wait_ge(a_dve, ADV0.value("keys0"))
                nc.vector.tensor_tensor(a_t1, pp[2][:, g, :], cos, ALU.mult)
                nc.vector.tensor_tensor(a_t2, pp[3][:, g, :], sin, ALU.mult).then_inc(ADV0.sem(f"mul{g}"), 1)
                dve.wait_ge(a_dve, ADV0.value(f"mul{g}"))
                nc.vector.tensor_tensor(a_keys[:, g, P:TOK], a_t1, a_t2, ALU.add).then_inc(ADV0.sem(f"keys{g}"), 1)
            with dve.Fori(0, 4) as it:
                dve.wait_ge(a_pe, APE.value("rot", it))
                nc.vector.tensor_copy(a_sk, a_sink.rearrange("p (a b) -> p a b", b=2)[:, it, :])
                nc.vector.tensor_tensor(a_t1, big[:, it, 0:LAT], cos, ALU.mult)
                nc.vector.tensor_tensor(a_t2, pp[3][:, 0, :], sin, ALU.mult).then_inc(ADV.sem("rope1"), 1)
                dve.wait_ge(a_dve, ADV.value("rope1", it))
                nc.vector.tensor_tensor(a_q, a_t1, a_t2, ALU.add).then_inc(ADV.sem("rope"), 1)
                for h in range(2):
                    dve.wait_ge(a_pe, APE.value(f"sc{h}", it))
                    for b in range(NB):
                        m = band[:, 0:ENDS[b]] if b else band[:, 512:512 + ENDS[b]]
                        nc.vector.scalar_tensor_tensor(out=a_s[:, b, 0:ENDS[b]], in0=pp[b // 2][:, b % 2, 0:ENDS[b]], scalar=SCALE,
                                                       in1=m, op0=ALU.mult, op1=ALU.add)
                    nc.vector.tensor_scalar(a_s[:, NB, 0:P], pp[2][:, 0, 0:P], SCALE, None, ALU.mult
                                            ).then_inc(ADV.sem(f"s{h}"), 1)
                    dve.wait_ge(a_dve, ADV.value(f"s{h}", it))
                    for b in range(5):
                        ins = nc.vector.tensor_reduce(a_max[:, b:b + 1], a_s[:, b, 0:(ENDS[b] if b < NB else P)], AX.X, ALU.max)
                    ins.then_inc(ADV.sem(f"mx{h}"), 1)
                    dve.wait_ge(a_dve, ADV.value(f"mx{h}", it))
                    nc.vector.tensor_scalar(a_neg, a_max, a_sk[:, h:h + 1], -1.0, ALU.max, ALU.mult
                                            ).then_inc(ADV.sem(f"ng{h}"), 1)
                    dve.wait_ge(a_act, AAC.value(f"exp{h}", it))
                    nc.vector.tensor_tensor(a_den, a_den, a_es, ALU.add).then_inc(ADV.sem(f"dn{h}"), 1)
                    dve.wait_ge(a_dve, ADV.value(f"dn{h}", it))
                    nc.vector.reciprocal(a_rden, a_den).then_inc(ADV.sem(f"rd{h}"), 1)
                    dve.wait_ge(a_dve, ADV.value(f"rd{h}", it))
                    for b in range(5):
                        n = ENDS[b] if b < NB else P
                        ins = nc.vector.tensor_scalar(a_e[:, b, 0:n], a_e[:, b, 0:n], a_rden[:, b:b + 1], None, ALU.mult)
                    ins.then_inc(ADV.sem(f"pn{h}"), 1)

        r_ar = hh[:, 0:1280].rearrange("p (c two n) -> p c two n", c=NCH, two=2)
        r_beta, r_kappa, r_kkn, r_y = (hh[:, 1280 + 640 * i:1920 + 640 * i] for i in range(4))
        r_vtok = hh[:, 3840:4480].rearrange("p (c n) -> p c n", c=NCH)
        r_rhop = hh[:, 4480:4992]
        r_ktok = hl[:, 0:640].rearrange("p (c n) -> p c n", c=NCH)
        r_btok = hl[:, 640:1280].rearrange("p (c n) -> p c n", c=NCH)
        r_av = hl[:, 1280:2560].rearrange("p (u n) -> p u n", n=P)
        r_nwu = hl[:, 2560:3840].rearrange("p (u n) -> p u n", n=P)
        r_v, r_tb = hl[:, 3840:4480], hl[:, 4480:5120]
        r_sig, r_cum, r_a, r_kd, r_e1, r_e2 = (wh[:, 640 * i:640 * (i + 1)] for i in range(6))
        r_ft2, r_ft1 = wh[:, 3840:4096].rearrange("p (c n) -> p c n", n=P), hh[:, 4992:5120]
        r_ft = [r_ft2[:, 0, :], r_ft2[:, 1, :], r_ft1]
        r_p = wl[:, 0:640].rearrange("p (u n) -> p u n", n=HD)
        r_n = wl[:, 640:1280].rearrange("p (u n) -> p u n", n=HD)
        r_g = wl[:, 1280:1600].rearrange("p (c n) -> p c n", n=HD)
        r_z = wl[:, 1600:1920].rearrange("p (c n) -> p c n", n=HD)
        r_ht, r_d1, r_dd = (wl[:, 1920 + 8 * i:1925 + 8 * i] for i in range(3))
        r_w2, r_a2, r_g2 = (wl[:, 1952 + P * i:1952 + P * (i + 1)] for i in range(3))
        r_so = wl[0:HD, 2336:2592].rearrange("p (d n) -> p d n", d=2)
        r_kds, r_bonus = wl[:, 2592:3232], wl[:, 3232:3872]
        r_mask = [rw[:, 512 * i:512 * (i + 1)] for i in range(2)]
        r_late = rw[:, 1024:1472].rearrange("p (l n) -> p l n", n=HD)
        r_early = rw[:, 1472:1920].rearrange("p (l n) -> p l n", n=HD)
        r_reset, r_eye2 = rw[:, 1920:2560], rw[:, 2560:2624]
        r_s0t = rw[:, 2624:3136].rearrange("p (q n) -> p q n", n=HD)
        r_gate = rw[:, 3136:3776]
        r_s0 = work[0:HD, 0:1024].rearrange("p (q n) -> p q n", n=P)
        r_u4 = work[:, 0:5120].rearrange("p (u m n) -> p u m n", m=4, n=P)
        r_am = work[:, 5120:6400].rearrange("p (u n) -> p u n", n=P)
        r_t = R[:, 12160:13440].rearrange("p (u n) -> p u n", n=P)
        r_tt = R[:, 13440:14720].rearrange("p (u n) -> p u n", n=P)
        NU = 2 * NCH
        NL = 7

        def bank(i):
            return pp[i // 2][:, i % 2, :]

        def level_cols(ap, lev, half):
            return ap.rearrange("p u (k two b) -> p u k two b", two=2, b=1 << lev)[:, :, :, half, :]

        def sides(d):
            return (0, 1, r_late, r_early) if d == 0 else (1, 0, r_early, r_late)

        def lv_bank(k, g, n):
            u0, u1 = GROUPS[g]
            return bank(LBANK[k][g])[:, 0:(u1 - u0) * n].rearrange("p (u n) -> p u n", n=n)

        def chunks(d):
            return (0, 1, 2, 3) if d == 0 else (3, 2, 1, 0)

        b_load, b_lora, b_pe, b_act, b_dve, b_out = (sem(f"b_{n}") for n in ("load", "lora", "pe", "act", "dve", "out"))
        GROUPS = [(0, 4), (4, 7), (7, 10)]
        GS = range(len(GROUPS))
        LV = [("P", 1, g) for g in GS]
        for lev in range(1, NL - 1):
            LV += [("Q", lev, g) for g in GS]
            for g in GS:
                LV += [("X", lev, g)] + ([("P", lev + 1, g)] if lev < NL - 2 else [])
        LV += [(k, NL - 1, g) for k in "NR" for g in GS]
        LD = [({"P": "pn", "N": "pn", "Q": "t", "R": "t"}[k], lev, g) for k, lev, g in LV if k != "X"]
        LX = [("x", lev, g) for k, lev, g in LV if k == "X"]
        LBANK = {"P": (0, 1, 2), "N": (0, 1, 2), "Q": (3, 4, 5), "R": (3, 4, 5), "X": (6, 7, 6)}
        named = lambda steps, d: [f"{k}{lev}{g}_{d}" for k, lev, g in steps]
        BPE = Steps(b_pe, ["vT", "kkss"] + [f"{n}_{d}" for d in range(2) for n in
                    ["z", "tr"] + [f"pr{u}" for u in range(NU)] + ["A", "RV"]
                    + [f"{k}{lev}{g}" for k, lev, g in LV] + ["WU", "FG", "S0", "S1", "S2", "Y", "So"]] + ["bs", "gate", "mu", "var"], 1)
        BAC = Steps(b_act, ["vcopy", "kksq", "kkroot", "vtok", "sig_0", "ex_0", "tok_0", "rv_0"] + named(LX, 0) + ["wu_0", "y0", "so_0",
                            "sig_1", "ex_1", "tok_1", "rv_1"] + named(LX, 1) + ["wu_1", "so_1", "gt", "ysq", "sd"], 1)
        BDV = Steps(b_dve, ["kkmul", "kkmax", "kkrec", "kkn"] + [f"{n}_{d}" for d in range(2) for n in
                    ["cum", "ht", "q", "m", "kd1", "kd", "arr", "beta"] + [f"U{u}" for u in range(NU)] + ["Am", "id", "T0"]
                    + [f"{k}{lev}{g}" for k, lev, g in LD] + ["FG", "Z0", "Z1", "Z2"]] + ["y1", "bn", "bonus", "yc", "rs", "yn", "yg", "yb", "yo"], 1)

        def sp_rwkv(sp):
            sp.wait_ge(lo_full, IN_AB + AB_TILES + RING)
            sp.wait_ge(a_act, AAC.before(4))
            sp.dma_start(rw[:, 0:RWKV_W], T["t_rwkv"]).then_inc(b_load, 16)
            for d in range(2):
                sp.dma_start(r_s0[:, 4 * d:4 * d + 4, :].rearrange("p q (h n) -> p (q h) n", h=2),
                             T["state_b_wkv"][0, 0, d].rearrange("h i j -> i h j")).then_inc(b_load, 16)
            w2 = T["b_w2"][0].rearrange("d l (t w) -> (d l) t w", w=P)
            a2 = T["b_a2"][0].rearrange("d l (t w) -> (d l) t w", w=P)
            g2 = T["b_g2"][0].rearrange("l (t w) -> l t w", w=P)
            with sp.Fori(0, BT) as it:
                sp.wait_ge(b_pe, BPE.before(it))
                sp.wait_ge(b_out, 32 * it + 32)
                sp.dma_start(r_w2, w2[:, it, :]).then_inc(b_lora, 16)
                sp.dma_start(r_a2, a2[:, it, :]).then_inc(b_lora, 16)
                sp.dma_start(r_g2, g2[:, it, :]).then_inc(b_lora, 16)
                for d in range(2):
                    sp.wait_ge(b_act, BAC.value(f"so_{d}", it))
                    dst = T["new_b_wkv"][0, 0, d].rearrange("(t h) i j -> i t h j", h=2)[:, it, :, :]
                    sp.dma_start(dst, r_so[:, d, :].rearrange("p (h n) -> p h n", h=2)).then_inc(b_out, 16)
            sp.wait_ge(b_out, 32 * BT + 32)
            sp.wait_ge(b_dve, BDV.before(BT))

        def pe_rwkv(pe):
            pe.wait_ge(b_load, 48)
            pe.wait_ge(a_act, AAC.before(4))
            for q in range(2 * BT):
                ins = nc.tensor.transpose(bank(0)[:, q * HD:(q + 1) * HD], r_s0[:, q, :], ident[0:HD, 0:HD])
            ins.then_inc(b_pe, 1)
            heads = [slice(h * HD, h * HD + HD) for h in range(2)]
            with pe.Fori(0, BT) as it:
                def V(steps, name):
                    return steps.value(name, it)

                pe.wait_ge(b_act, V(BAC, "vcopy"))
                for c in range(NCH):
                    ins = nc.tensor.transpose(bank(c // 4)[:, c % 4 * P:c % 4 * P + P], r_v[:, c * P:(c + 1) * P], ident)
                ins.then_inc(BPE.sem("vT"), 1)
                pe.wait_ge(b_act, V(BAC, "kksq"))
                for c in range(2):
                    ins = nc.tensor.matmul(bank(2 + c)[:, 0:HALF], blk, r_tb[:, c * HALF:(c + 1) * HALF], start=True, stop=True)
                ins.then_inc(BPE.sem("kkss"), 1)
                for d in range(2):
                    dr = heads[d]
                    if d == 0:
                        pe.wait_ge(b_lora, 48 * it + 48)
                    for c in range(2):
                        nc.tensor.matmul(bank(4 + c)[:, 0:HALF], r_w2[dr, :], big[dr, T_W, c * HALF:(c + 1) * HALF],
                                         start=True, stop=True)
                        ins = nc.tensor.matmul(bank(6 + c)[:, 0:HALF], r_a2[dr, :], big[dr, T_A, c * HALF:(c + 1) * HALF],
                                               start=True, stop=True)
                    ins.then_inc(BPE.sem(f"z_{d}"), 1)
                    pe.wait_ge(b_dve, V(BDV, f"beta_{d}"))
                    for s in range(3 * NCH):
                        c = s % NCH
                        src = (r_ar[:, c, 0, :], r_beta[:, c * P:(c + 1) * P], r_kappa[:, c * P:(c + 1) * P])[s // NCH]
                        ins = nc.tensor.transpose(bank(s // 4)[:, s % 4 * P:s % 4 * P + P], src, ident)
                    ins.then_inc(BPE.sem(f"tr_{d}"), 1)
                    for u in range(NU):
                        c, r = u % NCH, heads[u // NCH]
                        if u >= 4:
                            pe.wait_ge(b_dve, V(BDV, f"U{u - 4}_{d}"))
                        ps = bank(4 + u % 4)
                        tk = slice(c * P, (c + 1) * P)
                        ar = r_ar[r, c, :, :]
                        nc.tensor.matmul(ps[:, 0:2 * P], r_beta[r, tk], ar, start=True, stop=True)
                        nc.tensor.matmul(ps[:, 2 * P:4 * P], r_kappa[r, tk], ar, start=True, stop=True
                                         ).then_inc(BPE.sem(f"pr{u}_{d}"), 1)
                    pe.wait_ge(b_act, V(BAC, f"tok_{d}"))
                    for u in range(NU):
                        c, r = u % NCH, heads[u // NCH]
                        ins = nc.tensor.matmul(bank(2 * (u // NCH) + c // 4)[:, c % 4 * P:c % 4 * P + P], r_ar[r, c, 0, :],
                                               r_beta[r, c * P:(c + 1) * P], start=True, stop=True)
                    ins.then_inc(BPE.sem(f"A_{d}"), 1)
                    pe.wait_ge(b_dve, V(BDV, f"U{NU - 1}_{d}"))
                    for u in range(NU):
                        c, r = u % NCH, heads[u // NCH]
                        ins = nc.tensor.matmul(bank(6 + u // 8)[:, u % 8 * HD:u % 8 * HD + HD], r_u4[:, u, 2, :],
                                               r_vtok[:, c, r], start=True, stop=True)
                    ins.then_inc(BPE.sem(f"RV_{d}"), 1)
                    hp, hn, _, _ = sides(d)
                    for k, lev, g in LV:
                        step = f"{k}{lev}{g}_{d}"
                        if k == "P":
                            pe.wait_ge(b_dve, V(BDV, f"T0_{d}" if lev == 1 else f"t{lev - 1}{g}_{d}"))
                        elif k == "X":
                            if lev == 1 and g == 0:
                                pe.wait_ge(b_act, V(BAC, f"rv_{d}"))
                            if g == 2:
                                pe.wait_ge(b_act, V(BAC, f"x{lev}0_{d}"))
                            pe.wait_ge(b_dve, V(BDV, f"t{lev}{g}_{d}"))
                        elif k == "N":
                            pe.wait_ge(b_act, V(BAC, f"x{lev - 1}{g}_{d}"))
                        else:
                            if k == "Q" and lev > 1:
                                pe.wait_ge(b_act, V(BAC, f"x{lev - 1}{g}_{d}"))
                            pe.wait_ge(b_dve, V(BDV, f"pn{lev}{g}_{d}"))
                        for u in range(*GROUPS[g]):
                            out = lv_bank(k, g, P if k in "PX" else HD)[:, u - GROUPS[g][0], :]
                            if k == "X":
                                ins = nc.tensor.transpose(out, r_t[:, u, :], ident)
                                continue
                            w, m = {"P": (r_u4[:, u, 0, :], r_t[:, u, :]), "Q": (r_tt[:, u, :], r_p[:, u, :]),
                                    "N": (r_am[:, u, :], level_cols(r_tt, lev, hn)[:, u]),
                                    "R": (r_t[:, u, :], r_n[:, u, :])}[k]
                            ins = nc.tensor.matmul(out, w, m, start=True, stop=True)
                        ins.then_inc(BPE.sem(step), 1)
                    pe.wait_ge(b_dve, V(BDV, f"t{NL - 1}2_{d}"))
                    for u in range(NU):
                        ins = nc.tensor.matmul(bank(u // 4)[:, u % 4 * P:u % 4 * P + P], r_tt[:, u, :], r_av[:, u, :],
                                               start=True, stop=True)
                    ins.then_inc(BPE.sem(f"WU_{d}"), 1)
                    pe.wait_ge(b_act, V(BAC, f"wu_{d}"))
                    order = chunks(d)
                    for h in range(2):
                        r = heads[h]
                        for i, c in enumerate(order[:3]):
                            nc.tensor.matmul(bank(3)[r, i * HD:(i + 1) * HD], r_nwu[:, NCH * h + c, 0:HD], r_btok[:, c, r],
                                             start=True, stop=True)
                        for c in range(NB):
                            nc.tensor.matmul(bank(5)[r, c * P:(c + 1) * P], r_nwu[:, NCH * h + c, 0:HD], r_u4[:, NCH * h + c, 1, :],
                                             start=True, stop=True)
                        for c in range(NCH):
                            nc.tensor.matmul(bank(4)[r, c * HD:(c + 1) * HD], r_ktok[:, c, r], r_vtok[:, c, r],
                                             start=True, stop=False)
                            ins = nc.tensor.matmul(bank(4)[r, c * HD:(c + 1) * HD], r_btok[:, c, r],
                                                   r_nwu[:, NCH * h + c, HD:P], start=False, stop=True)
                    ins.then_inc(BPE.sem(f"FG_{d}"), 1)
                    for i in range(3):
                        pe.wait_ge(b_dve, V(BDV, f"Z{i - 1}_{d}" if i else f"FG_{d}"))
                        nc.tensor.matmul(bank(7)[:, i * HD:(i + 1) * HD], r_ft[i], r_z[:, order[i], :], start=True, stop=True
                                         ).then_inc(BPE.sem(f"S{i}_{d}"), 1)
                    pe.wait_ge(b_dve, V(BDV, f"Z2_{d}"))
                    for h in range(2):
                        r = heads[h]
                        for c in range(NCH):
                            u = NCH * h + c
                            out = bank(c // 4)[r, c % 4 * P:c % 4 * P + P]
                            nc.tensor.matmul(out, r_vtok[:, c, r], r_u4[:, u, 3, :], start=True, stop=False)
                            ins = nc.tensor.matmul(out, r_nwu[:, u, HD:P], r_u4[:, u, 1, :], start=False, stop=(c == NB))
                            if c < NB:
                                ins = nc.tensor.matmul(out, r_z[r, c, :], r_rhop[r, c * P:(c + 1) * P], start=False, stop=True)
                    ins.then_inc(BPE.sem(f"Y_{d}"), 1)
                    nc.tensor.transpose(bank(2)[0:HD, 0:P], r_g[:, NB, :], ident).then_inc(BPE.sem(f"So_{d}"), 1)
                pe.wait_ge(b_dve, V(BDV, "bn"))
                pe.wait_ge(b_act, V(BAC, "so_1"))
                for c in range(2):
                    ins = nc.tensor.matmul(bank(2 + c)[:, 0:HALF], blk, r_e2[:, c * HALF:(c + 1) * HALF], start=True, stop=True)
                ins.then_inc(BPE.sem("bs"), 1)
                for c in range(2):
                    ins = nc.tensor.matmul(bank(4 + c)[:, 0:HALF], r_g2, big[:, T_G, c * HALF:(c + 1) * HALF], start=True, stop=True)
                ins.then_inc(BPE.sem("gate"), 1)
                for c in range(2):
                    ins = nc.tensor.matmul(bank(6 + c)[:, 0:HALF], blk, r_y[:, c * HALF:(c + 1) * HALF], start=True, stop=True)
                ins.then_inc(BPE.sem("mu"), 1)
                pe.wait_ge(b_act, V(BAC, "ysq"))
                for c in range(2):
                    ins = nc.tensor.matmul(bank(c)[:, 0:HALF], blk, r_sig[:, c * HALF:(c + 1) * HALF], start=True, stop=True)
                ins.then_inc(BPE.sem("var"), 1)

        def act_rwkv(act):
            act.wait_ge(ab_shift, 3 * AB_TILES)
            nc.scalar.activation(big[:, T_W, :], big[:, T_W, :], ACT.Tanh)
            nc.scalar.activation(big[:, T_G, :], big[:, T_G, :], ACT.Sigmoid)
            act.wait_ge(b_pe, 1)
            nc.scalar.activation(r_s0t, bank(0).rearrange("p (q n) -> p q n", n=HD), ACT.Copy).then_inc(b_act, 1)
            with act.Fori(0, BT) as it:
                def V(steps, name):
                    return steps.value(name, it)

                act.wait_ge(b_act, BAC.before(it))
                act.wait_ge(b_dve, BDV.value("kkmul", it))
                nc.scalar.activation(r_v, big[:, it + T_V, :], ACT.Copy).then_inc(BAC.sem("vcopy"), 1)
                nc.scalar.activation(r_tb, r_kkn, ACT.Square).then_inc(BAC.sem("kksq"), 1)
                act.wait_ge(b_pe, V(BPE, "kkss"))
                nc.scalar.activation(halves(r_e1), pp[1][:, :, 0:HALF], ACT.Sqrt).then_inc(BAC.sem("kkroot"), 1)
                nc.scalar.activation(r_vtok[:, 0:4, :], bank(0).rearrange("p (c n) -> p c n", n=P), ACT.Copy)
                nc.scalar.activation(r_vtok[:, 4, :], bank(1)[:, 0:P], ACT.Copy).then_inc(BAC.sem("vtok"), 1)
                for d in range(2):
                    act.wait_ge(b_pe, V(BPE, f"z_{d}"))
                    nc.scalar.activation(halves(r_sig), pp[2][:, :, 0:HALF], ACT.Sigmoid, bias=cols3[:, it + (C_W0 + BT * d), :])
                    nc.scalar.activation(halves(r_a), pp[3][:, :, 0:HALF], ACT.Sigmoid, bias=cols3[:, it + (C_A0 + BT * d), :]
                                         ).then_inc(BAC.sem(f"sig_{d}"), 1)
                    act.wait_ge(b_dve, V(BDV, f"m_{d}"))
                    q, m = (r_cum.rearrange("p (c n) -> p c n", n=P), r_sig.rearrange("p (c n) -> p c n", n=P))
                    e1 = r_e1.rearrange("p (c n) -> p c n", n=P)
                    for out, src, sg in (((r_ar[:, :, 0, :], m, -1), (r_ar[:, :, 1, :], q, -1), (e1, q, 1)) if d == 0 else
                                         ((r_ar[:, :, 0, :], q, 1), (r_ar[:, :, 1, :], m, 1), (e1, m, -1))):
                        nc.scalar.activation(out, src, ACT.Exp, scale=sg * DECAY)
                    nc.scalar.activation(r_d1, r_ht, ACT.Exp, scale=-DECAY).then_inc(BAC.sem(f"ex_{d}"), 1)
                    act.wait_ge(b_pe, V(BPE, f"tr_{d}"))
                    av = r_av.rearrange("p (h c) n -> p c h n", h=2)
                    c3 = lambda a, n: a.rearrange("p (c n) -> p c n", n=n)
                    nc.scalar.activation(av[:, 0:4, :, 0:HD], bank(0).rearrange("p (c h n) -> p c h n", h=2, n=HD), ACT.Copy)
                    nc.scalar.activation(av[:, 4, :, 0:HD], c3(bank(1)[:, 0:P], HD), ACT.Copy)
                    nc.scalar.activation(r_btok[:, 0:3, :], c3(bank(1)[:, P:512], P), ACT.Copy)
                    nc.scalar.activation(r_btok[:, 3:5, :], c3(bank(2)[:, 0:256], P), ACT.Copy)
                    nc.scalar.activation(r_ktok[:, 0:2, :], c3(bank(2)[:, 256:512], P), ACT.Copy)
                    nc.scalar.activation(r_ktok[:, 2:5, :], c3(bank(3)[:, 0:384], P), ACT.Copy).then_inc(BAC.sem(f"tok_{d}"), 1)
                    act.wait_ge(b_pe, V(BPE, f"RV_{d}"))
                    nc.scalar.activation(r_av[:, 0:8, HD:P], c3(bank(6), HD), ACT.Copy)
                    nc.scalar.activation(r_av[:, 8:10, HD:P], c3(bank(7)[:, 0:P], HD), ACT.Copy).then_inc(BAC.sem(f"rv_{d}"), 1)
                    for _, lev, g in LX:
                        act.wait_ge(b_pe, V(BPE, f"X{lev}{g}_{d}"))
                        nc.scalar.activation(r_tt[:, slice(*GROUPS[g]), :], lv_bank("X", g, P), ACT.Copy
                                             ).then_inc(BAC.sem(f"x{lev}{g}_{d}"), 1)
                    act.wait_ge(b_pe, V(BPE, f"WU_{d}"))
                    nc.scalar.activation(r_nwu[:, 0:4, :], c3(bank(0), P), ACT.Copy, scale=-1.0)
                    nc.scalar.activation(r_nwu[:, 4:8, :], c3(bank(1), P), ACT.Copy, scale=-1.0)
                    nc.scalar.activation(r_nwu[:, 8:10, :], c3(bank(2)[:, 0:256], P), ACT.Copy, scale=-1.0
                                         ).then_inc(BAC.sem(f"wu_{d}"), 1)
                    if d == 0:
                        act.wait_ge(b_pe, V(BPE, "Y_0"))
                        nc.scalar.activation(r_y[:, 0:LAT], bank(0), ACT.Copy)
                        nc.scalar.activation(r_y[:, LAT:TOK], bank(1)[:, 0:P], ACT.Copy).then_inc(BAC.sem("y0"), 1)
                    act.wait_ge(b_pe, V(BPE, f"So_{d}"))
                    nc.scalar.activation(r_so[:, d, :], bank(2)[0:HD, 0:P], ACT.Copy).then_inc(BAC.sem(f"so_{d}"), 1)
                act.wait_ge(b_pe, V(BPE, "gate"))
                nc.scalar.activation(halves(r_gate), pp[2][:, :, 0:HALF], ACT.Copy).then_inc(BAC.sem("gt"), 1)
                act.wait_ge(b_dve, V(BDV, "yc"))
                nc.scalar.activation(r_sig, r_cum, ACT.Square).then_inc(BAC.sem("ysq"), 1)
                act.wait_ge(b_pe, V(BPE, "var"))
                nc.scalar.activation(halves(r_e1), pp[0][:, :, 0:HALF], ACT.Sqrt, scale=1.0 / HD, bias=eps[:, 1:2]
                                     ).then_inc(BAC.sem("sd"), 1)

        def dve_rwkv(dve):
            dve.wait_ge(b_act, 1)
            dve.wait_ge(b_load, 48)
            dve.wait_ge(a_out, 32)
            v = nc.vector
            v.memset(r_ft2, 0.0)
            v.memset(r_ft1, 0.0).then_inc(b_dve, 1)
            dve.wait_ge(b_dve, 1)
            with dve.Fori(0, BT) as it:
                def V(steps, name):
                    return steps.value(name, it)


                def own(name):
                    dve.wait_ge(b_dve, V(BDV, name))

                dve.wait_ge(b_act, BAC.before(it))
                v.tensor_scalar(r_kkn, big[:, it + T_K, :], cols3[:, it + C_KK, :], None, ALU.mult).then_inc(BDV.sem("kkmul"), 1)
                dve.wait_ge(b_act, V(BAC, "kkroot"))
                v.tensor_scalar(r_e1, r_e1, 1e-12, None, ALU.max).then_inc(BDV.sem("kkmax"), 1)
                own("kkmax")
                v.reciprocal(r_e1, r_e1).then_inc(BDV.sem("kkrec"), 1)
                own("kkrec")
                v.tensor_tensor(r_kkn, r_kkn, r_e1, ALU.mult).then_inc(BDV.sem("kkn"), 1)
                for d in range(2):
                    n = lambda a, d=d: f"{a}_{d}"
                    dve.wait_ge(b_act, V(BAC, n("sig")))
                    v.tensor_tensor_scan(r_cum, r_reset, r_sig, 0.0, ALU.mult, ALU.add).then_inc(BDV.sem(n("cum")), 1)
                    own(n("cum"))
                    cum3 = r_cum.rearrange("p (c n) -> p c n", n=P)
                    v.tensor_scalar(r_ht, cum3[:, :, P - 1], 0.5, None, ALU.mult).then_inc(BDV.sem(n("ht")), 1)
                    own(n("ht"))
                    v.tensor_tensor(cum3, cum3, r_ht.unsqueeze(2).to_broadcast([P, NCH, P]), ALU.subtract
                                    ).then_inc(BDV.sem(n("q")), 1)
                    own(n("q"))
                    v.tensor_tensor(r_sig, r_cum, r_sig, ALU.subtract).then_inc(BDV.sem(n("m")), 1)
                    v.tensor_scalar(r_e2, r_a, cols3[:, it + C_KA, :], kam3[:, it, :], ALU.mult, ALU.add
                                    ).then_inc(BDV.sem(n("kd1")), 1)
                    own(n("kd1"))
                    kd = r_kd if d else r_kds
                    v.tensor_tensor(kd, r_e2, big[:, it + T_K, :], ALU.mult).then_inc(BDV.sem(n("kd")), 1)
                    own(n("kd"))
                    dve.wait_ge(b_act, V(BAC, n("ex")))
                    al, rh = r_ar[:, :, 0, :], r_ar[:, :, 1, :]
                    b3 = lambda a: a.rearrange("p (c n) -> p c n", n=P)
                    v.tensor_tensor(al, al, b3(r_kkn), ALU.mult)
                    v.tensor_tensor(rh, rh, b3(big[:, it + T_R, :]), ALU.mult)
                    v.tensor_tensor(r_kappa, kd, r_e1, ALU.mult)
                    if d:
                        v.tensor_tensor(r_kds, r_kds, kd, ALU.add)
                    lo, hi = (0, 1) if d == 0 else (1, 0)
                    v.tensor_tensor(r_dd[:, lo:lo + 3], r_d1[:, lo:lo + 3], r_d1[:, hi:hi + 3], ALU.mult)
                    v.tensor_copy(r_dd[:, NB:NCH], r_d1[:, NB:NCH])
                    v.tensor_copy(r_dd[:, 3 * (1 - d):3 * (1 - d) + 1], r_d1[:, 0:1])
                    v.tensor_tensor(r_a, r_kkn, r_a, ALU.mult).then_inc(BDV.sem(n("arr")), 1)
                    own(n("arr"))
                    v.tensor_tensor(r_beta, r_a, r_e1, ALU.mult).then_inc(BDV.sem(n("beta")), 1)
                    for u in range(NU):
                        dve.wait_ge(b_pe, V(BPE, n(f"pr{u}")))
                        v.tensor_tensor(r_u4[:, u, :, :].rearrange("p m n -> p (m n)"), bank(4 + u % 4), r_mask[d], ALU.mult
                                        ).then_inc(BDV.sem(n(f"U{u}")), 1)
                    dve.wait_ge(b_pe, V(BPE, n("A")))
                    ma = r_mask[1 - d][:, 0:P].unsqueeze(1)
                    for q, (a, b) in enumerate(((0, 4), (4, 5), (5, 9), (9, 10))):
                        ins = v.tensor_tensor(r_am[:, a:b, :], bank(q)[:, 0:(b - a) * P].rearrange("p (u n) -> p u n", n=P),
                                              ma.to_broadcast([P, b - a, P]), ALU.mult)
                    ins.then_inc(BDV.sem(n("Am")), 1)
                    v.tensor_copy(r_t, ident.unsqueeze(1).to_broadcast([P, NU, P]))
                    v.tensor_copy(r_tt, ident.unsqueeze(1).to_broadcast([P, NU, P]))
                    own(n("Am"))
                    hp, hn, mp, mn = sides(d)
                    wide = lambda m, lev, k: m[:, lev, :].unsqueeze(1).to_broadcast([P, k, HD])
                    at = r_u4[:, :, 0, :]
                    v.tensor_tensor(r_p, level_cols(r_am, 0, hp)[:, :, :, 0], wide(mp, 0, NU), ALU.mult)
                    v.tensor_tensor(r_n, at.rearrange("p u (k two) -> p u k two", two=2)[:, :, :, hn], wide(mn, 0, NU),
                                    ALU.mult).then_inc(BDV.sem(n("id")), 1)
                    own(n("id"))
                    tc, ttc = level_cols(r_t, 0, hp)[:, :, :, 0], level_cols(r_tt, 0, hn)[:, :, :, 0]
                    v.tensor_tensor(tc, tc, r_p, ALU.subtract)
                    v.tensor_tensor(ttc, ttc, r_n, ALU.subtract).then_inc(BDV.sem(n("T0")), 1)
                    for k, lev, g in LV:
                        if k == "X":
                            continue
                        us = slice(*GROUPS[g])
                        nu = us.stop - us.start
                        dve.wait_ge(b_pe, V(BPE, n(f"{k}{lev}{g}")))
                        if k == "P":
                            dst = r_p[:, us, :].rearrange("p u (k b) -> p u k b", b=1 << lev)
                            m = mp[:, lev, :].rearrange("p (k b) -> p k b", b=1 << lev).unsqueeze(1)
                            v.tensor_tensor(dst, level_cols(lv_bank(k, g, P), lev, hp), m.to_broadcast([P, nu, HD >> lev, 1 << lev]),
                                            ALU.mult).then_inc(BDV.sem(n(f"pn{lev}{g}")), 1)
                        elif k == "N":
                            v.tensor_tensor(r_n[:, us, :], lv_bank(k, g, HD), wide(mn, lev, nu), ALU.mult
                                            ).then_inc(BDV.sem(n(f"pn{lev}{g}")), 1)
                        else:
                            src = lv_bank(k, g, HD).rearrange("p u (k b) -> p u k b", b=1 << lev)
                            dst = level_cols(r_t[:, us, :], lev, hp) if k == "Q" else level_cols(r_tt[:, us, :], lev, hn)
                            v.tensor_tensor(dst, dst, src, ALU.subtract).then_inc(BDV.sem(n(f"t{lev}{g}")), 1)
                    dve.wait_ge(b_pe, V(BPE, n("FG")))
                    order = chunks(d)
                    for r in (slice(0, HD), slice(HD, P)):
                        v.tensor_tensor(r_ft2[r, :, r], bank(3)[r, 0:2 * HD].rearrange("p (c n) -> p c n", n=HD),
                                        r_eye2[r].unsqueeze(1).to_broadcast([HD, 2, HD]), ALU.add)
                        v.tensor_tensor(r_ft1[r, r], bank(3)[r, 2 * HD:3 * HD], r_eye2[r], ALU.add)
                    v.tensor_tensor(r_g, bank(4)[:, 0:NCH * HD].rearrange("p (c n) -> p c n", n=HD),
                                    r_dd.unsqueeze(2).to_broadcast([P, NCH, HD]), ALU.mult)
                    v.tensor_tensor(r_rhop.rearrange("p (c n) -> p c n", n=P), bank(5).rearrange("p (c n) -> p c n", n=P),
                                    r_ar[:, 0:NB, 1, :], ALU.add)
                    f = order[0]
                    v.tensor_scalar(r_z[:, f, :], r_s0t[:, it + BT * d, :], r_d1[:, f:f + 1], None, ALU.mult
                                    ).then_inc(BDV.sem(n("FG")), 1)
                    for i in range(3):
                        c, nx = order[i], order[i + 1]
                        dve.wait_ge(b_pe, V(BPE, n(f"S{i}")))
                        if i == 0:
                            own(n("FG"))
                        v.scalar_tensor_tensor(out=r_z[:, nx, :], in0=bank(7)[:, i * HD:(i + 1) * HD], scalar=r_dd[:, c:c + 1],
                                               in1=r_g[:, c, :], op0=ALU.mult, op1=ALU.add).then_inc(BDV.sem(n(f"Z{i}")), 1)
                dve.wait_ge(b_pe, V(BPE, "Y_1"))
                dve.wait_ge(b_act, V(BAC, "y0"))
                v.tensor_tensor(r_y[:, 0:LAT], r_y[:, 0:LAT], bank(0), ALU.add)
                v.tensor_tensor(r_y[:, LAT:TOK], r_y[:, LAT:TOK], bank(1)[:, 0:P], ALU.add).then_inc(BDV.sem("y1"), 1)
                v.scalar_tensor_tensor(out=r_e2, in0=big[:, it + T_R, :], scalar=cols3[:, it + C_RK, :], in1=r_kds,
                                       op0=ALU.mult, op1=ALU.mult).then_inc(BDV.sem("bn"), 1)
                dve.wait_ge(b_pe, V(BPE, "bs"))
                v.tensor_tensor(halves(r_bonus), pp[1][:, :, 0:HALF], halves(r_v), ALU.mult).then_inc(BDV.sem("bonus"), 1)
                dve.wait_ge(b_pe, V(BPE, "mu"))
                v.scalar_tensor_tensor(out=halves(r_cum), in0=pp[3][:, :, 0:HALF], scalar=-1.0 / HD, in1=halves(r_y),
                                       op0=ALU.mult, op1=ALU.add).then_inc(BDV.sem("yc"), 1)
                dve.wait_ge(b_act, V(BAC, "sd"))
                v.reciprocal(r_e1, r_e1).then_inc(BDV.sem("rs"), 1)
                own("rs")
                v.tensor_tensor(r_cum, r_cum, r_e1, ALU.mult).then_inc(BDV.sem("yn"), 1)
                own("yn")
                v.tensor_scalar(r_cum, r_cum, cols3[:, it + C_GNW, :], cols3[:, it + C_GNB, :], ALU.mult, ALU.add
                                ).then_inc(BDV.sem("yg"), 1)
                own("yg")
                v.tensor_tensor(r_cum, r_cum, r_bonus, ALU.add).then_inc(BDV.sem("yb"), 1)
                own("yb")
                v.tensor_tensor(big[:, it + T_R, :], r_cum, r_gate, ALU.mult).then_inc(BDV.sem("yo"), 1)

        LAM_INIT = 0.8 - 0.6 * math.exp(-0.3)
        c_keys, c_q, c_qp = hh[:, 0:640], hh[:, 640:1152], hh[:, 1152:1280]
        c_v = hh[:, 1280:1920]
        c_vtok = hh[:, 1920:2560].rearrange("p (c n) -> p c n", n=P)
        c_kout, c_vpast, c_kpast = hh[:, 2560:2688], hh[:, 2688:2816], hh[:, 2816:2944]
        c_t1 = hh[:, 2944:3968].rearrange("p (a n) -> p a n", a=2)
        c_t2 = hh[:, 3968:4992].rearrange("p (a n) -> p a n", a=2)
        NQ = NB + 1
        c_mxa, c_mxb, c_mx, c_neg, c_da, c_db, c_den, c_rd = (
            hh[:, 4992 + 2 * NQ * i:4992 + 2 * NQ * (i + 1)].rearrange("p (b m) -> p b m", m=2) for i in range(8))
        c_e = hl[:, 0:2560].rearrange("p (q m n) -> p q m n", q=2, m=2)
        c_a = hl[:, 2560:3840].rearrange("p (q n) -> p q n", q=2)
        c_t = hl[:, 3840:4480]
        c_at = wh[:, 0:2560].rearrange("p (i n) -> p i n", i=5)
        c_atp = wh[:, 2560:2688]
        c_o, c_sq = wh[:, 2688:3328], wh[:, 3328:3968]
        c_rs = wl[:, 0:640]
        c_lq = wl[:, 640:896].rearrange("p (a n) -> p a n", n=HD)
        c_lp = wl[:, 896:1024].rearrange("p (a n) -> p a n", n=HD)
        c_ls, c_le = wl[:, 1024:1026], wl[:, 1026:1028]
        c_kp = wl[:, 1032:1160]
        c_l1 = wl[:, 1160:1160 + NQ]
        nlam, csub = small[:, 28:29], small[:, 29:30]

        c_loadv = sem("c_loadv")
        c_load, c_lam, c_pe, c_act, c_dve, c_out = (sem(f"c_{n}") for n in ("load", "lam", "pe", "act", "dve", "out"))
        ORDER = [("s", 0), ("s", 1), ("t", 0), ("s", 2), ("t", 1), ("s", 3), ("t", 2), ("s", 4), ("t", 3), ("t", 4)]
        S_, T_ = (lambda *bs: [("s", b) for b in bs]), (lambda *bs: [("t", b) for b in bs])
        ORDER_DV = S_(0, 1) + T_(0, 1) + [x for b in (2, 3, 4) for x in S_(b) + T_(b)]
        ORDER_AC = S_(0, 1) + T_(0, 1) + [x for b in (2, 3, 4) for x in S_(b) + T_(b)]

        def c_steps(q, names, extra, own_end=()):
            after = [n for n in names if n[-1] == "+"][-1]
            credit = 0 if q is c_pe else len(names) - 1 - names.index(after)
            first = Steps(q, [n for n in names if n[-1] != "-"], extra + credit)
            main = Steps(q, names, first.before(1) - len(names))
            tail = Steps(q, [n for n in names if n[-1] != "+"] + list(own_end), main.before(CH - 1))
            return (first, main, tail), credit

        def c_names(order, s_names, t_names, at, ahead, behind=()):
            out = []
            for a, b in order:
                if (a, b) == at:
                    out += ahead
                out += [n + str(b) for n in (s_names if a == "s" else t_names)]
                if (a, b) == ("s", 0):
                    out += behind
            return out

        CPE, _ = c_steps(c_pe, c_names(ORDER, ["sc"], ["tr"], ("s", 4), ["rot+"]) + ["pv", "kt+", "vt+", "ms"], 3)
        CAC, act_credit = c_steps(c_act, c_names(ORDER_AC, ["ex"], ["at"], ("t", 4), ["cp+"]) + ["o", "sq", "kt+", "vt+", "rt"], 4)
        CDV, dve_credit = c_steps(c_dve, c_names(ORDER_DV, ["mx", "m2", "ng"], ["dn", "rd", "lm", "tm", "A"], ("s", 4),
                                                 ["r1+", "r2+"], ["rc-", "fin-"]), 6, ["rc", "fin"])

        def c_turns(eng, turn):
            def run(h, which):
                def S(steps, name):
                    return steps[which].sem(name)

                def V(steps, name):
                    return steps[which].value(name, h if which == 1 else 0)

                def B(steps, name=None):
                    m = steps[1]
                    back = len(m.names) - 1 - m.index[name] if name else 0
                    return m.before(h) - back if which == 1 else steps[which].offset - back

                turn(h, S, V, B, which == 0, which == 2)

            run(0, 0)
            with eng.Fori(1, CH - 1) as h:
                run(h, 1)
            run(CH - 1, 2)

        def c_main(b):
            return pp[2 * (b % 2)]

        def c_rest(b, m):
            return pp[2 * (b % 2) + 1][:, m, 0:P]

        def c_turn(b, i):
            return pp[2 * (b % 2) + 1][:, i // 3, (i % 3 + 1) * P:(i % 3 + 2) * P]

        def sp_attn_c(sp):
            sp.wait_ge(slab_used, IN_C + C_TILES + RING)
            for i, name in enumerate(("c_lq1", "c_lq2", "c_lk1", "c_lk2")):
                sp.dma_start(c_lq[:, i, :], T[name].to_broadcast([P, HD])).then_inc(c_lam, 16)
            kc = T["cache_c_k"][0, 0]
            vc = T["cache_c_v"][0, 0]
            sp.dma_start(c_kpast, kc[:, 0, :]).then_inc(c_load, 16)
            sp.dma_start(c_vpast, vc[:, 0, :]).then_inc(c_loadv, 16)

            def rows_out(h):
                sp.dma_start(T["new_c_k"][0, 0][:, h, :], c_kout).then_inc(c_out, 16)
                sp.dma_start(T["new_c_v"][0, 0][:, h, :], c_vtok[:, 4, :]).then_inc(c_out, 16)

            def turn(h, S, V, B, first, last):
                sp.wait_ge(c_act, B(CAC, "vt+"))
                rows_out(h)
                sp.wait_ge(c_out, 32 * h + 64)
                if not last:
                    sp.dma_start(c_kpast, kc[:, h + 1, :]).then_inc(c_load, 16)
                    sp.wait_ge(c_pe, V(CPE, "pv"))
                    sp.dma_start(c_vpast, vc[:, h + 1, :]).then_inc(c_loadv, 16)

            c_turns(sp, turn)

        def pe_attn_c(pe):
            pe.wait_ge(pair_free, IN_C + C_TILES + RING)

            def rotate(h, q):
                nc.tensor.matmul(pp[0][:, 0, :], rot, big[:, h, 0:LAT], start=True, stop=True)
                nc.tensor.matmul(pp[0][:, 1, :], rot, big[:, h + CH, 0:LAT], start=True, stop=True).then_inc(q, 1)

            def turn_keys(q):
                nc.tensor.transpose(pp[1][:, 0, 0:P], c_kpast, ident)
                nc.tensor.transpose(pp[1][:, 0, P:2 * P], c_kp, ident).then_inc(q, 1)

            def turn_values(q):
                for c in range(NCH):
                    ins = nc.tensor.transpose(pp[0][:, c // 4, c % 4 * P:c % 4 * P + P], c_v[:, c * P:(c + 1) * P], ident)
                ins.then_inc(q, 1)

            rotate(0, c_pe)
            pe.wait_ge(c_act, 2)
            pe.wait_ge(c_load, 16)
            turn_keys(c_pe)
            pe.wait_ge(c_dve, 6)
            turn_values(c_pe)

            def turn(h, S, V, B, first, last):
                for kind, b in ORDER:
                    if (kind, b) == ("s", 4) and not last:
                        rotate(h + 1, S(CPE, "rot+"))
                    if kind == "s":
                        if b == 0:
                            pe.wait_ge(c_dve, B(CDV, "r2+"))
                            pe.wait_ge(c_act, B(CAC, "vt+"))
                        elif b == 1:
                            pe.wait_ge(c_act, B(CAC))
                        else:
                            pe.wait_ge(c_act, V(CAC, f"at{b - 2}"))
                        for m in range(2):
                            r = slice(m * HD, m * HD + HD)
                            if b < NB:
                                q = c_q[r, b * P:(b + 1) * P]
                                nc.tensor.matmul(c_main(b)[:, m, :], q, c_keys[r, 0:512], start=True, stop=True)
                                ins = nc.tensor.matmul(c_rest(b, m), q, c_keys[r, 512:640], start=True, stop=True)
                            else:
                                ins = nc.tensor.matmul(c_rest(b, m), c_qp[r, :], c_kp[r, :],
                                                       start=True, stop=True)
                        ins.then_inc(S(CPE, f"sc{b}"), 1)
                    else:
                        pe.wait_ge(c_dve, V(CDV, f"A{b}"))
                        for i in range(5 if b < NB else 1):
                            ins = nc.tensor.transpose(c_turn(b, i), c_a[:, b % 2, i * P:(i + 1) * P], ident)
                        ins.then_inc(S(CPE, f"tr{b}"), 1)
                pe.wait_ge(c_act, V(CAC, "at4"))
                pe.wait_ge(c_loadv, 16 * h + 16)
                for i in range(5):
                    nc.tensor.matmul(pp[2][:, 0, :], c_vtok[:, i - 1, :] if i else c_vpast, c_at[:, i, :],
                                     start=(i == 0), stop=(i == 4))
                nc.tensor.matmul(pp[2][:, 1, 0:P], c_vtok[:, 4, :], c_atp, start=True, stop=True).then_inc(S(CPE, "pv"), 1)
                if not last:
                    pe.wait_ge(c_load, 16 * h + 32)
                    turn_keys(S(CPE, "kt+"))
                    pe.wait_ge(c_dve, V(CDV, "r2+"))
                    turn_values(S(CPE, "vt+"))
                pe.wait_ge(c_act, V(CAC, "sq"))
                for c in range(2):
                    ins = nc.tensor.matmul(pp[3][:, c, 0:HALF], mean_p, c_sq[:, c * HALF:(c + 1) * HALF], start=True, stop=True)
                ins.then_inc(S(CPE, "ms"), 1)

            c_turns(pe, turn)

        def act_attn_c(act):
            act.wait_ge(c_dve, 2)
            act.wait_ge(pair_free, IN_C + C_TILES + RING)
            nc.scalar.activation(c_le, c_ls, ACT.Exp).then_inc(c_act, 1)

            def copies(h, q):
                nc.scalar.activation(c_qp, big[:, h, LAT:TOK], ACT.Copy)
                nc.scalar.activation(c_kp, big[:, h + CH, LAT:TOK], ACT.Copy)
                nc.scalar.activation(c_v, big[:, h + 2 * CH, :], ACT.Copy).then_inc(q, 1)

            def keys(q):
                nc.scalar.activation(c_keys[:, 0:P], pp[1][:, 0, 0:P], ACT.Copy)
                nc.scalar.activation(c_kout, pp[1][:, 0, P:2 * P], ACT.Copy).then_inc(q, 1)

            def values(q):
                nc.scalar.activation(c_vtok[:, 0:4, :], pp[0][:, 0, :].rearrange("p (c n) -> p c n", n=P), ACT.Copy)
                nc.scalar.activation(c_vtok[:, 4, :], pp[0][:, 1, 0:P], ACT.Copy).then_inc(q, 1)

            copies(0, c_act)
            act.wait_ge(c_pe, 2)
            keys(c_act)
            act.wait_ge(c_pe, 3)
            values(c_act)
            nc.scalar.activation(c_le, c_ls, ACT.Exp).then_inc(c_act, act_credit)

            def turn(h, S, V, B, first, last):
                for kind, b in ORDER_AC:
                    if (kind, b) == ("t", 4) and not last:
                        act.wait_ge(c_pe, V(CPE, "sc4"))
                        copies(h + 1, S(CAC, "cp+"))
                    if kind == "s":
                        act.wait_ge(c_dve, V(CDV, f"ng{b}"))
                        for m in range(2):
                            bias = c_neg[:, b, m:m + 1]
                            if b < NB:
                                nc.scalar.activation(c_e[:, b % 2, m, 0:512], c_main(b)[:, m, :], ACT.Exp, bias=bias, scale=SCALE,
                                                     accum_out=c_da[:, b, m:m + 1])
                                ins = nc.scalar.activation(c_e[:, b % 2, m, 512:640], c_rest(b, m), ACT.Exp,
                                                           bias=bias, scale=SCALE, accum_out=c_db[:, b, m:m + 1])
                            else:
                                ins = nc.scalar.activation(c_e[:, b % 2, m, 0:P], c_rest(b, m), ACT.Exp,
                                                           bias=bias, scale=SCALE, accum_out=c_den[:, b, m:m + 1])
                        ins.then_inc(S(CAC, f"ex{b}"), 1)
                    else:
                        act.wait_ge(c_pe, V(CPE, f"tr{b}"))
                        if b < NB:
                            ps = pp[2 * (b % 2) + 1]
                            nc.scalar.activation(c_at[:, 0:3, b * P:(b + 1) * P], ps[:, 0, P:4 * P].rearrange(
                                "p (i n) -> p i n", n=P), ACT.Copy)
                            nc.scalar.activation(c_at[:, 3:5, b * P:(b + 1) * P], ps[:, 1, P:3 * P].rearrange(
                                "p (i n) -> p i n", n=P), ACT.Copy).then_inc(S(CAC, f"at{b}"), 1)
                        else:
                            nc.scalar.activation(c_atp, c_turn(b, 0), ACT.Copy).then_inc(S(CAC, "at4"), 1)
                act.wait_ge(c_pe, V(CPE, "pv"))
                if not first:
                    act.wait_ge(c_dve, V(CDV, "fin-"))
                nc.scalar.activation(c_o[:, 0:LAT], pp[2][:, 0, :], ACT.Copy)
                nc.scalar.activation(c_o[:, LAT:TOK], pp[2][:, 1, 0:P], ACT.Copy).then_inc(S(CAC, "o"), 1)
                act.wait_ge(c_act, V(CAC, "o"))
                nc.scalar.activation(c_sq, c_o, ACT.Square).then_inc(S(CAC, "sq"), 1)
                if not last:
                    act.wait_ge(c_pe, V(CPE, "kt+"))
                    keys(S(CAC, "kt+"))
                    act.wait_ge(c_pe, V(CPE, "vt+"))
                    values(S(CAC, "vt+"))
                act.wait_ge(c_pe, V(CPE, "ms"))
                nc.scalar.activation(halves(c_rs), pp[3][:, :, 0:HALF], ACT.Sqrt, bias=eps[:, 2:3]).then_inc(S(CAC, "rt"), 1)

            c_turns(act, turn)

        def dve_attn_c(dve):
            v = nc.vector
            dve.wait_ge(c_lam, 64)
            v.tensor_tensor(c_lp, c_lq[:, 0:2, :], c_lq[:, 2:4, :], ALU.mult).then_inc(c_dve, 1)
            dve.wait_ge(c_dve, 1)
            v.tensor_reduce(c_ls, c_lp, AX.X, ALU.add).then_inc(c_dve, 1)
            dve.wait_ge(c_act, 1)
            v.tensor_scalar(nlam, c_le[:, 1:2], -LAM_INIT, None, ALU.add)
            v.tensor_scalar(csub, col(C_SUB), 1.0 - LAM_INIT, None, ALU.mult).then_inc(c_dve, 1)
            dve.wait_ge(c_dve, 3)
            v.tensor_tensor(nlam, nlam, c_le[:, 0:1], ALU.subtract).then_inc(c_dve, 1)

            def products(h, waits, q):
                v.tensor_tensor(c_t1[:, 0, :], big[:, h, 0:LAT], cos, ALU.mult)
                v.tensor_tensor(c_t1[:, 1, :], big[:, h + CH, 0:LAT], cos, ALU.mult)
                dve.wait_ge(c_pe, waits)
                v.tensor_tensor(c_t2, pp[0][:, :, :], sin.unsqueeze(1).to_broadcast([P, 2, LAT]), ALU.mult).then_inc(q, 1)

            def rotated(q):
                v.tensor_tensor(c_q, c_t1[:, 0, :], c_t2[:, 0, :], ALU.add)
                v.tensor_tensor(c_keys[:, P:TOK], c_t1[:, 1, :], c_t2[:, 1, :], ALU.add).then_inc(q, 1)

            def finish(h, S, mark, own):
                v.reciprocal(c_rs, c_rs).then_inc(S(CDV, "rc" + mark), 1)
                own("rc" + mark)
                v.scalar_tensor_tensor(out=big[:, h, :], in0=c_o, scalar=csub, in1=c_rs, op0=ALU.mult, op1=ALU.mult
                                       ).then_inc(S(CDV, "fin" + mark), 1)

            products(0, 1, c_dve)
            dve.wait_ge(c_dve, 5)
            rotated(c_dve)
            v.memset(small[:, 30:31], 0.0).then_inc(c_dve, dve_credit)

            def turn(h, S, V, B, first, last):
                def own(name):
                    dve.wait_ge(c_dve, V(CDV, name))

                dve.wait_ge(c_dve, B(CDV))
                for kind, b in ORDER_DV:
                    if (kind, b) == ("s", 4) and not last:
                        products(h + 1, V(CPE, "rot+"), S(CDV, "r1+"))
                        own("r1+")
                        rotated(S(CDV, "r2+"))
                    if kind == "s":
                        dve.wait_ge(c_pe, V(CPE, f"sc{b}"))
                        if b < NB:
                            v.tensor_reduce(c_mxa[:, b, :], c_main(b)[:, :, :], AX.X, ALU.max)
                        v.tensor_reduce(c_mxb[:, b, :], pp[2 * (b % 2) + 1][:, :, 0:P], AX.X, ALU.max
                                        ).then_inc(S(CDV, f"mx{b}"), 1)
                        own(f"mx{b}")
                        v.tensor_tensor(c_mx[:, b, :], (c_mxa if b < NB else c_mxb)[:, b, :], c_mxb[:, b, :], ALU.max
                                        ).then_inc(S(CDV, f"m2{b}"), 1)
                        own(f"m2{b}")
                        v.tensor_scalar(c_neg[:, b, :], c_mx[:, b, :], -SCALE, None, ALU.mult).then_inc(S(CDV, f"ng{b}"), 1)
                        if b == 0 and not first:
                            dve.wait_ge(c_act, B(CAC))
                            finish(h - 1, S, "-", own)
                    else:
                        n = TOK if b < NB else P
                        dve.wait_ge(c_act, V(CAC, f"ex{b}"))
                        if b < NB:
                            v.tensor_tensor(c_den[:, b, :], c_da[:, b, :], c_db[:, b, :], ALU.add).then_inc(S(CDV, f"dn{b}"), 1)
                            own(f"dn{b}")
                        else:
                            v.tensor_copy(c_da[:, b, :], c_den[:, b, :]).then_inc(S(CDV, f"dn{b}"), 1)
                        v.reciprocal(c_rd[:, b, :], c_den[:, b, :]).then_inc(S(CDV, f"rd{b}"), 1)
                        own(f"rd{b}")
                        v.tensor_tensor(c_l1[:, b:b + 1], c_rd[:, b, 1:2], nlam, ALU.mult).then_inc(S(CDV, f"lm{b}"), 1)
                        own(f"lm{b}")
                        v.tensor_scalar(c_t[:, 0:n], c_e[:, b % 2, 1, 0:n], c_l1[:, b:b + 1], None, ALU.mult
                                        ).then_inc(S(CDV, f"tm{b}"), 1)
                        own(f"tm{b}")
                        v.scalar_tensor_tensor(out=c_a[:, b % 2, 0:n], in0=c_e[:, b % 2, 0, 0:n], scalar=c_rd[:, b, 0:1],
                                               in1=c_t[:, 0:n], op0=ALU.mult, op1=ALU.add).then_inc(S(CDV, f"A{b}"), 1)
                if last:
                    dve.wait_ge(c_act, V(CAC, "rt"))
                    finish(h, S, "", own)

            c_turns(dve, turn)

        MIXED = {0: [(b_dve, BDV.before(BT)), (a_act, AAC.before(4))], 1: [(c_dve, CDV[2].value("fin")), (c_out, 32 * CH + 32)]}

        loads = []
        loads.append((base[:, :], T["t_base"]))
        loads.append((x_rows[:, 0:4, :], T["x_sample"][0].rearrange("(t p) n -> p t n", p=P)))
        loads.append((x_rows[:, 4, :], T["x_prompt"][0]))
        r0, r1, r2 = rows
        v = lambda a: a.rearrange("(r c) -> r c", c=P)
        loads.append((r0[C_NORM:C_NORM + 48, :], T["norms"].rearrange("l s (r c) -> (l s r) c", c=P)))
        loads.append((r0[C_FINAL:C_FINAL + 8, :], v(T["final_norm"])))
        loads.append((r0[C_MUP + 4:C_MUP + 19, :], v(T["b_mu_prev"][0])))
        loads.append((r0[C_MUN + 4:C_MUN + 19, :], v(T["b_mu_next"][0])))
        loads.append((r0[C_W0:C_W0 + 8, :], T["b_w0"][0].rearrange("d (r c) -> (d r) c", c=P)))
        loads.append((r0[C_A0:C_A0 + 8, :], T["b_a0"][0].rearrange("d (r c) -> (d r) c", c=P)))
        loads.append((r0[C_KK:C_KK + 4, :], v(T["b_k_k"][0])))
        loads.append((r0[C_KA:C_KA + 4, :], v(T["b_k_a"][0])))
        loads.append((r0[C_RK:C_RK + 4, :], T["b_r_k"][0].rearrange("(r two) c -> r (two c)", two=2)))
        o = -P
        loads.append((r1[C_GNW + o:C_GNW + o + 4, :], v(T["b_gn_w"][0])))
        loads.append((r1[C_GNB + o:C_GNB + o + 4, :], v(T["b_gn_b"][0])))
        loads.append((r1[C_SUB + o:C_SUB + o + 1, :], T["c_subln"]))
        loads.append((r1[C_COND + o:C_COND + o + 8, :], v(T["c"][0])))
        loads.append((r1[C_COND + o + 8:C_COND + o + 16, :], v(T["c_ctx"])))
        mb = T["mod_b"].rearrange("l (r c) -> (l r) c", c=P)
        loads.append((r1[C_MODB + o:C_MODB + o + 16, :], mb[P:P + 16, :]))
        loads.append((r2, mb[0:P, :]))
        loads.append((attn[:, :], T["t_attn"]))
        LOADS = len(loads)

        block = ctx.enter_context(nc.Block())

        @block.sync
        def _(sp):
            def weights(key, cnt):
                kind, l, f, b = key
                n0 = start[key]

                def slab(i, j, src):
                    sp.wait_ge(lo_full, 4 * i + (j + 1))
                    sp.dma_start(raw[:, j % RING, :, :], src).then_inc(raw_full[j % RING], 16)

                def section_rows(q, k, slot, less=0):
                    l2, c = (q + FIRST) // NMOD, (q + FIRST) % NMOD
                    sp.wait_ge(sec_acc, 2 * k + (18 * q + 1 + less))
                    src = T["mod_w"][l2].rearrange("(k p) n -> p k n", p=P)[:, k, c * D:(c + 1) * D]
                    sp.dma_start(sec_ring[:, slot, :], src).then_inc(sec_full[slot], 16)

                if kind == "up":
                    q = SECTIONS.get(key)
                    w1 = T["ffn_w1"][l, f].rearrange("(k p) (t w) -> p k t w", p=P, w=W)
                    w3 = T["ffn_w3"][l, f].rearrange("(k p) (t w) -> p k t w", p=P, w=W)
                    t0 = BLOCKS[b][0]
                    with sp.Fori(0, cnt // 4) as i:
                        for j in range(4):
                            src = (w1 if j % 2 == 0 else w3)[:, :, 2 * i + (t0 + j // 2), :]
                            slab(i, n0 + j, src)
                            if q is not None and j % 2:
                                section_rows(q, 2 * i + j // 2, j // 2)
                    if q is not None:
                        for k in range(cnt // 2, DT):
                            section_rows(q, k, k % 2)
                elif kind == "down":
                    r0 = min(BLOCKS[b][0], FT - DT) * P
                    w2 = T["ffn_w2"][l, f][r0:r0 + D, :].rearrange("(k p) (t w) -> p k t w", p=P, w=W)
                    if key in SECTIONS:
                        q = SECTIONS[key]
                        for j in range(cnt + 2):
                            if j < cnt:
                                slab(0, n0 + j, w2[:, :, j, :])
                            if j >= 2:
                                section_rows(q, j - 2, j % 2, -2 if j < 4 else 0)
                    else:
                        with sp.Fori(0, cnt // 4) as i:
                            for j in range(4):
                                slab(i, n0 + j, w2[:, :, 4 * i + j, :])
                else:
                    src = {("in", 0): "w_in_ab", ("in", 1): "w_in_c", ("out", 0): "w_out_ab", ("out", 1): "w_out_c"}
                    v = T[src[kind, l % 2]][l // 2].rearrange("(k p) (t w) -> p k t w", p=P, w=W)
                    for j in range(cnt):
                        c = AB_COLUMN[j] if (kind, l % 2) == ("in", 0) else j
                        slab(0, n0 + j, v[:, :, c, :])

            sp.wait_ge(s_zero, 2)
            for dst, src in loads:
                sp.dma_start(dst, src).then_inc(s_load, 16)
            mw = T["mod_w"][0].rearrange("(k p) (t w) -> p k t w", p=P, w=W)
            with sp.Fori(0, FIRST * DT // 4) as i:
                for j in range(RING):
                    sp.wait_ge(m_used, 4 * i + (j + 1))
                    sp.dma_start(mod_ring[:, j, :, :], mw[:, :, 4 * i + j, :]).then_inc(mraw_full[j], 16)
            sp.wait_ge(m_used, FIRST * DT + RING)
            for i in range(len(stages)):
                kind, l = stages[i][:2]
                if kind == "out":
                    if l % 2 == 0:
                        sp_attn_ab(sp)
                        sp_rwkv(sp)
                    else:
                        sp_attn_c(sp)
                weights(stages[i][:4], stages[i][4])
            n_out = 0
            for t in range(NCH):
                sp.wait_ge(y_ev, t + 1)
                dst = T["y_sample"][0, t * P:(t + 1) * P, :] if t < NB else T["y_prompt"][0]
                sp.dma_start(dst, x_rows[:, t, :]).then_inc(s_out, 16)
            sp.wait_ge(s_out, 16 * NCH)
            sp.wait_ge(a_out, 32)
            sp.wait_ge(b_out, 32 * BT + 32)
            sp.wait_ge(c_out, 32 * CH + 32)
        @block.scalar
        def _(act):
            def split_hi(i, j):
                act.wait_ge(raw_full[j % RING], 16 * i + (16 * (j // RING) + 16))
                act.wait_ge(slab_used, 4 * i + (j + 1))
                nc.scalar.activation(w_hi[:, j % RING, :, :], raw[:, j % RING, :, :], ACT.Copy).then_inc(hi_full, 1)

            act.wait_ge(s_load, 16 * LOADS)
            for t in range(NCH):
                act.wait_ge(s_tr, t + 1)
                dst = x[:, :, t * P:(t + 1) * P].rearrange("p (a b) c -> p a b c", a=2)
                nc.scalar.activation(dst, pp[t % 4][:, :, :].rearrange("p a (b c) -> p a b c", c=P), ACT.Copy).then_inc(s_ev, 1)
            act.wait_ge(s_tr, NCH + 1)
            nc.scalar.activation(cols[:, :], pp[1][:, 0, 0:C_END], ACT.Copy).then_inc(s_ev, 1)
            act.wait_ge(s_ev, NCH + 1)
            nc.scalar.activation(col(C_COND, 16), col(C_COND, 16), ACT.Silu).then_inc(s_cond, 1)

            def norm(k):
                l, s, u = norm_no[k]
                for t in range(DT):
                    if k:
                        act.wait_ge(pair_free, norm_at[k] + RING - DT + t + 1)
                    nc.scalar.activation(norm_t[:, t, :], x[:, t, :], ACT.Square).then_inc(n_sq, 1)
                act.wait_ge(n_sum, k + 1)
                nc.scalar.activation(halves(rt_t), pp[norm_at[k] % 4][:, :, 0:HALF], ACT.Sqrt, bias=eps[:, 0:1]).then_inc(n_root, 1)
                if k == NORMS - 1:
                    return
                sh = mod_at(l, 3 * s)
                for t in range(DT):
                    act.wait_ge(n_scaled, DT * k + t + 1)
                    for a, b, g in SEGS:
                        ins = nc.scalar.activation(h_hi[:, t, a:b], norm_t[:, t, a:b], ACT.Identity,
                                                   bias=mod[:, sh + t, g:g + 1])
                    ins.then_inc(n_hi, 1)

            def stage(i):
                kind, l, f, b, cnt = stages[i]
                key = stages[i][:4]
                n0 = start[key]
                ahead = LOOKAHEAD(i)
                if key in norm_before:
                    norm(norm_before[key])
                if FRESH(i):
                    split_hi(0, n0)
                    split_hi(0, n0 + 1)
                if kind == "up":
                    h0 = hid[key]
                    nc.scalar.preload_act_table(ACT.Silu)

                    def turn(i, last):
                        for e in range(2):
                            if not (last and e == 1 and not ahead):
                                for j in (2 * e + 2, 2 * e + 3):
                                    split_hi(i, n0 + j)
                            act.wait_ge(slab_used, 4 * i + (n0 + 2 * e + 1 + RING))
                            act.wait_ge(pair_free, 4 * i + (n0 + 2 * e + RING))
                            nc.scalar.activation(silu_t, pp[(n0 + 2 * e) % 4][:, :, 0:HALF], ACT.Silu).then_inc(silu_done, 1)
                            act.wait_ge(pair_free, 4 * i + (n0 + 2 * e + 2 + RING))
                            nc.scalar.activation(halves2(g_hi, 2 * i + e), prod_t, ACT.Copy).then_inc(ghi_done, 1)

                    loop_and_last(act, cnt // 4, turn)
                elif kind in ("down", "out"):
                    for j in range(cnt):
                        if j + 2 < cnt or ahead:
                            split_hi(0, n0 + j + 2)
                elif l % 2 == 0:
                    for j in range(cnt):
                        if j + 2 < cnt or ahead:
                            split_hi(0, n0 + j + 2)
                        act.wait_ge(slab_used, n0 + j + 1 + RING)
                        if j >= 2:
                            act.wait_ge(ab_shift, 3 * (j - 1))
                        else:
                            act.wait_ge(ab_pad, 1)
                        ps = pp[(n0 + j) % 4]
                        dst = praw[j % 2]
                        nc.scalar.activation(dst[:, 1:321], ps[:, 0, 0:HALF], ACT.Copy)
                        nc.scalar.activation(dst[:, 321:513], ps[:, 1, 0:LAT - HALF], ACT.Copy)
                        nc.scalar.activation(dst[:, 515:643], ps[:, 1, LAT - HALF:HALF], ACT.Copy).then_inc(pair_free, 1)
                else:
                    for j in range(cnt):
                        if j + 2 < cnt or ahead:
                            split_hi(0, n0 + j + 2)
                        act.wait_ge(slab_used, n0 + j + 1 + RING)
                        nc.scalar.activation(halves(big[:, j, :]), pp[(n0 + j) % 4][:, :, 0:HALF], ACT.Copy).then_inc(pair_free, 1)

            def split_out(m):
                for t in range(DT):
                    for q, value in MIXED[m]:
                        act.wait_ge(q, value)
                    nc.scalar.activation(h_hi[:, t, :], big[:, t, :], ACT.Copy).then_inc(o_hi, 1)

            for i in range(len(stages)):
                if stages[i][0] == "out":
                    (act_attn_ab if stages[i][1] % 2 == 0 else act_attn_c)(act)
                    if stages[i][1] % 2 == 0:
                        act_rwkv(act)
                    split_out(stages[i][1])
                stage(i)
            norm(NORMS - 1)
            for t in range(NCH):
                act.wait_ge(y_tr, t + 1)
                nc.scalar.activation(x_rows[:, t, :].rearrange("p (a b) -> p a b", a=2), pp[t % 4][:, :, :],
                                     ACT.Copy).then_inc(y_ev, 1)

        @block.vector
        def _(dve):
            def split_lo(i, j):
                dve.wait_ge(hi_full, 4 * i + (j + 1))
                nc.vector.tensor_tensor(w_lo[:, j % RING, :, :], raw[:, j % RING, :, :], f32(w_hi[:, j % RING, :, :]),
                                        ALU.subtract).then_inc(lo_full, 1)

            nc.vector.memset(R[:, 0:3 * P], 0.0).then_inc(s_zero, 1)
            nc.vector.memset(eps[:, 0:1], 1e-6)
            nc.vector.memset(eps[:, 1:2], 64e-5)
            nc.vector.memset(eps[:, 2:3], 1e-5).then_inc(s_zero, 1)
            for i, (q, c) in enumerate(((lo_full, 4), (slab_used, 4), (pair_free, 4), (m_used, 4), (m_taken, 2), (g_ready, 1), (b_out, 32), (c_out, 32),
                                    (sec_acc, 1))):
                nc.vector.memset(eps[:, 3 + i:4 + i], 0.0).then_inc(q, c)
            nc.vector.memset(ones, 1.0)
            dve.wait_ge(s_ev, NCH + 1)
            c = [0, 0]

            def vec(ins):
                ins.then_inc(s_vec, 1)
                c[0] += 1

            def fin(ins):
                ins.then_inc(mod_fin, 1)
                c[1] += 1
                dve.wait_ge(mod_fin, c[1])

            def gain(l, s):
                sc = mod[:, mod_at(l, 3 * s + 1):mod_at(l, 3 * s + 1) + DT, :]
                g_in = col(C_NORM + (3 * l + s) * DT, DT).unsqueeze(2).to_broadcast([P, DT, 2])
                fin(nc.vector.tensor_tensor(sc, sc, g_in, ALU.mult))

            def halved(cc):
                return 0.5 if cc % 3 == 2 and cc // 3 != 1 else 1.0

            vec(nc.vector.tensor_copy(mod[:, 0:P, :], col(256, P).unsqueeze(2).to_broadcast([P, P, 2])))
            vec(nc.vector.tensor_copy(mod[:, P:P + 16, :], col(C_MODB, 16).unsqueeze(2).to_broadcast([P, 16, 2])))
            vec(nc.vector.tensor_tensor(c0, col(C_MUP, AB_TILES), col(C_MUN, AB_TILES), ALU.add))
            vec(nc.vector.tensor_scalar(kam, col(C_KA, 4), -1.0, 1.0, ALU.mult, ALU.add))
            dve.wait_ge(s_vec, c[0])
            vec(nc.vector.tensor_scalar(c0, c0, -1.0, 1.0, ALU.mult, ALU.add))
            for l in range(DEPTH):
                for cc in range(NMOD):
                    m = mod[:, mod_at(l, cc):mod_at(l, cc) + DT, :]
                    if cc % 3 == 1:
                        vec(nc.vector.tensor_scalar(m, m, 1.0, None, ALU.add))
                    elif halved(cc) != 1.0:
                        vec(nc.vector.tensor_scalar(m, m, halved(cc), None, ALU.mult))
            dve.wait_ge(s_vec, c[0])
            for g in range(FIRST * DT // 4):
                dve.wait_ge(m_used, 4 * g + 8)
                m = mod[:, 4 * g:4 * g + 4, :]
                nc.vector.scalar_tensor_tensor(out=m, in0=pp[2 + g % 2][:, 0, 0:8].rearrange("p (a b) -> p a b", b=2),
                                               scalar=halved(g // 2), in1=m, op0=ALU.mult, op1=ALU.add).then_inc(m_taken, 1)
            dve.wait_ge(m_taken, FIRST * DT // 4 + 2)
            gain(0, 0)

            def clear_sums(q):
                for g in range(2):
                    nc.vector.memset(sec_sum[:, q % 2, g, :], 0.0).then_inc(sec_acc, 1)

            def sum_rows(q, turn2, k, e):
                dve.wait_ge(sec_full[e], 16 * turn2 + (64 * q + 16))
                for g in range(2):
                    dve.wait_ge(sec_acc, sum_steps(q, k, g))
                    sm = sec_sum[:, q % 2, g, :]
                    nc.vector.scalar_tensor_tensor(out=sm, in0=sec_ring[:, e, :], scalar=cols3[:, k + (C_COND + DT * g), :],
                                                   in1=sm, op0=ALU.mult, op1=ALU.add).then_inc(sec_acc, 1)

            def take_section(q, ps):
                l2, cc = (q + FIRST) // NMOD, (q + FIRST) % NMOD
                m = mod[:, mod_at(l2, cc):mod_at(l2, cc) + DT, :]
                fin(nc.vector.scalar_tensor_tensor(out=m, in0=ps[:, 1, HALF:HALF + 2 * DT].rearrange("p (a b) -> p a b", b=2),
                                                   scalar=halved(cc), in1=m, op0=ALU.mult, op1=ALU.add))
                if cc % 3 == 1:
                    gain(l2, cc // 3)

            def norm(k):
                l, s, u = norm_no[k]
                dve.wait_ge(n_root, k + 1)
                nc.vector.reciprocal(rt_t, rt_t).then_inc(n_recip, 1)
                dve.wait_ge(n_recip, k + 1)
                last = k == NORMS - 1
                for t in range(DT):
                    for a, b, g in SEGS:
                        sc = col(C_FINAL + t) if last else mod[:, mod_at(l, 3 * s + 1) + t, g:g + 1]
                        ins = nc.vector.scalar_tensor_tensor(out=norm_t[:, t, a:b], in0=x[:, t, a:b], scalar=sc,
                                                             in1=rt_t[:, a:b], op0=ALU.mult, op1=ALU.mult)
                    ins.then_inc(n_scaled, 1)
                if last:
                    return
                sh = mod_at(l, 3 * s)
                for t in range(DT):
                    dve.wait_ge(n_hi, DT * k + t + 1)
                    for a, b, g in SEGS:
                        ins = nc.vector.scalar_tensor_tensor(out=h_lo[:, t, a:b], in0=norm_t[:, t, a:b],
                                                             scalar=mod[:, sh + t, g:g + 1], in1=f32(h_hi[:, t, a:b]),
                                                             op0=ALU.add, op1=ALU.subtract)
                    ins.then_inc(n_lo, 1)

            def stage(i):
                kind, l, f, b, cnt = stages[i]
                key = stages[i][:4]
                n0 = start[key]
                ahead = LOOKAHEAD(i)
                q = SECTIONS.get(key)
                if key in norm_before:
                    norm(norm_before[key])
                    if q is not None:
                        dve.wait_ge(n_lo, DT * norm_before[key] + DT)
                if FRESH(i):
                    split_lo(0, n0)
                    split_lo(0, n0 + 1)
                if q is not None:
                    clear_sums(q)
                if kind == "up":
                    h0 = hid[key]

                    def turn(i, last):
                        for e in range(2):
                            early = q is not None and last and e == 1 and cnt // 2 < DT
                            if early:
                                sum_rows(q, i, 2 * i + e, e)
                            if not (last and e == 1 and not ahead):
                                for j in (2 * e + 2, 2 * e + 3):
                                    split_lo(i, n0 + j)
                            dve.wait_ge(slab_used, 4 * i + (n0 + 2 * e + 2 + RING))
                            dve.wait_ge(silu_done, 2 * i + (h0 + e + 1))
                            dve.wait_ge(g_ready, 2 * i + (h0 + e + 1))
                            nc.vector.tensor_tensor(prod_t, silu_t, pp[(n0 + 2 * e + 1) % 4][:, :, 0:HALF],
                                                    ALU.mult).then_inc(pair_free, 2)
                            dve.wait_ge(ghi_done, 2 * i + (h0 + e + 1))
                            nc.vector.tensor_tensor(halves2(g_lo, 2 * i + e), prod_t, f32(halves2(g_hi, 2 * i + e)),
                                                    ALU.subtract).then_inc(g_ready, 1)
                            if q is not None and not early:
                                sum_rows(q, i, 2 * i + e, e)

                    loop_and_last(dve, cnt // 4, turn)
                    if q is not None:
                        for k in range(cnt // 2, DT):
                            sum_rows(q, k // 2, k, k % 2)
                elif kind in ("down", "out"):
                    gate = mod_at(l, 5 if kind == "out" else (2 if f == 0 else 8))
                    for j in range(cnt):
                        if j + 2 < cnt or ahead:
                            split_lo(0, n0 + j + 2)
                        if q is not None:
                            sum_rows(q, j // 2, j, j % 2)
                        dve.wait_ge(slab_used, n0 + j + 1 + RING)
                        if j == 0:
                            dve.wait_ge(pair_free, n0 + RING)
                        ps = pp[(n0 + j) % 4]
                        if kind == "down":
                            for q2 in sections_at(key, j):
                                take_section(q2, ps)
                        for (a, b2), src, g in (((0, HALF), ps[:, 0, 0:HALF], 0),
                                                ((HALF, LAT), ps[:, 1, 0:LAT - HALF], 0),
                                                ((LAT, TOK), ps[:, 1, LAT - HALF:HALF], 1)):
                            ins = nc.vector.scalar_tensor_tensor(out=x[:, j, a:b2], in0=src,
                                                                 scalar=mod[:, gate + j, g:g + 1], in1=x[:, j, a:b2],
                                                                 op0=ALU.mult, op1=ALU.add)
                        ins.then_inc(pair_free, 1)
                elif l % 2 == 0:
                    for q in range(2):
                        for z in (0, 513, 643):
                            w = 2 if z == 513 else 1
                            ins = nc.vector.memset(praw[q][:, z:z + w], 0.0)
                    ins.then_inc(ab_pad, 1)
                    for j in range(cnt):
                        if j + 2 < cnt or ahead:
                            split_lo(0, n0 + j + 2)
                        dve.wait_ge(pair_free, n0 + j + 1 + RING)
                        src = praw[j % 2]
                        for op in range(3):
                            if op:
                                dve.wait_ge(ab_shift, 3 * j + op)
                            for a, b2, o in ((0, LAT, 1), (LAT, TOK, 3)):
                                dst = big[:, j, a:b2]
                                if op == 0:
                                    ins = nc.vector.tensor_scalar(dst, src[:, a + o:b2 + o], c0[:, j:j + 1], None, ALU.mult)
                                else:
                                    d = -1 if op == 1 else 1
                                    mu = col((C_MUP if op == 1 else C_MUN) + j)
                                    ins = nc.vector.scalar_tensor_tensor(out=dst, in0=src[:, a + o + d:b2 + o + d], scalar=mu,
                                                                         in1=dst, op0=ALU.mult, op1=ALU.add)
                            ins.then_inc(ab_shift, 1)
                else:
                    for j in range(cnt):
                        if j + 2 < cnt or ahead:
                            split_lo(0, n0 + j + 2)

            def split_out(m):
                for t in range(DT):
                    dve.wait_ge(o_hi, DT * m + t + 1)
                    nc.vector.tensor_tensor(h_lo[:, t, :], big[:, t, :], f32(h_hi[:, t, :]), ALU.subtract).then_inc(o_lo, 1)

            for i in range(len(stages)):
                if stages[i][0] == "out":
                    (dve_attn_ab if stages[i][1] % 2 == 0 else dve_attn_c)(dve)
                    if stages[i][1] % 2 == 0:
                        dve_rwkv(dve)
                    split_out(stages[i][1])
                stage(i)
            norm(NORMS - 1)

        @block.tensor
        def _(pe):
            pe.wait_ge(s_load, 16 * LOADS)
            for t in range(NCH):
                if t == 4:
                    pe.wait_ge(s_ev, 1)
                for d in range(DT):
                    ins = nc.tensor.transpose(pp[t % 4][:, d // 4, (d % 4) * P:(d % 4 + 1) * P],
                                              x_rows[:, t, d * P:(d + 1) * P], ident)
                ins.then_inc(s_tr, 1)
            pe.wait_ge(s_ev, 2)
            for r in range(3):
                ins = nc.tensor.transpose(pp[1][:, 0, r * P:(r + 1) * P], rows[r], ident)
            ins.then_inc(s_tr, 1)
            pe.wait_ge(s_cond, 1)
            pe.wait_ge(s_ev, NCH + 1)
            cond = col(C_COND, 16).rearrange("p (g k) -> p k g", g=2)
            with pe.Fori(0, FIRST * DT // 8) as i:
                for j in range(8):
                    pe.wait_ge(mraw_full[j % RING], 32 * i + (16 * (j // RING) + 16))
                    if j % 4 == 0:
                        pe.wait_ge(m_taken, 2 * i + (j // 4 + 1))
                    for k in range(DT):
                        ins = nc.tensor.matmul(pp[2 + j // 4][:, 0, 2 * (j % 4):2 * (j % 4) + 2], mod_ring[:, j % RING, k, :],
                                               cond[:, k, :], start=(k == 0), stop=(k == DT - 1))
                    ins.then_inc(m_used, 1)

            def norm(k):
                pair = pp[norm_at[k] % 4]
                if k == 0:
                    pe.wait_ge(m_taken, FIRST * DT // 4 + 2)
                else:
                    pe.wait_ge(pair_free, norm_at[k] + 1)
                for t in range(DT):
                    pe.wait_ge(n_sq, DT * k + t + 1)
                    for c in range(2):
                        ins = nc.tensor.matmul(pair[:, c, 0:HALF], mean_d, norm_t[:, t, c * HALF:(c + 1) * HALF],
                                               start=(t == 0), stop=(t == DT - 1))
                ins.then_inc(n_sum, 1)

            def slab(i, j, kts, k0, xh, xl, wait_tile, sections=()):
                pe.wait_ge(lo_full, 4 * i + (j + 1 + RING))
                pe.wait_ge(pair_free, 4 * i + (j + 1))
                ps = pp[j % 4]
                for k in range(kts):
                    if wait_tile:
                        wait_tile(k)
                    hi, lo = w_hi[:, j % RING, k + k0, :], w_lo[:, j % RING, k + k0, :]
                    for w, v in ((hi, xh), (hi, xl), (lo, xh)):
                        for c in range(2):
                            ins = nc.tensor.matmul(ps[:, c, 0:HALF], w, v[:, k, c * HALF:(c + 1) * HALF],
                                                   start=(k == 0 and w is hi and v is xh),
                                                   stop=(k == kts - 1 and w is lo))
                for q in sections:
                    pe.wait_ge(sec_acc, sum_steps(q, DT) + 1)
                    for t in range(DT):
                        for g in range(2):
                            c = HALF + 2 * t + g
                            ins = nc.tensor.matmul(ps[:, 1, c:c + 1], sec_sum[:, q % 2, g, t * P:(t + 1) * P], ones,
                                                   start=True, stop=True)
                ins.then_inc(slab_used, 1)

            def stage(i):
                kind, l, f, b, cnt = stages[i]
                key = stages[i][:4]
                n0 = start[key]
                if key in norm_before:
                    norm(norm_before[key])
                k0, kts = 0, DT
                if kind == "down":
                    kts = BLOCKS[b][1]
                    k0 = BLOCKS[b][0] - min(BLOCKS[b][0], FT - DT)
                    xh, xl = g_hi, g_lo
                    tile_ready = lambda k: pe.wait_ge(g_ready, hid[key] - kts + k + 2)
                elif kind == "out":
                    xh, xl = h_hi, h_lo
                    tile_ready = lambda k: pe.wait_ge(o_lo, DT * l + k + 1)
                else:
                    xh, xl = h_hi, h_lo
                    kk = norm_before.get(key)
                    tile_ready = None if kk is None else (lambda k: pe.wait_ge(n_lo, DT * kk + k + 1))
                looped = 0
                if not (kind == "down" and ("up", l, f, b) in SECTIONS):
                    looped = cnt // 4 * 4
                    with pe.Fori(0, cnt // 4) as i2:
                        for j in range(4):
                            slab(i2, n0 + j, kts, k0, xh, xl, tile_ready if j == 0 else None)
                else:
                    for j in range(cnt):
                        slab(0, n0 + j, kts, k0, xh, xl, tile_ready if j == 0 else None, sections_at(key, j))
                    looped = cnt
                for j in range(looped, cnt):
                    slab(0, n0 + j, kts, k0, xh, xl, None)

            for i in range(len(stages)):
                if stages[i][0] == "out":
                    (pe_attn_ab if stages[i][1] % 2 == 0 else pe_attn_c)(pe)
                    if stages[i][1] % 2 == 0:
                        pe_rwkv(pe)
                stage(i)
            norm(NORMS - 1)
            for t in range(NCH):
                if t == 0:
                    pe.wait_ge(n_scaled, DT * NORMS)
                if t == 4:
                    pe.wait_ge(y_ev, 1)
                for d in range(DT):
                    ins = nc.tensor.transpose(pp[t % 4][:, d // 4, (d % 4) * P:(d % 4 + 1) * P],
                                              norm_t[:, d, t * P:(t + 1) * P], ident)
                ins.then_inc(y_tr, 1)


_INS = ["x_prompt", "x_sample", "c", "c_ctx", "cache_a_k", "cache_a_v", "state_b_wkv", "cache_c_k", "cache_c_v", "norms",
        "mod_w", "mod_b", "ffn_w1", "ffn_w3", "ffn_w2", "w_in_ab", "w_out_ab", "a_sink", "b_mu_prev", "b_mu_next", "b_w0",
        "b_w2", "b_a0", "b_a2", "b_k_k", "b_k_a", "b_r_k", "b_g2", "b_gn_w", "b_gn_b", "w_in_c", "w_out_c", "c_lq1",
        "c_lk1", "c_lq2", "c_lk2", "c_subln", "final_norm"]
_OUTS = [("y_prompt", (1, CTX, D)), ("y_sample", (1, LAT, D)), ("new_a_k", (1, 1, CTX, 2, HD)),
         ("new_a_v", (1, 1, CTX, 2, HD)), ("new_b_wkv", (1, 1, 2, 8, HD, HD)), ("new_c_k", (1, 1, CTX, CH, P)),
         ("new_c_v", (1, 1, CTX, CH, P))]


def kernel(**inputs):
    import concourse.bacc as _bacc
    from concourse.bass_utils import run_bass_kernel_spmd as _run

    nc = _bacc.Bacc("TRN2", target_bir_lowering=False, num_devices=1)
    arrays, T = {}, {}
    for name in _INS:
        arrays[name] = np.ascontiguousarray(inputs[name])
    for name, a in zip(("t_base", "t_attn", "t_rwkv"), tables()):
        arrays[name] = np.ascontiguousarray(a)
    for name, a in arrays.items():
        T[name] = nc.dram_tensor(name, a.shape, mybir.dt.from_np(a.dtype), kind="ExternalInput").ap()
    for name, shape in _OUTS:
        T[name] = nc.dram_tensor(name, shape, F32, kind="ExternalOutput").ap()
    build(nc, T)
    r = _run(nc, [arrays], core_ids=[0])
    return tuple(r.results[0][name] for name, _ in _OUTS)
```

```python
from contextlib import ExitStack
import math

import numpy as np

import concourse.bass as bass
from concourse import mybir

F32 = mybir.dt.float32
F32R = mybir.dt.float32r
ALU = mybir.AluOpType
ACT = mybir.ActivationFunctionType
AX = mybir.AxisListType

P = 128
D = 1024
DT = D // P
LAT, CTX = 512, 128
TOK = LAT + CTX
HALF = TOK // 2
NB = LAT // P
NCH = TOK // P
DEPTH = 2
FF = 2816
FT = FF // P
BLOCKS = [(0, 8), (8, 8), (16, 6)]
NMOD = 9
HD = 64
AH, CH = 8, 8
BW = 512
BT = BW // P
AB_TILES = 21
C_TILES = 24
RING = 4
W = P
SCALE = HD ** -0.5
DECAY = math.exp(-0.5)
SEGS = ((0, LAT, 0), (LAT, TOK, 1))

AB_COLUMN = [0, 1, 2, 3] + list(range(6, 21)) + [4, 5]
T_R, T_K, T_V, T_W, T_A, T_G, T_KA, T_VA = 4, 8, 12, 16, 17, 18, 19, 20

C_NORM, C_FINAL, C_MUP, C_MUN, C_W0, C_A0, C_KK, C_KA, C_RK = 0, 48, 56, 77, 98, 106, 114, 118, 122
C_GNW, C_GNB, C_SUB, C_COND, C_MODB = 128, 132, 136, 137, 153
C_END = 384


class Steps:

    def __init__(self, sem, names, offset=0):
        self.s, self.names, self.index, self.next = sem, names, {n: i for i, n in enumerate(names)}, 0
        self.offset = offset
        assert len(self.index) == len(names)

    def sem(self, name):
        assert self.names[self.next % len(self.names)] == name, (name, self.names[self.next % len(self.names)])
        self.next += 1
        return self.s

    def value(self, name, turn=0):
        return turn * len(self.names) + (self.offset + self.index[name] + 1)

    def before(self, turn):
        return turn * len(self.names) + self.offset


def tables():
    i = np.arange(P)
    eye = np.eye(P, dtype=np.float32)
    blk = (i[:, None] // HD == i[None, :] // HD).astype(np.float32)
    base = np.concatenate([eye, np.full((P, P), 1 / D, np.float32), np.full((P, P), 1 / P, np.float32), blk], 1)

    n_freq = HD // 4
    inv = np.power(np.float32(10000.0), -np.arange(n_freq, dtype=np.float32) / n_freq).astype(np.float32)
    t = np.arange(LAT)
    f = i % HD
    pos = np.where((f < HD // 2)[:, None], (t // 64)[None, :], (t % 64)[None, :]).astype(np.float32)
    ang = (pos * inv[f % n_freq][:, None]).astype(np.float32)
    second = (f % 32) >= n_freq
    rot = np.zeros((P, P), np.float32)
    for m in range(P):
        rot[m - n_freq if second[m] else m + n_freq, m] = 1.0 if second[m] else -1.0
    dup = [np.zeros((P, P), np.float32) for _ in range(2)]
    for g in range(2):
        dup[g][g * HD + i % HD, i] = 1.0
    rdup = [np.zeros((P, P), np.float32) for _ in range(2)]
    for g in range(2):
        rdup[g] = dup[g] @ rot
    q, k = i[:, None], i[None, :]
    low = np.float32(-1e30)
    none, prev, nxt = np.zeros((P, P)), np.where(k >= q, 0, low), np.where(k <= q, 0, low)
    band = np.concatenate([none, prev, none, nxt, none, none, nxt], 1).astype(np.float32)
    attn = np.concatenate([dup[0], dup[1], rdup[0], rdup[1], rot, np.cos(ang), np.sin(ang), band], 1)

    s, t2 = i[:, None], i[None, :]
    fwd = [(s < t2), (s <= t2)] * 2
    bwd = [(s > t2), (s >= t2)] * 2
    late, early = [], []
    for lev in range(7):
        b = 1 << lev
        blkc = np.repeat(np.arange(HD // b), b)[None, :]
        same = (s // (2 * b)) == blkc
        late.append(same & (s % (2 * b) >= b))
        early.append(same & (s % (2 * b) < b))
    reset = np.ones((P, TOK), np.float32)
    reset[:, ::P] = 0.0
    eye2 = np.concatenate([np.eye(HD), np.eye(HD)], 0)
    rwkv = np.concatenate([np.concatenate(x, 1).astype(np.float32) for x in (fwd, bwd, late, early)] + [reset, eye2], 1)
    return base.astype(np.float32), attn.astype(np.float32), rwkv.astype(np.float32)


BASE_W, ATTN_W, RWKV_W = 512, 2560, 2624


def build(nc, T):
    ctx = ExitStack()
    with ctx:
        def sb(name, shape, dt=F32):
            return ctx.enter_context(nc.sbuf_tensor(name, shape, dt))

        def sem(name):
            return ctx.enter_context(nc.semaphore(name))

        def sb_two(name, shape, first, second):
            at = (nc.sbuf_base + 31) // 32 * 32
            a = sb(name, shape, first)
            return a, nc.alloc_sbuf_tensor_at(name + "_as_" + ("f32r" if second == F32R else "f32"), shape, second, offset=at)

        x = sb("x", [P, DT, TOK])
        h_hi, h_hi_f = sb_two("h_hi", [P, DT, TOK], F32R, F32)
        h_lo, h_lo_f = sb_two("h_lo", [P, DT, TOK], F32R, F32)
        big, hidden = sb_two("big", [P, 24, TOK], F32, F32R)
        raw = sb("raw", [P, RING, DT, W])
        w_hi, w_hi_f = sb_two("w_hi", [P, RING, DT, W], F32R, F32)
        w_lo, w_lo_f = sb_two("w_lo", [P, RING, DT, W], F32R, F32)
        work = sb("work", [P, 6400])
        mod = sb("mod", [P, DEPTH * NMOD * DT, 2])
        cols = sb("cols", [P, C_END])
        base = sb("base", [P, BASE_W])
        attn = sb("attn", [P, ATTN_W])
        eps = sb("eps", [P, 16])
        small = sb("small", [P, 32])
        pp = [ctx.enter_context(nc.psum_tensor(f"pair{i}", [P, 2, 512], F32)) for i in range(4)]

        ident, mean_d, mean_p, blk = (base[:, i * P:(i + 1) * P] for i in range(4))
        dup = [attn[:, g * P:(g + 1) * P] for g in range(2)]
        rdup = [attn[:, (2 + g) * P:(3 + g) * P] for g in range(2)]
        rot = attn[:, 512:640]
        cos, sin = attn[:, 640:1152], attn[:, 1152:1664]
        band = attn[:, 1664:2560]
        g_hi = hidden[:, 0:8, :]
        g_lo = hidden[:, 8:16, :]
        mod_ring = work[:, 0:RING * DT * W].rearrange("p (s k w) -> p s k w", s=RING, k=DT)
        silu_t = work[:, 4096:4736].rearrange("p (a b) -> p a b", a=2)
        prod_t = work[:, 4736:5376].rearrange("p (a b) -> p a b", a=2)
        rt_t = work[:, 5376:6016]
        def col(i, n=1):
            return cols[:, i:i + n]

        def mod_at(l, c):
            return (l * NMOD + c) * DT

        def halves(ap):
            return ap.rearrange("p (a b) -> p a b", a=2)

        def f32(ap):
            return ap.bitcast(F32)

        raw_full = [sem(f"raw_full{i}") for i in range(RING)]
        hi_full = sem("hi_full")
        lo_full = sem("lo_full")
        slab_used = sem("slab_used")
        pair_free = sem("pair_free")
        silu_done = sem("silu_done")
        ghi_done = sem("ghi_done")
        g_ready = sem("g_ready")
        mraw_full = [sem(f"mraw_full{i}") for i in range(RING)]
        m_used = sem("m_used")
        m_taken = sem("m_taken")
        sec_full = [sem(f"sec_full{i}") for i in range(2)]
        sec_acc = sem("sec_acc")
        mod_fin = sem("mod_fin")
        s_load = sem("s_load")
        s_zero = sem("s_zero")
        s_tr = sem("s_tr")
        s_ev = sem("s_ev")
        s_cond = sem("s_cond")
        s_vec = sem("s_vec")
        s_out = sem("s_out")

        NORMS = 2 * 3 + 1
        NM = [sem(f"norm_{n}") for n in ("sq", "sum", "root", "recip", "scaled", "hi", "lo")]
        n_sq, n_sum, n_root, n_recip, n_scaled, n_hi, n_lo = NM

        stages = []
        for l in range(DEPTH):
            for f in range(2):
                if f == 1:
                    stages.append(("in", l, 0, 0, AB_TILES if l % 2 == 0 else C_TILES))
                    stages.append(("out", l, 0, 0, DT))
                for b, (_, cnt) in enumerate(BLOCKS):
                    stages.append(("up", l, f, b, 2 * cnt))
                    stages.append(("down", l, f, b, DT))
        start, n = {}, 0
        for st in stages:
            start[st[:4]] = n
            n += st[4]
        total = n
        upd, hid, u, hh = {}, {}, 0, 0
        for st in stages:
            upd[st[:4]], hid[st[:4]] = u, hh
            u += DT if st[0] in ("down", "out") else 0
            hh += st[4] // 2 if st[0] == "up" else 0
        norm_before = {}
        norm_no = {}
        k = 0
        for l in range(DEPTH):
            for s, key in enumerate([("up", l, 0, 0), ("in", l, 0, 0), ("up", l, 1, 0)]):
                norm_before[key] = k
                norm_no[k] = (l, s, upd[key])
                k += 1
        norm_no[k] = (DEPTH, 0, u)

        R = big[:, :, :].rearrange("p t n -> p (t n)")
        rows = [R[:, i * P:(i + 1) * P] for i in range(3)]
        x_rows = h_hi_f[:, :, :].rearrange("p t n -> p (t n)").rearrange("p (t n) -> p t n", t=5)
        norm_t = big[:, 16:24, :]
        praw = [work[:, 4096 + 644 * q:4096 + 644 * (q + 1)] for q in range(2)]
        c0 = small[:, 0:AB_TILES]
        kam = small[:, 24:28]
        ab_shift, ab_pad = sem("ab_shift"), sem("ab_pad")
        o_hi, o_lo = sem("o_hi"), sem("o_lo")
        y_tr, y_ev = sem("y_tr"), sem("y_ev")

        def halves2(ap, t):
            return ap[:, t, :].rearrange("p (a b) -> p a b", a=2)

        def LOOKAHEAD(i):
            return i + 1 < len(stages) and stages[i + 1][0] != "out"

        def FRESH(i):
            return i == 0 or stages[i][0] == "out"

        norm_at = {norm_before[q]: start[q] for q in norm_before}
        norm_at[NORMS - 1] = total

        FIRST = 3
        SECTIONS = {}
        for fi, (l, f) in enumerate(((0, 0), (0, 1), (1, 0))):
            for st, (kind, b) in enumerate((("up", 0), ("down", 0), ("up", 1), ("down", 1), ("up", 2))):
                SECTIONS[kind, l, f, b] = 5 * fi + st
        COLUMNWISE = 2
        gate_ring = w_hi_f[:, :, :, :].rearrange("p s k w -> p (s k w)")[:, 0:2 * D].rearrange("p (s n) -> p s n", s=2)
        gate_sums = work[:, RING * D:RING * D + 2 * D].rearrange("p (g n) -> p g n", g=2)
        gate_full = [sem(f"gate_full{i}") for i in range(2)]
        gate_acc = sem("gate_acc")
        gate_sum = sem("gate_sum")
        sec_ring = work[:, 0:2 * D].rearrange("p (s n) -> p s n", s=2)
        sec_sum = big[:, 16:24, :].rearrange("p t n -> p (t n)")[:, 0:4 * D].rearrange("p (a g n) -> p a g n", a=2, g=2)
        ones = eps[:, 15:16]

        def sum_steps(q, k, g=0):
            return 2 * k + (18 * q + g + 2)

        def sections_at(key, j):
            kind, l, f, b = key
            up = SECTIONS.get(("up", l, f, b))
            own = SECTIONS.get(key)
            return ([up] if j == min(b, 1) and up is not None else []) + ([own] if j == DT - 1 and own is not None else [])

        def loop_and_last(eng, turns, turn):
            if turns > 1:
                with eng.Fori(0, turns - 1) as i:
                    turn(i, False)
            turn(turns - 1, True)

        cols3 = cols[:, :].unsqueeze(2)
        kam3 = kam.unsqueeze(2)

        hh = h_hi_f[:, :, :].rearrange("p t n -> p (t n)")
        hl = h_lo_f[:, :, :].rearrange("p t n -> p (t n)")
        wh = w_hi_f[:, :, :, :].rearrange("p s k w -> p (s k w)")
        wl = w_lo_f[:, :, :, :].rearrange("p s k w -> p (s k w)")
        rw = raw[:, :, :, :].rearrange("p s k w -> p (s k w)")

        a_keys = hh[:, 0:1280].rearrange("p (g n) -> p g n", g=2)
        a_pkeys = hh[:, 1280:1536].rearrange("p (g n) -> p g n", g=2)
        a_vtok = hh[:, 1536:2176].rearrange("p (t n) -> p t n", n=P)
        a_vpast, a_kpast = hh[:, 2176:2304], hh[:, 2304:2432]
        a_kpast_t, a_kout = hh[:, 2432:2560], hh[:, 2560:2688]
        a_sink = hh[:, 2688:2696]
        a_q, a_qp = hh[:, 2700:3212], hh[:, 3212:3340]
        a_t1, a_t2 = hh[:, 3340:3852], hh[:, 3852:4364]
        a_max, a_neg, a_es, a_den, a_rden = ([hh[:, o + 8 * i:o + 5 + 8 * i] for o in (4400, 4448)] for i in range(5))
        a_sk = hh[:, 4440:4442]
        a_s, a_e = ([o[:, q:q + 2560].rearrange("p (b n) -> p b n", b=5) for o in (hl, work)] for q in (0, 2560))
        a_pt = wh[:, 0:2048]
        WIN = [(max(0, b - 1), min(NB, b + 2)) for b in range(NB)]
        ENDS = [P + (k1 - k0) * P for k0, k1 in WIN]
        PIECES = [(b, i) for b in range(NB) for i in range(ENDS[b] // P)] + [(NB, 0)]

        a_load, a_pe, a_act, a_dve, a_out = (sem(f"a_{n}") for n in ("load", "pe", "act", "dve", "out"))
        APE0 = Steps(a_pe, ["past_t", "v_t", "dup", "dup2"])
        AAC0 = Steps(a_act, ["past_t", "v_t", "dup2"])
        ADV0 = Steps(a_dve, ["mul0", "keys0", "mul1", "keys1"])
        APE = Steps(a_pe, ["rot", "sc0", "sc1", "ta0", "tb0", "pv0", "ta1", "tb1", "pv1"], 4)
        AAC = Steps(a_act, ["qp", "exp0", "pa0", "exp1", "pb0", "o0", "pa1", "pb1", "o1"], 3)
        ADV = Steps(a_dve, ["rope1", "rope", "s0", "mx0", "ng0", "s1", "dn0", "rd0", "pn0", "mx1", "ng1", "dn1", "rd1", "pn1"], 4)
        HALF_PIECES = 8
        IN_AB = start["in", 0, 0, 0]
        IN_C = start["in", 1, 0, 0]

        def sp_attn_ab(sp):
            sp.wait_ge(slab_used, IN_AB + AB_TILES + RING)
            sp.dma_start(a_vpast, T["cache_a_v"][0, 0].rearrange("t g d -> t (g d)")).then_inc(a_load, 16)
            sp.dma_start(a_kpast, T["cache_a_k"][0, 0].rearrange("t g d -> t (g d)")).then_inc(a_load, 16)
            sp.dma_start(a_sink, T["a_sink"].to_broadcast([P, AH])).then_inc(a_load, 16)
            sp.wait_ge(a_act, AAC0.value("v_t"))
            sp.dma_start(T["new_a_k"][0, 0].rearrange("t g d -> t (g d)"), a_kout).then_inc(a_out, 16)
            sp.dma_start(T["new_a_v"][0, 0].rearrange("t g d -> t (g d)"), a_vtok[:, 4, :]).then_inc(a_out, 16)

        def pe_attn_ab(pe):
            pe.wait_ge(a_load, 48)
            pe.wait_ge(ab_shift, 3 * AB_TILES)
            nc.tensor.transpose(pp[0][:, 0, 0:P], a_kpast, ident)
            nc.tensor.transpose(pp[0][:, 0, P:2 * P], big[:, T_KA, LAT:TOK], ident).then_inc(APE0.sem("past_t"), 1)
            for t in range(NCH):
                ins = nc.tensor.transpose(pp[1][:, t // 4, (t % 4) * P:(t % 4 + 1) * P], big[:, T_VA, t * P:(t + 1) * P], ident)
            ins.then_inc(APE0.sem("v_t"), 1)
            for g in range(2):
                nc.tensor.matmul(pp[2][:, g, :], dup[g], big[:, T_KA, 0:LAT], start=True, stop=True)
                ins = nc.tensor.matmul(pp[3][:, g, :], rdup[g], big[:, T_KA, 0:LAT], start=True, stop=True)
            ins.then_inc(APE0.sem("dup"), 1)
            pe.wait_ge(a_act, AAC0.value("past_t"))
            for g in range(2):
                nc.tensor.matmul(pp[0][:, g, 0:P], dup[g], a_kpast_t, start=True, stop=True)
                ins = nc.tensor.matmul(pp[0][:, g, P:2 * P], dup[g], big[:, T_KA, LAT:TOK], start=True, stop=True)
            ins.then_inc(APE0.sem("dup2"), 1)

            for g in range(2):
                with pe.Fori(0, 2) as jj:
                    it = jj + 2 * g
                    pe.wait_ge(a_act, AAC.before(it) - 1)
                    pe.wait_ge(a_dve, ADV.before(it))
                    nc.tensor.matmul(pp[2][:, 0, :], rot, big[:, it, 0:LAT], start=True, stop=True).then_inc(APE.sem("rot"), 1)
                    for h in range(2):
                        r = slice(h * HD, h * HD + HD)
                        if h == 0:
                            pe.wait_ge(a_dve, ADV.value("rope", it))
                            pe.wait_ge(a_act, AAC.value("qp", it))
                        else:
                            pe.wait_ge(a_dve, ADV.value("s0", it))
                        for b in range(NB):
                            ps = pp[b // 2][:, b % 2, :]
                            q = a_q[r, b * P:(b + 1) * P]
                            k0, k1 = WIN[b]
                            nc.tensor.matmul(ps[:, 0:P], q, a_keys[r, g, 0:P], start=True, stop=True)
                            nc.tensor.matmul(ps[:, P:ENDS[b]], q, a_keys[r, g, P + k0 * P:P + k1 * P], start=True, stop=True)
                        nc.tensor.matmul(pp[0][:, 0, ENDS[0]:ENDS[0] + P], a_qp[r, :], a_pkeys[r, g, :], start=True, stop=True
                                         ).then_inc(APE.sem(f"sc{h}"), 1)
                    for h in range(2):
                        r = slice(h * HD, h * HD + HD)

                        def turn(part):
                            for s in part:
                                b, i = PIECES[s]
                                z = s % HALF_PIECES
                                ins = nc.tensor.transpose(pp[2][:, z // 4, z % 4 * P:z % 4 * P + P],
                                                          a_e[h][:, b, i * P:(i + 1) * P], ident)
                            return ins

                        def weigh(part):
                            for s in part:
                                b, i = PIECES[s]
                                last = s + 1 == len(PIECES) or PIECES[s + 1][0] != b
                                if b == NB:
                                    v = a_vtok[:, NB, g * HD:(g + 1) * HD]
                                elif i == 0:
                                    v = a_vpast[:, g * HD:(g + 1) * HD]
                                else:
                                    v = a_vtok[:, WIN[b][0] + i - 1, g * HD:(g + 1) * HD]
                                out = pp[3][r, b // NB, (b % NB) * P:(b % NB + 1) * P]
                                ins = nc.tensor.matmul(out, v, a_pt[:, s * P:(s + 1) * P], start=(i == 0), stop=last)
                            return ins

                        pe.wait_ge(a_dve, ADV.value(f"pn{h}", it))
                        if h:
                            pe.wait_ge(a_act, AAC.value("pb0", it))
                        turn(range(HALF_PIECES)).then_inc(APE.sem(f"ta{h}"), 1)
                        pe.wait_ge(a_act, AAC.value(f"pa{h}", it))
                        turn(range(HALF_PIECES, len(PIECES))).then_inc(APE.sem(f"tb{h}"), 1)
                        weigh(range(HALF_PIECES))
                        pe.wait_ge(a_act, AAC.value(f"pb{h}", it))
                        weigh(range(HALF_PIECES, len(PIECES))).then_inc(APE.sem(f"pv{h}"), 1)

        def act_attn_ab(act):
            act.wait_ge(a_pe, APE0.value("past_t"))
            nc.scalar.activation(hh[:, 2432:2688], pp[0][:, 0, 0:2 * P], ACT.Copy).then_inc(AAC0.sem("past_t"), 1)
            act.wait_ge(a_pe, APE0.value("v_t"))
            nc.scalar.activation(hh[:, 1536:2048], pp[1][:, 0, :], ACT.Copy)
            nc.scalar.activation(hh[:, 2048:2176], pp[1][:, 1, 0:P], ACT.Copy).then_inc(AAC0.sem("v_t"), 1)
            act.wait_ge(a_pe, APE0.value("dup2"))
            nc.scalar.activation(a_keys[:, :, 0:P], pp[0][:, :, 0:P], ACT.Copy)
            nc.scalar.activation(a_pkeys, pp[0][:, :, P:2 * P], ACT.Copy).then_inc(AAC0.sem("dup2"), 1)
            nc.scalar.preload_act_table(ACT.Exp)
            with act.Fori(0, 4) as it:
                act.wait_ge(a_act, AAC.before(it))
                nc.scalar.activation(a_qp, big[:, it, LAT:TOK], ACT.Copy).then_inc(AAC.sem("qp"), 1)

                def exps(h):
                    act.wait_ge(a_dve, ADV.value(f"ng{h}", it))
                    nc.scalar.activation(a_es[h], a_neg[h], ACT.Exp, bias=a_sk[:, h:h + 1])
                    for b in range(5):
                        n = ENDS[b] if b < NB else P
                        ins = nc.scalar.activation(a_e[h][:, b, 0:n], a_s[h][:, b, 0:n], ACT.Exp, bias=a_neg[h][:, b:b + 1],
                                                   accum_out=a_den[h][:, b:b + 1])
                    ins.then_inc(AAC.sem(f"exp{h}"), 1)

                def turned(h, part):
                    act.wait_ge(a_pe, APE.value(f"t{part}{h}", it))
                    if part == "a":
                        ins = nc.scalar.activation(halves(a_pt[:, 0:1024]), pp[2][:, :, :], ACT.Copy)
                    else:
                        nc.scalar.activation(a_pt[:, 1024:1536], pp[2][:, 0, :], ACT.Copy)
                        ins = nc.scalar.activation(a_pt[:, 1536:1920], pp[2][:, 1, 0:384], ACT.Copy)
                    ins.then_inc(AAC.sem(f"p{part}{h}"), 1)

                for h in range(2):
                    if h == 0:
                        exps(0)
                    turned(h, "a")
                    if h == 0:
                        exps(1)
                    turned(h, "b")
                    act.wait_ge(a_pe, APE.value(f"pv{h}", it))
                    r = slice(h * HD, h * HD + HD)
                    nc.scalar.activation(big[r, it, 0:LAT], pp[3][r, 0, :], ACT.Copy)
                    nc.scalar.activation(big[r, it, LAT:TOK], pp[3][r, 1, 0:P], ACT.Copy).then_inc(AAC.sem(f"o{h}"), 1)

        def dve_attn_ab(dve):
            dve.wait_ge(a_pe, APE0.value("dup"))
            for g in range(2):
                if g:
                    dve.wait_ge(a_dve, ADV0.value("keys0"))
                nc.vector.tensor_tensor(a_t1, pp[2][:, g, :], cos, ALU.mult)
                nc.vector.tensor_tensor(a_t2, pp[3][:, g, :], sin, ALU.mult).then_inc(ADV0.sem(f"mul{g}"), 1)
                dve.wait_ge(a_dve, ADV0.value(f"mul{g}"))
                nc.vector.tensor_tensor(a_keys[:, g, P:TOK], a_t1, a_t2, ALU.add).then_inc(ADV0.sem(f"keys{g}"), 1)
            with dve.Fori(0, 4) as it:
                dve.wait_ge(a_pe, APE.value("rot", it))
                nc.vector.tensor_copy(a_sk, a_sink.rearrange("p (a b) -> p a b", b=2)[:, it, :])
                nc.vector.tensor_tensor(a_t1, big[:, it, 0:LAT], cos, ALU.mult)
                nc.vector.tensor_tensor(a_t2, pp[2][:, 0, :], sin, ALU.mult).then_inc(ADV.sem("rope1"), 1)
                dve.wait_ge(a_dve, ADV.value("rope1", it))
                nc.vector.tensor_tensor(a_q, a_t1, a_t2, ALU.add).then_inc(ADV.sem("rope"), 1)

                def scaled(h):
                    dve.wait_ge(a_pe, APE.value(f"sc{h}", it))
                    for b in range(NB):
                        m = band[:, 0:ENDS[b]] if b else band[:, 512:512 + ENDS[b]]
                        nc.vector.scalar_tensor_tensor(out=a_s[h][:, b, 0:ENDS[b]], in0=pp[b // 2][:, b % 2, 0:ENDS[b]],
                                                       scalar=SCALE, in1=m, op0=ALU.mult, op1=ALU.add)
                    nc.vector.tensor_scalar(a_s[h][:, NB, 0:P], pp[0][:, 0, ENDS[0]:ENDS[0] + P], SCALE, None, ALU.mult
                                            ).then_inc(ADV.sem(f"s{h}"), 1)

                def maxima(h):
                    dve.wait_ge(a_dve, ADV.value(f"s{h}", it))
                    for b in range(5):
                        ins = nc.vector.tensor_reduce(a_max[h][:, b:b + 1], a_s[h][:, b, 0:(ENDS[b] if b < NB else P)], AX.X, ALU.max)
                    ins.then_inc(ADV.sem(f"mx{h}"), 1)
                    dve.wait_ge(a_dve, ADV.value(f"mx{h}", it))
                    nc.vector.tensor_scalar(a_neg[h], a_max[h], a_sk[:, h:h + 1], -1.0, ALU.max, ALU.mult
                                            ).then_inc(ADV.sem(f"ng{h}"), 1)

                def divided(h):
                    dve.wait_ge(a_act, AAC.value(f"exp{h}", it))
                    nc.vector.tensor_tensor(a_den[h], a_den[h], a_es[h], ALU.add).then_inc(ADV.sem(f"dn{h}"), 1)
                    dve.wait_ge(a_dve, ADV.value(f"dn{h}", it))
                    nc.vector.reciprocal(a_rden[h], a_den[h]).then_inc(ADV.sem(f"rd{h}"), 1)
                    dve.wait_ge(a_dve, ADV.value(f"rd{h}", it))
                    for b in range(5):
                        n = ENDS[b] if b < NB else P
                        ins = nc.vector.tensor_scalar(a_e[h][:, b, 0:n], a_e[h][:, b, 0:n], a_rden[h][:, b:b + 1], None, ALU.mult)
                    ins.then_inc(ADV.sem(f"pn{h}"), 1)

                scaled(0)
                maxima(0)
                scaled(1)
                divided(0)
                maxima(1)
                divided(1)

        r_ar = hh[:, 0:1280].rearrange("p (c two n) -> p c two n", c=NCH, two=2)
        r_beta, r_kappa, r_kkn, r_y = (hh[:, 1280 + 640 * i:1920 + 640 * i] for i in range(4))
        r_vtok = hh[:, 3840:4480].rearrange("p (c n) -> p c n", c=NCH)
        r_rhop = hh[:, 4480:4992]
        r_ktok = hl[:, 0:640].rearrange("p (c n) -> p c n", c=NCH)
        r_btok = hl[:, 640:1280].rearrange("p (c n) -> p c n", c=NCH)
        r_av = hl[:, 1280:2560].rearrange("p (u n) -> p u n", n=P)
        r_nwu = hl[:, 2560:3840].rearrange("p (u n) -> p u n", n=P)
        r_v, r_tb = hl[:, 3840:4480], hl[:, 4480:5120]
        r_sig, r_cum, r_a, r_kd, r_e1, r_e2 = (wh[:, 640 * i:640 * (i + 1)] for i in range(6))
        r_ft2, r_ft1 = wh[:, 3840:4096].rearrange("p (c n) -> p c n", n=P), hh[:, 4992:5120]
        r_ft = [r_ft2[:, 0, :], r_ft2[:, 1, :], r_ft1]
        r_p = wl[:, 0:640].rearrange("p (u n) -> p u n", n=HD)
        r_n = wl[:, 640:1280].rearrange("p (u n) -> p u n", n=HD)
        r_g = wl[:, 1280:1600].rearrange("p (c n) -> p c n", n=HD)
        r_z = wl[:, 1600:1920].rearrange("p (c n) -> p c n", n=HD)
        r_ht = wl[:, 1920:1925]
        r_d1, r_dd = ([wl[:, o + 8 * d:o + 8 * d + 5] for d in range(2)] for o in (3872, 3888))
        r_sigs, r_as, r_kdd = (r_sig, R[:, 23 * TOK:24 * TOK]), (r_a, r_kd), (None, r_sig)
        r_w2, r_a2, r_g2 = (wl[:, 1952 + P * i:1952 + P * (i + 1)] for i in range(3))
        r_so = wl[0:HD, 2336:2592].rearrange("p (d n) -> p d n", d=2)
        r_kds, r_bonus = wl[:, 2592:3232], wl[:, 3232:3872]
        r_mask = [rw[:, 512 * i:512 * (i + 1)] for i in range(2)]
        r_late = rw[:, 1024:1472].rearrange("p (l n) -> p l n", n=HD)
        r_early = rw[:, 1472:1920].rearrange("p (l n) -> p l n", n=HD)
        r_reset, r_eye2 = rw[:, 1920:2560], rw[:, 2560:2624]
        r_s0t = rw[:, 2624:3136].rearrange("p (q n) -> p q n", n=HD)
        r_gate = rw[:, 3136:3776]
        r_s0 = work[0:HD, 0:1024].rearrange("p (q n) -> p q n", n=P)
        r_u4 = work[:, 0:5120].rearrange("p (u m n) -> p u m n", m=4, n=P)
        r_am = work[:, 5120:6400].rearrange("p (u n) -> p u n", n=P)
        r_t = R[:, 12160:13440].rearrange("p (u n) -> p u n", n=P)
        r_tt = R[:, 13440:14720].rearrange("p (u n) -> p u n", n=P)
        NU = 2 * NCH
        NL = 7

        def bank(i):
            return pp[i // 2][:, i % 2, :]

        def level_cols(ap, lev, half):
            return ap.rearrange("p u (k two b) -> p u k two b", two=2, b=1 << lev)[:, :, :, half, :]

        def sides(d):
            return (0, 1, r_late, r_early) if d == 0 else (1, 0, r_early, r_late)

        def lv_bank(k, g, n):
            u0, u1 = GROUPS[g]
            return bank(LBANK[k][g])[:, 0:(u1 - u0) * n].rearrange("p (u n) -> p u n", n=n)

        def chunks(d):
            return (0, 1, 2, 3) if d == 0 else (3, 2, 1, 0)

        b_gate = sem("b_gate")
        b_load, b_lora, b_pe, b_act, b_dve, b_out = (sem(f"b_{n}") for n in ("load", "lora", "pe", "act", "dve", "out"))
        GROUPS = [(0, 4), (4, 7), (7, 10)]
        GS = range(len(GROUPS))
        LV = [("P", 1, g) for g in GS]
        for lev in range(1, NL - 1):
            LV += [("Q", lev, g) for g in GS]
            for g in GS:
                LV += [("X", lev, g)] + ([("P", lev + 1, g)] if lev < NL - 2 else [])
        LV += [(k, NL - 1, g) for k in "NR" for g in GS]
        LD = [({"P": "pn", "N": "pn", "Q": "t", "R": "t"}[k], lev, g) for k, lev, g in LV if k != "X"]
        LX = [("x", lev, g) for k, lev, g in LV if k == "X"]
        LBANK = {"P": (0, 1, 2), "N": (0, 1, 2), "Q": (3, 4, 5), "R": (3, 4, 5), "X": (6, 7, 6)}
        named = lambda steps, d: [f"{k}{lev}{g}_{d}" for k, lev, g in steps]
        EARLY = {2: ["cum"], 5: ["ht", "q"], 8: ["m"], 9: ["kd1"], 11: ["kd"], 24: ["al"], 26: ["kap"], 28: ["arr"], 30: ["beta"]}
        EARLY_ACT = {5: 0, 7: 1, 8: 2, 10: 3}
        KK_AT = (20, 12)

        def with_early(steps, d):
            out = []
            for i, name in enumerate(steps):
                out.append(f"{name}_{d}")
                if d == 0:
                    out += [f"{n}_1" for n in EARLY.get(i, [])]
                elif i == KK_AT[0]:
                    out.append("kkmul+")
            return out

        BPE = Steps(b_pe, ["vT", "z_0", "z_1"] + [f"{n}_{d}" for d in range(2) for n in
                    ["tr"] + [f"pr{u}" for u in range(NU)] + ["A", "RV"]
                    + [f"{k}{lev}{g}" for k, lev, g in LV] + (["kkss+"] if d else []) + ["WU", "FG", "S0", "S1", "S2", "Y", "So"]] + ["bs", "gate", "mu", "var"], 2)
        lx0, lx1 = named(LX, 0), named(LX, 1)
        BAC = Steps(b_act, ["vcopy", "vtok", "sig_0", "sig_1", "ex_0", "tok_0", "rv_0"] + lx0[:11] + ["ex_1"]
                    + lx0[11:] + ["wu_0", "y0", "so_0", "tok_1", "rv_1"] + lx1[:13] + ["kksq+"] + lx1[13:] + ["wu_1", "kkroot+", "so_1", "gt", "ysq", "sd"], 3)
        BDV = Steps(b_dve, [f"{n}_0" for n in ("cum", "ht", "q", "m", "kd1", "kd", "arr", "beta")]
                    + [f"{n}_0" for n in [f"U{u}" for u in range(NU)] + ["Am"] + [f"{n}{g}" for g in GS for n in ("id", "T0")]]
                    + with_early([f"{k}{lev}{g}" for k, lev, g in LD], 0) + ["FG_0", "Z0_0", "Z1_0", "Z2_0", "rh_1"]
                    + [f"{n}_1" for n in [f"U{u}" for u in range(NU)] + ["Am"] + [f"{n}{g}" for g in GS for n in ("id", "T0")]]
                    + with_early([f"{k}{lev}{g}" for k, lev, g in LD], 1) + ["FG_1", "Z0_1", "Z1_1", "Z2_1"]
                    + ["kkmax+", "kkrec+", "kkn+", "y1", "bn", "bonus", "yc", "rs", "yn", "yg", "yb", "yo"], 10)

        def sp_rwkv(sp):
            sp.wait_ge(lo_full, IN_AB + AB_TILES + RING)
            sp.wait_ge(a_act, AAC.before(4))
            sp.dma_start(rw[:, 0:RWKV_W], T["t_rwkv"]).then_inc(b_load, 16)
            for d in range(2):
                sp.dma_start(r_s0[:, 4 * d:4 * d + 4, :].rearrange("p q (h n) -> p (q h) n", h=2),
                             T["state_b_wkv"][0, 0, d].rearrange("h i j -> i h j")).then_inc(b_load, 16)
            w2 = T["b_w2"][0].rearrange("d l (t w) -> (d l) t w", w=P)
            a2 = T["b_a2"][0].rearrange("d l (t w) -> (d l) t w", w=P)
            g2 = T["b_g2"][0].rearrange("l (t w) -> l t w", w=P)
            def lora(it):
                sp.dma_start(r_w2, w2[:, it, :]).then_inc(b_lora, 16)
                sp.dma_start(r_a2, a2[:, it, :]).then_inc(b_lora, 16)

            def turn(it, last):
                sp.wait_ge(b_pe, BPE.before(it))
                sp.dma_start(r_g2, g2[:, it, :]).then_inc(b_gate, 16)
                if not last:
                    sp.wait_ge(b_pe, BPE.value("z_1", it))
                    lora(it + 1)
                for d in range(2):
                    sp.wait_ge(b_act, BAC.value(f"so_{d}", it))
                    dst = T["new_b_wkv"][0, 0, d].rearrange("(t h) i j -> i t h j", h=2)[:, it, :, :]
                    sp.dma_start(dst, r_so[:, d, :].rearrange("p (h n) -> p h n", h=2)).then_inc(b_out, 16)

            lora(0)
            loop_and_last(sp, BT, turn)
            sp.wait_ge(b_out, 32 * BT + 32)
            sp.wait_ge(b_dve, BDV.before(BT))

        def pe_rwkv(pe):
            pe.wait_ge(b_load, 48)
            pe.wait_ge(a_act, AAC.before(4))
            for q in range(2 * BT):
                ins = nc.tensor.transpose(bank(0)[:, q * HD:(q + 1) * HD], r_s0[:, q, :], ident[0:HD, 0:HD])
            ins.then_inc(b_pe, 1)

            def kk_squares():
                for c in range(2):
                    ins = nc.tensor.matmul(bank(6 + c)[:, 0:HALF], blk, r_tb[:, c * HALF:(c + 1) * HALF], start=True, stop=True)
                return ins

            pe.wait_ge(b_act, 2)
            kk_squares().then_inc(b_pe, 1)
            heads = [slice(h * HD, h * HD + HD) for h in range(2)]
            with pe.Fori(0, BT) as it:
                def V(steps, name):
                    return steps.value(name, it)

                pe.wait_ge(b_act, V(BAC, "vcopy"))
                for c in range(NCH):
                    ins = nc.tensor.transpose(bank(c // 4)[:, c % 4 * P:c % 4 * P + P], r_v[:, c * P:(c + 1) * P], ident)
                ins.then_inc(BPE.sem("vT"), 1)
                for d in range(2):
                    dr = heads[d]
                    if d == 0:
                        pe.wait_ge(b_lora, 32 * it + 32)
                    else:
                        pe.wait_ge(b_act, V(BAC, "vtok"))
                    for c in range(2):
                        nc.tensor.matmul(bank(4 - 4 * d + c)[:, 0:HALF], r_w2[dr, :], big[dr, T_W, c * HALF:(c + 1) * HALF],
                                         start=True, stop=True)
                        ins = nc.tensor.matmul(bank(6 - 4 * d + c)[:, 0:HALF], r_a2[dr, :], big[dr, T_A, c * HALF:(c + 1) * HALF],
                                               start=True, stop=True)
                    ins.then_inc(BPE.sem(f"z_{d}"), 1)
                for d in range(2):
                    pe.wait_ge(b_dve, V(BDV, f"beta_{d}"))
                    if d:
                        pe.wait_ge(b_dve, V(BDV, "rh_1"))
                        pe.wait_ge(b_act, V(BAC, "so_0"))
                    for s in range(3 * NCH):
                        c = s % NCH
                        src = (r_ar[:, c, 0, :], r_beta[:, c * P:(c + 1) * P], r_kappa[:, c * P:(c + 1) * P])[s // NCH]
                        ins = nc.tensor.transpose(bank(s // 4)[:, s % 4 * P:s % 4 * P + P], src, ident)
                    ins.then_inc(BPE.sem(f"tr_{d}"), 1)
                    for u in range(NU):
                        c, r = u % NCH, heads[u // NCH]
                        if u >= 4:
                            pe.wait_ge(b_dve, V(BDV, f"U{u - 4}_{d}"))
                        ps = bank(4 + u % 4)
                        tk = slice(c * P, (c + 1) * P)
                        ar = r_ar[r, c, :, :]
                        nc.tensor.matmul(ps[:, 0:2 * P], r_beta[r, tk], ar, start=True, stop=True)
                        nc.tensor.matmul(ps[:, 2 * P:4 * P], r_kappa[r, tk], ar, start=True, stop=True
                                         ).then_inc(BPE.sem(f"pr{u}_{d}"), 1)
                    pe.wait_ge(b_act, V(BAC, f"tok_{d}"))
                    for u in range(NU):
                        c, r = u % NCH, heads[u // NCH]
                        ins = nc.tensor.matmul(bank(2 * (u // NCH) + c // 4)[:, c % 4 * P:c % 4 * P + P], r_ar[r, c, 0, :],
                                               r_beta[r, c * P:(c + 1) * P], start=True, stop=True)
                    ins.then_inc(BPE.sem(f"A_{d}"), 1)
                    pe.wait_ge(b_dve, V(BDV, f"U{NU - 1}_{d}"))
                    for u in range(NU):
                        c, r = u % NCH, heads[u // NCH]
                        ins = nc.tensor.matmul(bank(6 + u // 8)[:, u % 8 * HD:u % 8 * HD + HD], r_u4[:, u, 2, :],
                                               r_vtok[:, c, r], start=True, stop=True)
                    ins.then_inc(BPE.sem(f"RV_{d}"), 1)
                    hp, hn, _, _ = sides(d)
                    for k, lev, g in LV:
                        step = f"{k}{lev}{g}_{d}"
                        if k == "P":
                            pe.wait_ge(b_dve, V(BDV, f"T0{g}_{d}" if lev == 1 else f"t{lev - 1}{g}_{d}"))
                        elif k == "X":
                            if lev == 1 and g == 0:
                                pe.wait_ge(b_act, V(BAC, f"rv_{d}"))
                            if g == 2:
                                pe.wait_ge(b_act, V(BAC, f"x{lev}0_{d}"))
                            pe.wait_ge(b_dve, V(BDV, f"t{lev}{g}_{d}"))
                        elif k == "N":
                            pe.wait_ge(b_act, V(BAC, f"x{lev - 1}{g}_{d}"))
                        else:
                            if k == "Q" and lev > 1:
                                pe.wait_ge(b_act, V(BAC, f"x{lev - 1}{g}_{d}"))
                            pe.wait_ge(b_dve, V(BDV, f"pn{lev}{g}_{d}"))
                        for u in range(*GROUPS[g]):
                            out = lv_bank(k, g, P if k in "PX" else HD)[:, u - GROUPS[g][0], :]
                            if k == "X":
                                ins = nc.tensor.transpose(out, r_t[:, u, :], ident)
                                continue
                            w, m = {"P": (r_u4[:, u, 0, :], r_t[:, u, :]), "Q": (r_tt[:, u, :], r_p[:, u, :]),
                                    "N": (r_am[:, u, :], level_cols(r_tt, lev, hn)[:, u]),
                                    "R": (r_t[:, u, :], r_n[:, u, :])}[k]
                            ins = nc.tensor.matmul(out, w, m, start=True, stop=True)
                        ins.then_inc(BPE.sem(step), 1)
                    if d:
                        pe.wait_ge(b_act, V(BAC, f"x{NL - 2}2_1"))
                        kk_squares().then_inc(BPE.sem("kkss+_1"), 1)
                    pe.wait_ge(b_dve, V(BDV, f"t{NL - 1}2_{d}"))
                    for u in range(NU):
                        ins = nc.tensor.matmul(bank(u // 4)[:, u % 4 * P:u % 4 * P + P], r_tt[:, u, :], r_av[:, u, :],
                                               start=True, stop=True)
                    ins.then_inc(BPE.sem(f"WU_{d}"), 1)
                    pe.wait_ge(b_act, V(BAC, f"wu_{d}"))
                    order = chunks(d)
                    for h in range(2):
                        r = heads[h]
                        for i, c in enumerate(order[:3]):
                            nc.tensor.matmul(bank(3)[r, i * HD:(i + 1) * HD], r_nwu[:, NCH * h + c, 0:HD], r_btok[:, c, r],
                                             start=True, stop=True)
                        for c in range(NB):
                            nc.tensor.matmul(bank(5)[r, c * P:(c + 1) * P], r_nwu[:, NCH * h + c, 0:HD], r_u4[:, NCH * h + c, 1, :],
                                             start=True, stop=True)
                        for c in range(NCH):
                            nc.tensor.matmul(bank(4)[r, c * HD:(c + 1) * HD], r_ktok[:, c, r], r_vtok[:, c, r],
                                             start=True, stop=False)
                            ins = nc.tensor.matmul(bank(4)[r, c * HD:(c + 1) * HD], r_btok[:, c, r],
                                                   r_nwu[:, NCH * h + c, HD:P], start=False, stop=True)
                    ins.then_inc(BPE.sem(f"FG_{d}"), 1)
                    for i in range(3):
                        if d and i == 0:
                            pe.wait_ge(b_act, V(BAC, "kkroot+"))
                        pe.wait_ge(b_dve, V(BDV, f"Z{i - 1}_{d}" if i else f"FG_{d}"))
                        nc.tensor.matmul(bank(7)[:, i * HD:(i + 1) * HD], r_ft[i], r_z[:, order[i], :], start=True, stop=True
                                         ).then_inc(BPE.sem(f"S{i}_{d}"), 1)
                    pe.wait_ge(b_dve, V(BDV, f"Z2_{d}"))
                    for h in range(2):
                        r = heads[h]
                        for c in range(NCH):
                            u = NCH * h + c
                            out = bank(c // 4)[r, c % 4 * P:c % 4 * P + P]
                            nc.tensor.matmul(out, r_vtok[:, c, r], r_u4[:, u, 3, :], start=True, stop=False)
                            ins = nc.tensor.matmul(out, r_nwu[:, u, HD:P], r_u4[:, u, 1, :], start=False, stop=(c == NB))
                            if c < NB:
                                ins = nc.tensor.matmul(out, r_z[r, c, :], r_rhop[r, c * P:(c + 1) * P], start=False, stop=True)
                    ins.then_inc(BPE.sem(f"Y_{d}"), 1)
                    nc.tensor.transpose(bank(2)[0:HD, 0:P], r_g[:, NB, :], ident).then_inc(BPE.sem(f"So_{d}"), 1)
                pe.wait_ge(b_dve, V(BDV, "bn"))
                pe.wait_ge(b_act, V(BAC, "so_1"))
                for c in range(2):
                    ins = nc.tensor.matmul(bank(2 + c)[:, 0:HALF], blk, r_e2[:, c * HALF:(c + 1) * HALF], start=True, stop=True)
                ins.then_inc(BPE.sem("bs"), 1)
                pe.wait_ge(b_gate, 16 * it + 16)
                for c in range(2):
                    ins = nc.tensor.matmul(bank(4 + c)[:, 0:HALF], r_g2, big[:, T_G, c * HALF:(c + 1) * HALF], start=True, stop=True)
                ins.then_inc(BPE.sem("gate"), 1)
                for c in range(2):
                    ins = nc.tensor.matmul(bank(6 + c)[:, 0:HALF], blk, r_y[:, c * HALF:(c + 1) * HALF], start=True, stop=True)
                ins.then_inc(BPE.sem("mu"), 1)
                pe.wait_ge(b_act, V(BAC, "ysq"))
                for c in range(2):
                    ins = nc.tensor.matmul(bank(c)[:, 0:HALF], blk, r_sig[:, c * HALF:(c + 1) * HALF], start=True, stop=True)
                ins.then_inc(BPE.sem("var"), 1)

        def act_rwkv(act):
            act.wait_ge(ab_shift, 3 * AB_TILES)
            nc.scalar.activation(big[:, T_W, :], big[:, T_W, :], ACT.Tanh)
            nc.scalar.activation(big[:, T_G, :], big[:, T_G, :], ACT.Sigmoid)
            act.wait_ge(b_pe, 1)
            nc.scalar.activation(r_s0t, bank(0).rearrange("p (q n) -> p q n", n=HD), ACT.Copy).then_inc(b_act, 1)
            act.wait_ge(b_dve, 7)
            nc.scalar.activation(r_tb, r_kkn, ACT.Square).then_inc(b_act, 1)
            act.wait_ge(b_pe, 2)
            nc.scalar.activation(halves(r_a), pp[3][:, :, 0:HALF], ACT.Sqrt).then_inc(b_act, 1)
            act.wait_ge(b_dve, 10)
            with act.Fori(0, BT) as it:
                def V(steps, name):
                    return steps.value(name, it)

                act.wait_ge(b_act, BAC.before(it))
                act.wait_ge(b_dve, BDV.before(it) - 5)
                nc.scalar.activation(r_v, big[:, it + T_V, :], ACT.Copy).then_inc(BAC.sem("vcopy"), 1)
                act.wait_ge(b_pe, V(BPE, "vT"))
                nc.scalar.activation(r_vtok[:, 0:4, :], bank(0).rearrange("p (c n) -> p c n", n=P), ACT.Copy)
                nc.scalar.activation(r_vtok[:, 4, :], bank(1)[:, 0:P], ACT.Copy).then_inc(BAC.sem("vtok"), 1)
                for d in range(2):
                    act.wait_ge(b_pe, V(BPE, f"z_{d}"))
                    nc.scalar.activation(halves(r_sigs[d]), pp[2 - 2 * d][:, :, 0:HALF], ACT.Sigmoid,
                                         bias=cols3[:, it + (C_W0 + BT * d), :])
                    nc.scalar.activation(halves(r_as[d]), pp[3 - 2 * d][:, :, 0:HALF], ACT.Sigmoid,
                                         bias=cols3[:, it + (C_A0 + BT * d), :]).then_inc(BAC.sem(f"sig_{d}"), 1)

                def exponentials(d):
                    c4 = lambda ap: ap.rearrange("p (c n) -> p c n", n=P)
                    q, m, e1 = c4(r_cum), c4(r_sigs[d]), c4(r_e1)
                    rho = r_ar[:, :, 1, :] if d == 0 else c4(r_a)
                    return [(out, src, sg * DECAY) for out, src, sg in
                            (((r_ar[:, :, 0, :], m, -1), (rho, q, -1), (e1, q, 1)) if d == 0 else
                             ((r_ar[:, :, 0, :], q, 1), (rho, m, 1), (e1, m, -1)))] + [(r_d1[d], r_ht, -DECAY)]

                act.wait_ge(b_dve, V(BDV, "m_0"))
                for out, src, sg in exponentials(0):
                    ins = nc.scalar.activation(out, src, ACT.Exp, scale=sg)
                ins.then_inc(BAC.sem("ex_0"), 1)
                for d in range(2):
                    act.wait_ge(b_pe, V(BPE, f"tr_{d}"))
                    av = r_av.rearrange("p (h c) n -> p c h n", h=2)
                    c3 = lambda a, n: a.rearrange("p (c n) -> p c n", n=n)
                    nc.scalar.activation(av[:, 0:4, :, 0:HD], bank(0).rearrange("p (c h n) -> p c h n", h=2, n=HD), ACT.Copy)
                    nc.scalar.activation(av[:, 4, :, 0:HD], c3(bank(1)[:, 0:P], HD), ACT.Copy)
                    nc.scalar.activation(r_btok[:, 0:3, :], c3(bank(1)[:, P:512], P), ACT.Copy)
                    nc.scalar.activation(r_btok[:, 3:5, :], c3(bank(2)[:, 0:256], P), ACT.Copy)
                    nc.scalar.activation(r_ktok[:, 0:2, :], c3(bank(2)[:, 256:512], P), ACT.Copy)
                    nc.scalar.activation(r_ktok[:, 2:5, :], c3(bank(3)[:, 0:384], P), ACT.Copy).then_inc(BAC.sem(f"tok_{d}"), 1)
                    act.wait_ge(b_pe, V(BPE, f"RV_{d}"))
                    nc.scalar.activation(r_av[:, 0:8, HD:P], c3(bank(6), HD), ACT.Copy)
                    nc.scalar.activation(r_av[:, 8:10, HD:P], c3(bank(7)[:, 0:P], HD), ACT.Copy).then_inc(BAC.sem(f"rv_{d}"), 1)
                    for n, (_, lev, g) in enumerate(LX):
                        act.wait_ge(b_pe, V(BPE, f"X{lev}{g}_{d}"))
                        nc.scalar.activation(r_tt[:, slice(*GROUPS[g]), :], lv_bank("X", g, P), ACT.Copy
                                             ).then_inc(BAC.sem(f"x{lev}{g}_{d}"), 1)
                        if d == 1 and n == KK_AT[1]:
                            act.wait_ge(b_dve, V(BDV, "kkmul+"))
                            nc.scalar.activation(r_tb, r_kkn, ACT.Square).then_inc(BAC.sem("kksq+"), 1)
                        if d == 0 and n in EARLY_ACT:
                            if EARLY_ACT[n] == 0:
                                act.wait_ge(b_dve, V(BDV, "m_1"))
                            out, src, sg = exponentials(1)[EARLY_ACT[n]]
                            ins = nc.scalar.activation(out, src, ACT.Exp, scale=sg)
                            if EARLY_ACT[n] == 3:
                                ins.then_inc(BAC.sem("ex_1"), 1)
                    act.wait_ge(b_pe, V(BPE, f"WU_{d}"))
                    nc.scalar.activation(r_nwu[:, 0:4, :], c3(bank(0), P), ACT.Copy, scale=-1.0)
                    nc.scalar.activation(r_nwu[:, 4:8, :], c3(bank(1), P), ACT.Copy, scale=-1.0)
                    nc.scalar.activation(r_nwu[:, 8:10, :], c3(bank(2)[:, 0:256], P), ACT.Copy, scale=-1.0
                                         ).then_inc(BAC.sem(f"wu_{d}"), 1)
                    if d:
                        act.wait_ge(b_pe, V(BPE, "kkss+_1"))
                        nc.scalar.activation(halves(r_a), pp[3][:, :, 0:HALF], ACT.Sqrt).then_inc(BAC.sem("kkroot+"), 1)
                    if d == 0:
                        act.wait_ge(b_pe, V(BPE, "Y_0"))
                        nc.scalar.activation(r_y[:, 0:LAT], bank(0), ACT.Copy)
                        nc.scalar.activation(r_y[:, LAT:TOK], bank(1)[:, 0:P], ACT.Copy).then_inc(BAC.sem("y0"), 1)
                    act.wait_ge(b_pe, V(BPE, f"So_{d}"))
                    if d == 0:
                        act.wait_ge(b_out, 32 * it + 32)
                    nc.scalar.activation(r_so[:, d, :], bank(2)[0:HD, 0:P], ACT.Copy).then_inc(BAC.sem(f"so_{d}"), 1)
                act.wait_ge(b_pe, V(BPE, "gate"))
                nc.scalar.activation(halves(r_gate), pp[2][:, :, 0:HALF], ACT.Copy).then_inc(BAC.sem("gt"), 1)
                act.wait_ge(b_dve, V(BDV, "yc"))
                nc.scalar.activation(r_sig, r_cum, ACT.Square).then_inc(BAC.sem("ysq"), 1)
                act.wait_ge(b_pe, V(BPE, "var"))
                nc.scalar.activation(halves(r_e1), pp[0][:, :, 0:HALF], ACT.Sqrt, scale=1.0 / HD, bias=eps[:, 1:2]
                                     ).then_inc(BAC.sem("sd"), 1)

        def dve_rwkv(dve):
            dve.wait_ge(b_act, 1)
            dve.wait_ge(b_load, 48)
            dve.wait_ge(a_out, 32)
            v = nc.vector
            v.memset(r_ft2, 0.0)
            v.memset(r_ft1, 0.0).then_inc(b_dve, 6)
            dve.wait_ge(b_dve, 6)

            def kk_product(it, q):
                v.tensor_scalar(r_kkn, big[:, it + T_K, :], cols3[:, it + C_KK, :], None, ALU.mult).then_inc(q, 1)

            def kk_norm(qs, waits):
                v.tensor_scalar(r_a, r_a, 1e-12, None, ALU.max).then_inc(qs[0], 1)
                dve.wait_ge(b_dve, waits[0])
                v.reciprocal(r_a, r_a).then_inc(qs[1], 1)
                dve.wait_ge(b_dve, waits[1])
                v.tensor_tensor(r_kkn, r_kkn, r_a, ALU.mult).then_inc(qs[2], 1)

            kk_product(0, b_dve)
            dve.wait_ge(b_act, 3)
            kk_norm([b_dve] * 3, (8, 9))
            with dve.Fori(0, BT) as it:
                def V(steps, name):
                    return steps.value(name, it)


                def own(name):
                    dve.wait_ge(b_dve, V(BDV, name))

                dve.wait_ge(b_act, BAC.before(it))
                dve.wait_ge(b_dve, BDV.before(it))
                b3 = lambda a: a.rearrange("p (c n) -> p c n", n=P)

                def prepare(step, d):
                    q = BDV.sem(f"{step}_{d}")
                    sig, a, kd = r_sigs[d], r_as[d], r_kdd[d] if d else r_kds
                    al, rh = r_ar[:, :, 0, :], r_ar[:, :, 1, :]
                    if step == "cum":
                        dve.wait_ge(b_act, V(BAC, f"sig_{d}"))
                        v.tensor_tensor_scan(r_cum, r_reset, sig, 0.0, ALU.mult, ALU.add).then_inc(q, 1)
                    elif step == "ht":
                        own(f"cum_{d}")
                        v.tensor_scalar(r_ht, b3(r_cum)[:, :, P - 1], 0.5, None, ALU.mult).then_inc(q, 1)
                    elif step == "q":
                        own(f"ht_{d}")
                        v.tensor_tensor(b3(r_cum), b3(r_cum), r_ht.unsqueeze(2).to_broadcast([P, NCH, P]), ALU.subtract
                                        ).then_inc(q, 1)
                    elif step == "m":
                        own(f"q_{d}")
                        v.tensor_tensor(sig, r_cum, sig, ALU.subtract).then_inc(q, 1)
                    elif step == "kd1":
                        v.tensor_scalar(r_e2, a, cols3[:, it + C_KA, :], kam3[:, it, :], ALU.mult, ALU.add).then_inc(q, 1)
                    elif step == "kd":
                        own(f"kd1_{d}")
                        v.tensor_tensor(kd, r_e2, big[:, it + T_K, :], ALU.mult).then_inc(q, 1)
                    elif step == "al":
                        dve.wait_ge(b_act, V(BAC, f"ex_{d}"))
                        v.tensor_tensor(al, al, b3(r_kkn), ALU.mult).then_inc(q, 1)
                    elif step == "kap":
                        v.tensor_tensor(r_kappa, kd, r_e1, ALU.mult)
                        v.tensor_tensor(r_kds, r_kds, kd, ALU.add).then_inc(q, 1)
                    elif step == "arr":
                        if d == 0:
                            own("kd_0")
                            dve.wait_ge(b_act, V(BAC, "ex_0"))
                            v.tensor_tensor(al, al, b3(r_kkn), ALU.mult)
                            v.tensor_tensor(rh, rh, b3(big[:, it + T_R, :]), ALU.mult)
                            v.tensor_tensor(r_kappa, kd, r_e1, ALU.mult)
                        lo, hi = (0, 1) if d == 0 else (1, 0)
                        d1, dd = r_d1[d], r_dd[d]
                        v.tensor_tensor(dd[:, lo:lo + 3], d1[:, lo:lo + 3], d1[:, hi:hi + 3], ALU.mult)
                        v.tensor_copy(dd[:, NB:NCH], d1[:, NB:NCH])
                        v.tensor_copy(dd[:, 3 * (1 - d):3 * (1 - d) + 1], d1[:, 0:1])
                        v.tensor_tensor(a, r_kkn, a, ALU.mult).then_inc(q, 1)
                    elif step == "beta":
                        own(f"arr_{d}")
                        v.tensor_tensor(r_beta, a, r_e1, ALU.mult).then_inc(q, 1)
                    elif step == "rh":
                        own("FG_0")
                        v.tensor_tensor(rh, b3(r_a), b3(big[:, it + T_R, :]), ALU.mult).then_inc(q, 1)

                for step in ("cum", "ht", "q", "m", "kd1", "kd", "arr", "beta"):
                    prepare(step, 0)
                for d in range(2):
                    n = lambda a, d=d: f"{a}_{d}"
                    for u in range(NU):
                        dve.wait_ge(b_pe, V(BPE, n(f"pr{u}")))
                        v.tensor_tensor(r_u4[:, u, :, :].rearrange("p m n -> p (m n)"), bank(4 + u % 4), r_mask[d], ALU.mult
                                        ).then_inc(BDV.sem(n(f"U{u}")), 1)
                        if u == 1:
                            v.tensor_copy(r_t, ident.unsqueeze(1).to_broadcast([P, NU, P]))
                        elif u == 3:
                            v.tensor_copy(r_tt, ident.unsqueeze(1).to_broadcast([P, NU, P]))
                    dve.wait_ge(b_pe, V(BPE, n("A")))
                    ma = r_mask[1 - d][:, 0:P].unsqueeze(1)
                    for q, (a, b) in enumerate(((0, 4), (4, 5), (5, 9), (9, 10))):
                        ins = v.tensor_tensor(r_am[:, a:b, :], bank(q)[:, 0:(b - a) * P].rearrange("p (u n) -> p u n", n=P),
                                              ma.to_broadcast([P, b - a, P]), ALU.mult)
                    ins.then_inc(BDV.sem(n("Am")), 1)
                    own(n("Am"))
                    hp, hn, mp, mn = sides(d)
                    wide = lambda m, lev, k: m[:, lev, :].unsqueeze(1).to_broadcast([P, k, HD])
                    for g in GS:
                        us = slice(*GROUPS[g])
                        nu = us.stop - us.start
                        v.tensor_tensor(r_p[:, us, :], level_cols(r_am[:, us, :], 0, hp)[:, :, :, 0], wide(mp, 0, nu), ALU.mult)
                        v.tensor_tensor(r_n[:, us, :], r_u4[:, us, 0, :].rearrange("p u (k two) -> p u k two", two=2)[:, :, :, hn],
                                        wide(mn, 0, nu), ALU.mult).then_inc(BDV.sem(n(f"id{g}")), 1)
                        own(n(f"id{g}"))
                        tc, ttc = level_cols(r_t[:, us, :], 0, hp)[:, :, :, 0], level_cols(r_tt[:, us, :], 0, hn)[:, :, :, 0]
                        v.tensor_tensor(tc, tc, r_p[:, us, :], ALU.subtract)
                        v.tensor_tensor(ttc, ttc, r_n[:, us, :], ALU.subtract).then_inc(BDV.sem(n(f"T0{g}")), 1)
                    done = 0
                    for k, lev, g in LV:
                        if k == "X":
                            continue
                        us = slice(*GROUPS[g])
                        nu = us.stop - us.start
                        dve.wait_ge(b_pe, V(BPE, n(f"{k}{lev}{g}")))
                        if k == "P":
                            dst = r_p[:, us, :].rearrange("p u (k b) -> p u k b", b=1 << lev)
                            m = mp[:, lev, :].rearrange("p (k b) -> p k b", b=1 << lev).unsqueeze(1)
                            v.tensor_tensor(dst, level_cols(lv_bank(k, g, P), lev, hp), m.to_broadcast([P, nu, HD >> lev, 1 << lev]),
                                            ALU.mult).then_inc(BDV.sem(n(f"pn{lev}{g}")), 1)
                        elif k == "N":
                            v.tensor_tensor(r_n[:, us, :], lv_bank(k, g, HD), wide(mn, lev, nu), ALU.mult
                                            ).then_inc(BDV.sem(n(f"pn{lev}{g}")), 1)
                        else:
                            src = lv_bank(k, g, HD).rearrange("p u (k b) -> p u k b", b=1 << lev)
                            dst = level_cols(r_t[:, us, :], lev, hp) if k == "Q" else level_cols(r_tt[:, us, :], lev, hn)
                            v.tensor_tensor(dst, dst, src, ALU.subtract).then_inc(BDV.sem(n(f"t{lev}{g}")), 1)
                        if d == 0:
                            for step in EARLY.get(done, []):
                                prepare(step, 1)
                        elif done == KK_AT[0]:
                            kk_product(it + 1, BDV.sem("kkmul+"))
                        done += 1
                    dve.wait_ge(b_pe, V(BPE, n("FG")))
                    order = chunks(d)
                    for r in (slice(0, HD), slice(HD, P)):
                        v.tensor_tensor(r_ft2[r, :, r], bank(3)[r, 0:2 * HD].rearrange("p (c n) -> p c n", n=HD),
                                        r_eye2[r].unsqueeze(1).to_broadcast([HD, 2, HD]), ALU.add)
                        v.tensor_tensor(r_ft1[r, r], bank(3)[r, 2 * HD:3 * HD], r_eye2[r], ALU.add)
                    v.tensor_tensor(r_g, bank(4)[:, 0:NCH * HD].rearrange("p (c n) -> p c n", n=HD),
                                    r_dd[d].unsqueeze(2).to_broadcast([P, NCH, HD]), ALU.mult)
                    v.tensor_tensor(r_rhop.rearrange("p (c n) -> p c n", n=P), bank(5).rearrange("p (c n) -> p c n", n=P),
                                    r_ar[:, 0:NB, 1, :], ALU.add)
                    f = order[0]
                    v.tensor_scalar(r_z[:, f, :], r_s0t[:, it + BT * d, :], r_d1[d][:, f:f + 1], None, ALU.mult
                                    ).then_inc(BDV.sem(n("FG")), 1)
                    for i in range(3):
                        c, nx = order[i], order[i + 1]
                        dve.wait_ge(b_pe, V(BPE, n(f"S{i}")))
                        if i == 0:
                            own(n("FG"))
                        v.scalar_tensor_tensor(out=r_z[:, nx, :], in0=bank(7)[:, i * HD:(i + 1) * HD], scalar=r_dd[d][:, c:c + 1],
                                               in1=r_g[:, c, :], op0=ALU.mult, op1=ALU.add).then_inc(BDV.sem(n(f"Z{i}")), 1)
                    if d == 0:
                        prepare("rh", 1)
                dve.wait_ge(b_act, V(BAC, "kkroot+"))
                kk_norm([BDV.sem(x) for x in ("kkmax+", "kkrec+", "kkn+")], [V(BDV, x) for x in ("kkmax+", "kkrec+")])
                dve.wait_ge(b_pe, V(BPE, "Y_1"))
                dve.wait_ge(b_act, V(BAC, "y0"))
                v.tensor_tensor(r_y[:, 0:LAT], r_y[:, 0:LAT], bank(0), ALU.add)
                v.tensor_tensor(r_y[:, LAT:TOK], r_y[:, LAT:TOK], bank(1)[:, 0:P], ALU.add).then_inc(BDV.sem("y1"), 1)
                v.scalar_tensor_tensor(out=r_e2, in0=big[:, it + T_R, :], scalar=cols3[:, it + C_RK, :], in1=r_kds,
                                       op0=ALU.mult, op1=ALU.mult).then_inc(BDV.sem("bn"), 1)
                dve.wait_ge(b_pe, V(BPE, "bs"))
                v.tensor_tensor(halves(r_bonus), pp[1][:, :, 0:HALF], halves(r_v), ALU.mult).then_inc(BDV.sem("bonus"), 1)
                dve.wait_ge(b_pe, V(BPE, "mu"))
                v.scalar_tensor_tensor(out=halves(r_cum), in0=pp[3][:, :, 0:HALF], scalar=-1.0 / HD, in1=halves(r_y),
                                       op0=ALU.mult, op1=ALU.add).then_inc(BDV.sem("yc"), 1)
                dve.wait_ge(b_act, V(BAC, "sd"))
                v.reciprocal(r_e1, r_e1).then_inc(BDV.sem("rs"), 1)
                own("rs")
                v.tensor_tensor(r_cum, r_cum, r_e1, ALU.mult).then_inc(BDV.sem("yn"), 1)
                own("yn")
                v.tensor_scalar(r_cum, r_cum, cols3[:, it + C_GNW, :], cols3[:, it + C_GNB, :], ALU.mult, ALU.add
                                ).then_inc(BDV.sem("yg"), 1)
                own("yg")
                v.tensor_tensor(r_cum, r_cum, r_bonus, ALU.add).then_inc(BDV.sem("yb"), 1)
                own("yb")
                v.tensor_tensor(big[:, it + T_R, :], r_cum, r_gate, ALU.mult).then_inc(BDV.sem("yo"), 1)

        LAM_INIT = 0.8 - 0.6 * math.exp(-0.3)
        c_keys, c_q, c_qp = hh[:, 0:640], hh[:, 640:1152], hh[:, 1152:1280]
        c_v = hh[:, 1280:1920]
        c_vtok = hh[:, 1920:2560].rearrange("p (c n) -> p c n", n=P)
        c_kout, c_vpast, c_kpast = hh[:, 2560:2688], hh[:, 2688:2816], hh[:, 2816:2944]
        c_t1 = hh[:, 2944:3968].rearrange("p (a n) -> p a n", a=2)
        c_t2 = hh[:, 3968:4992].rearrange("p (a n) -> p a n", a=2)
        NQ = NB + 1
        c_mxa, c_mxb, c_mx, c_neg, c_da, c_db, c_den, c_rd = (
            hh[:, 4992 + 2 * NQ * i:4992 + 2 * NQ * (i + 1)].rearrange("p (b m) -> p b m", m=2) for i in range(8))
        c_e = hl[:, 0:2560].rearrange("p (q m n) -> p q m n", q=2, m=2)
        c_a = hl[:, 2560:3840].rearrange("p (q n) -> p q n", q=2)
        c_t = hl[:, 3840:4480]
        c_at = wh[:, 0:2560].rearrange("p (i n) -> p i n", i=5)
        c_atp = wh[:, 2560:2688]
        c_o, c_sq = wh[:, 2688:3328], wh[:, 3328:3968]
        c_rs = wl[:, 0:640]
        c_lq = wl[:, 640:896].rearrange("p (a n) -> p a n", n=HD)
        c_lp = wl[:, 896:1024].rearrange("p (a n) -> p a n", n=HD)
        c_ls, c_le = wl[:, 1024:1026], wl[:, 1026:1028]
        c_kp = wl[:, 1032:1160]
        c_l1 = wl[:, 1160:1160 + NQ]
        nlam, csub = small[:, 28:29], small[:, 29:30]

        c_loadv = sem("c_loadv")
        c_load, c_lam, c_pe, c_act, c_dve, c_out = (sem(f"c_{n}") for n in ("load", "lam", "pe", "act", "dve", "out"))
        ORDER = [("s", 0), ("s", 1), ("t", 0), ("s", 2), ("t", 1), ("s", 3), ("t", 2), ("s", 4), ("t", 3), ("t", 4)]
        S_, T_ = (lambda *bs: [("s", b) for b in bs]), (lambda *bs: [("t", b) for b in bs])
        ORDER_DV = S_(0, 1) + T_(0, 1) + [x for b in (2, 3, 4) for x in S_(b) + T_(b)]
        ORDER_AC = S_(0, 1) + T_(0, 1) + [x for b in (2, 3, 4) for x in S_(b) + T_(b)]

        def c_steps(q, names, extra, own_end=()):
            after = [n for n in names if n[-1] == "+"][-1]
            credit = 0 if q is c_pe else len(names) - 1 - names.index(after)
            first = Steps(q, [n for n in names if n[-1] != "-"], extra + credit)
            main = Steps(q, names, first.before(1) - len(names))
            tail = Steps(q, [n for n in names if n[-1] != "+"] + list(own_end), main.before(CH - 1))
            return (first, main, tail), credit

        def c_names(order, s_names, t_names, at, ahead, behind=()):
            out = []
            for a, b in order:
                if (a, b) == at:
                    out += ahead
                out += [n + str(b) for n in (s_names if a == "s" else t_names)]
                if (a, b) == ("s", 0):
                    out += behind
            return out

        CPE, _ = c_steps(c_pe, c_names(ORDER, ["sc"], ["tr"], ("s", 4), ["rot+"]) + ["pv", "kt+", "vt+", "ms"], 3)
        CAC, act_credit = c_steps(c_act, c_names(ORDER_AC, ["ex"], ["at"], ("t", 4), ["cp+"]) + ["o", "sq", "kt+", "vt+", "rt"], 4)
        CDV, dve_credit = c_steps(c_dve, c_names(ORDER_DV, ["mx", "m2", "ng"], ["dn", "rd", "lm", "tm", "A"], ("s", 4),
                                                 ["r1+", "r2+"], ["rc-", "fin-"]), 6, ["rc", "fin"])

        def c_turns(eng, turn):
            def run(h, which):
                def S(steps, name):
                    return steps[which].sem(name)

                def V(steps, name):
                    return steps[which].value(name, h if which == 1 else 0)

                def B(steps, name=None):
                    m = steps[1]
                    back = len(m.names) - 1 - m.index[name] if name else 0
                    return m.before(h) - back if which == 1 else steps[which].offset - back

                turn(h, S, V, B, which == 0, which == 2)

            run(0, 0)
            with eng.Fori(1, CH - 1) as h:
                run(h, 1)
            run(CH - 1, 2)

        def c_main(b):
            return pp[2 * (b % 2)]

        def c_rest(b, m):
            return pp[2 * (b % 2) + 1][:, m, 0:P]

        def c_turn(b, i):
            return pp[2 * (b % 2) + 1][:, i // 3, (i % 3 + 1) * P:(i % 3 + 2) * P]

        def sp_attn_c(sp):
            sp.wait_ge(slab_used, IN_C + C_TILES + RING)
            for i, name in enumerate(("c_lq1", "c_lq2", "c_lk1", "c_lk2")):
                sp.dma_start(c_lq[:, i, :], T[name].to_broadcast([P, HD])).then_inc(c_lam, 16)
            kc = T["cache_c_k"][0, 0]
            vc = T["cache_c_v"][0, 0]
            sp.dma_start(c_kpast, kc[:, 0, :]).then_inc(c_load, 16)
            sp.dma_start(c_vpast, vc[:, 0, :]).then_inc(c_loadv, 16)

            def rows_out(h):
                sp.dma_start(T["new_c_k"][0, 0][:, h, :], c_kout).then_inc(c_out, 16)
                sp.dma_start(T["new_c_v"][0, 0][:, h, :], c_vtok[:, 4, :]).then_inc(c_out, 16)

            def turn(h, S, V, B, first, last):
                sp.wait_ge(c_act, B(CAC, "vt+"))
                rows_out(h)
                sp.wait_ge(c_out, 32 * h + 64)
                if not last:
                    sp.dma_start(c_kpast, kc[:, h + 1, :]).then_inc(c_load, 16)
                    sp.wait_ge(c_pe, V(CPE, "pv"))
                    sp.dma_start(c_vpast, vc[:, h + 1, :]).then_inc(c_loadv, 16)

            c_turns(sp, turn)

        def pe_attn_c(pe):
            pe.wait_ge(pair_free, IN_C + C_TILES + RING)

            def rotate(h, q):
                nc.tensor.matmul(pp[0][:, 0, :], rot, big[:, h, 0:LAT], start=True, stop=True)
                nc.tensor.matmul(pp[0][:, 1, :], rot, big[:, h + CH, 0:LAT], start=True, stop=True).then_inc(q, 1)

            def turn_keys(q):
                nc.tensor.transpose(pp[1][:, 0, 0:P], c_kpast, ident)
                nc.tensor.transpose(pp[1][:, 0, P:2 * P], c_kp, ident).then_inc(q, 1)

            def turn_values(q):
                for c in range(NCH):
                    ins = nc.tensor.transpose(pp[0][:, c // 4, c % 4 * P:c % 4 * P + P], c_v[:, c * P:(c + 1) * P], ident)
                ins.then_inc(q, 1)

            rotate(0, c_pe)
            pe.wait_ge(c_act, 2)
            pe.wait_ge(c_load, 16)
            turn_keys(c_pe)
            pe.wait_ge(c_dve, 6)
            turn_values(c_pe)

            def turn(h, S, V, B, first, last):
                for kind, b in ORDER:
                    if (kind, b) == ("s", 4) and not last:
                        rotate(h + 1, S(CPE, "rot+"))
                    if kind == "s":
                        if b == 0:
                            pe.wait_ge(c_dve, B(CDV, "r2+"))
                            pe.wait_ge(c_act, B(CAC, "vt+"))
                        elif b == 1:
                            pe.wait_ge(c_act, B(CAC))
                        else:
                            pe.wait_ge(c_act, V(CAC, f"at{b - 2}"))
                        for m in range(2):
                            r = slice(m * HD, m * HD + HD)
                            if b < NB:
                                q = c_q[r, b * P:(b + 1) * P]
                                nc.tensor.matmul(c_main(b)[:, m, :], q, c_keys[r, 0:512], start=True, stop=True)
                                ins = nc.tensor.matmul(c_rest(b, m), q, c_keys[r, 512:640], start=True, stop=True)
                            else:
                                ins = nc.tensor.matmul(c_rest(b, m), c_qp[r, :], c_kp[r, :],
                                                       start=True, stop=True)
                        ins.then_inc(S(CPE, f"sc{b}"), 1)
                    else:
                        pe.wait_ge(c_dve, V(CDV, f"A{b}"))
                        for i in range(5 if b < NB else 1):
                            ins = nc.tensor.transpose(c_turn(b, i), c_a[:, b % 2, i * P:(i + 1) * P], ident)
                        ins.then_inc(S(CPE, f"tr{b}"), 1)
                pe.wait_ge(c_act, V(CAC, "at4"))
                pe.wait_ge(c_loadv, 16 * h + 16)
                for i in range(5):
                    nc.tensor.matmul(pp[2][:, 0, :], c_vtok[:, i - 1, :] if i else c_vpast, c_at[:, i, :],
                                     start=(i == 0), stop=(i == 4))
                nc.tensor.matmul(pp[2][:, 1, 0:P], c_vtok[:, 4, :], c_atp, start=True, stop=True).then_inc(S(CPE, "pv"), 1)
                if not last:
                    pe.wait_ge(c_load, 16 * h + 32)
                    turn_keys(S(CPE, "kt+"))
                    pe.wait_ge(c_dve, V(CDV, "r2+"))
                    turn_values(S(CPE, "vt+"))
                pe.wait_ge(c_act, V(CAC, "sq"))
                for c in range(2):
                    ins = nc.tensor.matmul(pp[3][:, c, 0:HALF], mean_p, c_sq[:, c * HALF:(c + 1) * HALF], start=True, stop=True)
                ins.then_inc(S(CPE, "ms"), 1)

            c_turns(pe, turn)

        def act_attn_c(act):
            act.wait_ge(c_dve, 2)
            act.wait_ge(pair_free, IN_C + C_TILES + RING)
            nc.scalar.activation(c_le, c_ls, ACT.Exp).then_inc(c_act, 1)

            def copies(h, q):
                nc.scalar.activation(c_qp, big[:, h, LAT:TOK], ACT.Copy)
                nc.scalar.activation(c_kp, big[:, h + CH, LAT:TOK], ACT.Copy)
                nc.scalar.activation(c_v, big[:, h + 2 * CH, :], ACT.Copy).then_inc(q, 1)

            def keys(q):
                nc.scalar.activation(c_keys[:, 0:P], pp[1][:, 0, 0:P], ACT.Copy)
                nc.scalar.activation(c_kout, pp[1][:, 0, P:2 * P], ACT.Copy).then_inc(q, 1)

            def values(q):
                nc.scalar.activation(c_vtok[:, 0:4, :], pp[0][:, 0, :].rearrange("p (c n) -> p c n", n=P), ACT.Copy)
                nc.scalar.activation(c_vtok[:, 4, :], pp[0][:, 1, 0:P], ACT.Copy).then_inc(q, 1)

            copies(0, c_act)
            act.wait_ge(c_pe, 2)
            keys(c_act)
            act.wait_ge(c_pe, 3)
            values(c_act)
            nc.scalar.activation(c_le, c_ls, ACT.Exp).then_inc(c_act, act_credit)

            def turn(h, S, V, B, first, last):
                for kind, b in ORDER_AC:
                    if (kind, b) == ("t", 4) and not last:
                        act.wait_ge(c_pe, V(CPE, "sc4"))
                        copies(h + 1, S(CAC, "cp+"))
                    if kind == "s":
                        act.wait_ge(c_dve, V(CDV, f"ng{b}"))
                        for m in range(2):
                            bias = c_neg[:, b, m:m + 1]
                            if b < NB:
                                nc.scalar.activation(c_e[:, b % 2, m, 0:512], c_main(b)[:, m, :], ACT.Exp, bias=bias, scale=SCALE,
                                                     accum_out=c_da[:, b, m:m + 1])
                                ins = nc.scalar.activation(c_e[:, b % 2, m, 512:640], c_rest(b, m), ACT.Exp,
                                                           bias=bias, scale=SCALE, accum_out=c_db[:, b, m:m + 1])
                            else:
                                ins = nc.scalar.activation(c_e[:, b % 2, m, 0:P], c_rest(b, m), ACT.Exp,
                                                           bias=bias, scale=SCALE, accum_out=c_den[:, b, m:m + 1])
                        ins.then_inc(S(CAC, f"ex{b}"), 1)
                    else:
                        act.wait_ge(c_pe, V(CPE, f"tr{b}"))
                        if b < NB:
                            ps = pp[2 * (b % 2) + 1]
                            nc.scalar.activation(c_at[:, 0:3, b * P:(b + 1) * P], ps[:, 0, P:4 * P].rearrange(
                                "p (i n) -> p i n", n=P), ACT.Copy)
                            nc.scalar.activation(c_at[:, 3:5, b * P:(b + 1) * P], ps[:, 1, P:3 * P].rearrange(
                                "p (i n) -> p i n", n=P), ACT.Copy).then_inc(S(CAC, f"at{b}"), 1)
                        else:
                            nc.scalar.activation(c_atp, c_turn(b, 0), ACT.Copy).then_inc(S(CAC, "at4"), 1)
                act.wait_ge(c_pe, V(CPE, "pv"))
                if not first:
                    act.wait_ge(c_dve, V(CDV, "fin-"))
                nc.scalar.activation(c_o[:, 0:LAT], pp[2][:, 0, :], ACT.Copy)
                nc.scalar.activation(c_o[:, LAT:TOK], pp[2][:, 1, 0:P], ACT.Copy).then_inc(S(CAC, "o"), 1)
                act.wait_ge(c_act, V(CAC, "o"))
                nc.scalar.activation(c_sq, c_o, ACT.Square).then_inc(S(CAC, "sq"), 1)
                if not last:
                    act.wait_ge(c_pe, V(CPE, "kt+"))
                    keys(S(CAC, "kt+"))
                    act.wait_ge(c_pe, V(CPE, "vt+"))
                    values(S(CAC, "vt+"))
                act.wait_ge(c_pe, V(CPE, "ms"))
                nc.scalar.activation(halves(c_rs), pp[3][:, :, 0:HALF], ACT.Sqrt, bias=eps[:, 2:3]).then_inc(S(CAC, "rt"), 1)

            c_turns(act, turn)

        def dve_attn_c(dve):
            v = nc.vector
            dve.wait_ge(c_lam, 64)
            v.tensor_tensor(c_lp, c_lq[:, 0:2, :], c_lq[:, 2:4, :], ALU.mult).then_inc(c_dve, 1)
            dve.wait_ge(c_dve, 1)
            v.tensor_reduce(c_ls, c_lp, AX.X, ALU.add).then_inc(c_dve, 1)
            dve.wait_ge(c_act, 1)
            v.tensor_scalar(nlam, c_le[:, 1:2], -LAM_INIT, None, ALU.add)
            v.tensor_scalar(csub, col(C_SUB), 1.0 - LAM_INIT, None, ALU.mult).then_inc(c_dve, 1)
            dve.wait_ge(c_dve, 3)
            v.tensor_tensor(nlam, nlam, c_le[:, 0:1], ALU.subtract).then_inc(c_dve, 1)

            def products(h, waits, q):
                v.tensor_tensor(c_t1[:, 0, :], big[:, h, 0:LAT], cos, ALU.mult)
                v.tensor_tensor(c_t1[:, 1, :], big[:, h + CH, 0:LAT], cos, ALU.mult)
                dve.wait_ge(c_pe, waits)
                v.tensor_tensor(c_t2, pp[0][:, :, :], sin.unsqueeze(1).to_broadcast([P, 2, LAT]), ALU.mult).then_inc(q, 1)

            def rotated(q):
                v.tensor_tensor(c_q, c_t1[:, 0, :], c_t2[:, 0, :], ALU.add)
                v.tensor_tensor(c_keys[:, P:TOK], c_t1[:, 1, :], c_t2[:, 1, :], ALU.add).then_inc(q, 1)

            def finish(h, S, mark, own):
                v.reciprocal(c_rs, c_rs).then_inc(S(CDV, "rc" + mark), 1)
                own("rc" + mark)
                v.scalar_tensor_tensor(out=big[:, h, :], in0=c_o, scalar=csub, in1=c_rs, op0=ALU.mult, op1=ALU.mult
                                       ).then_inc(S(CDV, "fin" + mark), 1)

            products(0, 1, c_dve)
            dve.wait_ge(c_dve, 5)
            rotated(c_dve)
            v.memset(small[:, 30:31], 0.0).then_inc(c_dve, dve_credit)

            def turn(h, S, V, B, first, last):
                def own(name):
                    dve.wait_ge(c_dve, V(CDV, name))

                dve.wait_ge(c_dve, B(CDV))
                for kind, b in ORDER_DV:
                    if (kind, b) == ("s", 4) and not last:
                        products(h + 1, V(CPE, "rot+"), S(CDV, "r1+"))
                        own("r1+")
                        rotated(S(CDV, "r2+"))
                    if kind == "s":
                        dve.wait_ge(c_pe, V(CPE, f"sc{b}"))
                        if b < NB:
                            v.tensor_reduce(c_mxa[:, b, :], c_main(b)[:, :, :], AX.X, ALU.max)
                        v.tensor_reduce(c_mxb[:, b, :], pp[2 * (b % 2) + 1][:, :, 0:P], AX.X, ALU.max
                                        ).then_inc(S(CDV, f"mx{b}"), 1)
                        own(f"mx{b}")
                        v.tensor_tensor(c_mx[:, b, :], (c_mxa if b < NB else c_mxb)[:, b, :], c_mxb[:, b, :], ALU.max
                                        ).then_inc(S(CDV, f"m2{b}"), 1)
                        own(f"m2{b}")
                        v.tensor_scalar(c_neg[:, b, :], c_mx[:, b, :], -SCALE, None, ALU.mult).then_inc(S(CDV, f"ng{b}"), 1)
                        if b == 0 and not first:
                            dve.wait_ge(c_act, B(CAC))
                            finish(h - 1, S, "-", own)
                    else:
                        n = TOK if b < NB else P
                        dve.wait_ge(c_act, V(CAC, f"ex{b}"))
                        if b < NB:
                            v.tensor_tensor(c_den[:, b, :], c_da[:, b, :], c_db[:, b, :], ALU.add).then_inc(S(CDV, f"dn{b}"), 1)
                            own(f"dn{b}")
                        else:
                            v.tensor_copy(c_da[:, b, :], c_den[:, b, :]).then_inc(S(CDV, f"dn{b}"), 1)
                        v.reciprocal(c_rd[:, b, :], c_den[:, b, :]).then_inc(S(CDV, f"rd{b}"), 1)
                        own(f"rd{b}")
                        v.tensor_tensor(c_l1[:, b:b + 1], c_rd[:, b, 1:2], nlam, ALU.mult).then_inc(S(CDV, f"lm{b}"), 1)
                        own(f"lm{b}")
                        v.tensor_scalar(c_t[:, 0:n], c_e[:, b % 2, 1, 0:n], c_l1[:, b:b + 1], None, ALU.mult
                                        ).then_inc(S(CDV, f"tm{b}"), 1)
                        own(f"tm{b}")
                        v.scalar_tensor_tensor(out=c_a[:, b % 2, 0:n], in0=c_e[:, b % 2, 0, 0:n], scalar=c_rd[:, b, 0:1],
                                               in1=c_t[:, 0:n], op0=ALU.mult, op1=ALU.add).then_inc(S(CDV, f"A{b}"), 1)
                if last:
                    dve.wait_ge(c_act, V(CAC, "rt"))
                    finish(h, S, "", own)

            c_turns(dve, turn)

        MIXED = {0: [(b_dve, BDV.before(BT)), (a_act, AAC.before(4))], 1: [(c_dve, CDV[2].value("fin")), (c_out, 32 * CH + 32)]}

        loads = []
        loads.append((base[:, :], T["t_base"]))
        loads.append((x_rows[:, 0:4, :], T["x_sample"][0].rearrange("(t p) n -> p t n", p=P)))
        loads.append((x_rows[:, 4, :], T["x_prompt"][0]))
        r0, r1, r2 = rows
        v = lambda a: a.rearrange("(r c) -> r c", c=P)
        loads.append((r0[C_NORM:C_NORM + 48, :], T["norms"].rearrange("l s (r c) -> (l s r) c", c=P)))
        loads.append((r0[C_FINAL:C_FINAL + 8, :], v(T["final_norm"])))
        loads.append((r0[C_MUP + 4:C_MUP + 19, :], v(T["b_mu_prev"][0])))
        loads.append((r0[C_MUN + 4:C_MUN + 19, :], v(T["b_mu_next"][0])))
        loads.append((r0[C_W0:C_W0 + 8, :], T["b_w0"][0].rearrange("d (r c) -> (d r) c", c=P)))
        loads.append((r0[C_A0:C_A0 + 8, :], T["b_a0"][0].rearrange("d (r c) -> (d r) c", c=P)))
        loads.append((r0[C_KK:C_KK + 4, :], v(T["b_k_k"][0])))
        loads.append((r0[C_KA:C_KA + 4, :], v(T["b_k_a"][0])))
        loads.append((r0[C_RK:C_RK + 4, :], T["b_r_k"][0].rearrange("(r two) c -> r (two c)", two=2)))
        o = -P
        loads.append((r1[C_GNW + o:C_GNW + o + 4, :], v(T["b_gn_w"][0])))
        loads.append((r1[C_GNB + o:C_GNB + o + 4, :], v(T["b_gn_b"][0])))
        loads.append((r1[C_SUB + o:C_SUB + o + 1, :], T["c_subln"]))
        loads.append((r1[C_COND + o:C_COND + o + 8, :], v(T["c"][0])))
        loads.append((r1[C_COND + o + 8:C_COND + o + 16, :], v(T["c_ctx"])))
        mb = T["mod_b"].rearrange("l (r c) -> (l r) c", c=P)
        loads.append((r1[C_MODB + o:C_MODB + o + 16, :], mb[P:P + 16, :]))
        loads.append((r2, mb[0:P, :]))
        loads.append((attn[:, :], T["t_attn"]))
        LOADS = len(loads)

        block = ctx.enter_context(nc.Block())

        @block.sync
        def _(sp):
            def weights(key, cnt):
                kind, l, f, b = key
                n0 = start[key]

                def slab(i, j, src):
                    sp.wait_ge(lo_full, 4 * i + (j + 1))
                    sp.dma_start(raw[:, j % RING, :, :], src).then_inc(raw_full[j % RING], 16)

                def section_rows(q, k, slot, less=0):
                    l2, c = (q + FIRST) // NMOD, (q + FIRST) % NMOD
                    sp.wait_ge(sec_acc, 2 * k + (18 * q + 1 + less))
                    src = T["mod_w"][l2].rearrange("(k p) n -> p k n", p=P)[:, k, c * D:(c + 1) * D]
                    sp.dma_start(sec_ring[:, slot, :], src).then_inc(sec_full[slot], 16)

                if kind == "up":
                    q = SECTIONS.get(key)
                    w1 = T["ffn_w1"][l, f].rearrange("(k p) (t w) -> p k t w", p=P, w=W)
                    w3 = T["ffn_w3"][l, f].rearrange("(k p) (t w) -> p k t w", p=P, w=W)
                    t0 = BLOCKS[b][0]
                    with sp.Fori(0, cnt // 4) as i:
                        for j in range(4):
                            src = (w1 if j % 2 == 0 else w3)[:, :, 2 * i + (t0 + j // 2), :]
                            slab(i, n0 + j, src)
                            if q is not None and j % 2:
                                section_rows(q, 2 * i + j // 2, j // 2)
                    if q is not None:
                        for k in range(cnt // 2, DT):
                            section_rows(q, k, k % 2)
                elif kind == "down":
                    r0 = min(BLOCKS[b][0], FT - DT) * P
                    w2 = T["ffn_w2"][l, f][r0:r0 + D, :].rearrange("(k p) (t w) -> p k t w", p=P, w=W)
                    if key in SECTIONS:
                        q = SECTIONS[key]
                        for j in range(cnt + 2):
                            if j < cnt:
                                slab(0, n0 + j, w2[:, :, j, :])
                            if j >= 2:
                                section_rows(q, j - 2, j % 2, -2 if j < 4 else 0)
                    else:
                        with sp.Fori(0, cnt // 4) as i:
                            for j in range(4):
                                slab(i, n0 + j, w2[:, :, 4 * i + j, :])
                else:
                    src = {("in", 0): "w_in_ab", ("in", 1): "w_in_c", ("out", 0): "w_out_ab", ("out", 1): "w_out_c"}
                    v = T[src[kind, l % 2]][l // 2].rearrange("(k p) (t w) -> p k t w", p=P, w=W)
                    for j in range(cnt):
                        c = AB_COLUMN[j] if (kind, l % 2) == ("in", 0) else j
                        slab(0, n0 + j, v[:, :, c, :])

            sp.wait_ge(s_zero, 2)
            for dst, src in loads:
                sp.dma_start(dst, src).then_inc(s_load, 16)
            mw = T["mod_w"][0].rearrange("(k p) (t w) -> p k t w", p=P, w=W)
            rows_of = T["mod_w"][0].rearrange("(k p) n -> p k n", p=P)
            with sp.Fori(0, COLUMNWISE * DT // 4) as i:
                for j in range(RING):
                    sp.wait_ge(m_used, 4 * i + (j + 1))
                    sp.dma_start(mod_ring[:, j, :, :], mw[:, :, 4 * i + j, :]).then_inc(mraw_full[j], 16)
                    if j % 2:
                        sp.wait_ge(gate_acc, 4 * i + j)
                        sp.dma_start(gate_ring[:, j // 2, :], rows_of[:, 2 * i + j // 2, COLUMNWISE * D:FIRST * D]
                                     ).then_inc(gate_full[j // 2], 16)
            sp.wait_ge(m_used, COLUMNWISE * DT + RING)
            for i in range(len(stages)):
                kind, l = stages[i][:2]
                if kind == "out":
                    if l % 2 == 0:
                        sp_attn_ab(sp)
                        sp_rwkv(sp)
                    else:
                        sp_attn_c(sp)
                weights(stages[i][:4], stages[i][4])
            n_out = 0
            for t in range(NCH):
                sp.wait_ge(y_ev, t + 1)
                dst = T["y_sample"][0, t * P:(t + 1) * P, :] if t < NB else T["y_prompt"][0]
                sp.dma_start(dst, x_rows[:, t, :]).then_inc(s_out, 16)
            sp.wait_ge(s_out, 16 * NCH)
            sp.wait_ge(a_out, 32)
            sp.wait_ge(b_out, 32 * BT + 32)
            sp.wait_ge(c_out, 32 * CH + 32)
        @block.scalar
        def _(act):
            def split_hi(i, j):
                act.wait_ge(raw_full[j % RING], 16 * i + (16 * (j // RING) + 16))
                act.wait_ge(slab_used, 4 * i + (j + 1))
                nc.scalar.activation(w_hi[:, j % RING, :, :], raw[:, j % RING, :, :], ACT.Copy).then_inc(hi_full, 1)

            act.wait_ge(s_load, 16 * LOADS)
            for t in range(NCH):
                act.wait_ge(s_tr, t + 1)
                dst = x[:, :, t * P:(t + 1) * P].rearrange("p (a b) c -> p a b c", a=2)
                nc.scalar.activation(dst, pp[t % 4][:, :, :].rearrange("p a (b c) -> p a b c", c=P), ACT.Copy).then_inc(s_ev, 1)
            act.wait_ge(s_tr, NCH + 1)
            nc.scalar.activation(cols[:, :], pp[1][:, 0, 0:C_END], ACT.Copy).then_inc(s_ev, 1)
            act.wait_ge(s_ev, NCH + 1)
            nc.scalar.activation(col(C_COND, 16), col(C_COND, 16), ACT.Silu).then_inc(s_cond, 1)

            def norm(k):
                l, s, u = norm_no[k]
                for t in range(DT):
                    if k:
                        act.wait_ge(pair_free, norm_at[k] + RING - DT + t + 1)
                    nc.scalar.activation(norm_t[:, t, :], x[:, t, :], ACT.Square).then_inc(n_sq, 1)
                act.wait_ge(n_sum, k + 1)
                nc.scalar.activation(halves(rt_t), pp[norm_at[k] % 4][:, :, 0:HALF], ACT.Sqrt, bias=eps[:, 0:1]).then_inc(n_root, 1)
                if k == NORMS - 1:
                    return
                sh = mod_at(l, 3 * s)
                for t in range(DT):
                    act.wait_ge(n_scaled, DT * k + t + 1)
                    for a, b, g in SEGS:
                        ins = nc.scalar.activation(h_hi[:, t, a:b], norm_t[:, t, a:b], ACT.Identity,
                                                   bias=mod[:, sh + t, g:g + 1])
                    ins.then_inc(n_hi, 1)

            def stage(i):
                kind, l, f, b, cnt = stages[i]
                key = stages[i][:4]
                n0 = start[key]
                ahead = LOOKAHEAD(i)
                if key in norm_before:
                    norm(norm_before[key])
                if FRESH(i):
                    split_hi(0, n0)
                    split_hi(0, n0 + 1)
                if kind == "up":
                    h0 = hid[key]
                    nc.scalar.preload_act_table(ACT.Silu)

                    def turn(i, last):
                        for e in range(2):
                            if not (last and e == 1 and not ahead):
                                for j in (2 * e + 2, 2 * e + 3):
                                    split_hi(i, n0 + j)
                            act.wait_ge(slab_used, 4 * i + (n0 + 2 * e + 1 + RING))
                            act.wait_ge(pair_free, 4 * i + (n0 + 2 * e + RING))
                            nc.scalar.activation(silu_t, pp[(n0 + 2 * e) % 4][:, :, 0:HALF], ACT.Silu).then_inc(silu_done, 1)
                            act.wait_ge(pair_free, 4 * i + (n0 + 2 * e + 2 + RING))
                            nc.scalar.activation(halves2(g_hi, 2 * i + e), prod_t, ACT.Copy).then_inc(ghi_done, 1)

                    loop_and_last(act, cnt // 4, turn)
                elif kind in ("down", "out"):
                    for j in range(cnt):
                        if j + 2 < cnt or ahead:
                            split_hi(0, n0 + j + 2)
                elif l % 2 == 0:
                    for j in range(cnt):
                        if j + 2 < cnt or ahead:
                            split_hi(0, n0 + j + 2)
                        act.wait_ge(slab_used, n0 + j + 1 + RING)
                        if j >= 2:
                            act.wait_ge(ab_shift, 3 * (j - 1))
                        else:
                            act.wait_ge(ab_pad, 1)
                        ps = pp[(n0 + j) % 4]
                        dst = praw[j % 2]
                        nc.scalar.activation(dst[:, 1:321], ps[:, 0, 0:HALF], ACT.Copy)
                        nc.scalar.activation(dst[:, 321:513], ps[:, 1, 0:LAT - HALF], ACT.Copy)
                        nc.scalar.activation(dst[:, 515:643], ps[:, 1, LAT - HALF:HALF], ACT.Copy).then_inc(pair_free, 1)
                else:
                    for j in range(cnt):
                        if j + 2 < cnt or ahead:
                            split_hi(0, n0 + j + 2)
                        act.wait_ge(slab_used, n0 + j + 1 + RING)
                        nc.scalar.activation(halves(big[:, j, :]), pp[(n0 + j) % 4][:, :, 0:HALF], ACT.Copy).then_inc(pair_free, 1)

            def split_out(m):
                for t in range(DT):
                    for q, value in MIXED[m]:
                        act.wait_ge(q, value)
                    nc.scalar.activation(h_hi[:, t, :], big[:, t, :], ACT.Copy).then_inc(o_hi, 1)

            for i in range(len(stages)):
                if stages[i][0] == "out":
                    (act_attn_ab if stages[i][1] % 2 == 0 else act_attn_c)(act)
                    if stages[i][1] % 2 == 0:
                        act_rwkv(act)
                    split_out(stages[i][1])
                stage(i)
            norm(NORMS - 1)
            for t in range(NCH):
                act.wait_ge(y_tr, t + 1)
                nc.scalar.activation(x_rows[:, t, :].rearrange("p (a b) -> p a b", a=2), pp[t % 4][:, :, :],
                                     ACT.Copy).then_inc(y_ev, 1)

        @block.vector
        def _(dve):
            def split_lo(i, j):
                dve.wait_ge(hi_full, 4 * i + (j + 1))
                nc.vector.tensor_tensor(w_lo[:, j % RING, :, :], raw[:, j % RING, :, :], f32(w_hi[:, j % RING, :, :]),
                                        ALU.subtract).then_inc(lo_full, 1)

            nc.vector.memset(R[:, 0:3 * P], 0.0).then_inc(s_zero, 1)
            nc.vector.memset(eps[:, 0:1], 1e-6)
            nc.vector.memset(eps[:, 1:2], 64e-5)
            nc.vector.memset(eps[:, 2:3], 1e-5).then_inc(s_zero, 1)
            for i, (q, c) in enumerate(((lo_full, 4), (slab_used, 4), (pair_free, 4), (m_used, 4), (m_taken, 2), (g_ready, 1), (b_out, 32), (c_out, 32),
                                    (sec_acc, 1), (gate_acc, 1))):
                nc.vector.memset(eps[:, 3 + i:4 + i], 0.0).then_inc(q, c)
            nc.vector.memset(ones, 1.0)
            dve.wait_ge(s_ev, NCH + 1)
            dve.wait_ge(s_cond, 1)
            c = [0, 0]

            def vec(ins):
                ins.then_inc(s_vec, 1)
                c[0] += 1

            def fin(ins):
                ins.then_inc(mod_fin, 1)
                c[1] += 1
                dve.wait_ge(mod_fin, c[1])

            def gain(l, s):
                sc = mod[:, mod_at(l, 3 * s + 1):mod_at(l, 3 * s + 1) + DT, :]
                g_in = col(C_NORM + (3 * l + s) * DT, DT).unsqueeze(2).to_broadcast([P, DT, 2])
                fin(nc.vector.tensor_tensor(sc, sc, g_in, ALU.mult))

            def halved(cc):
                return 0.5 if cc % 3 == 2 and cc // 3 != 1 else 1.0

            vec(nc.vector.tensor_copy(mod[:, 0:P, :], col(256, P).unsqueeze(2).to_broadcast([P, P, 2])))
            vec(nc.vector.tensor_copy(mod[:, P:P + 16, :], col(C_MODB, 16).unsqueeze(2).to_broadcast([P, 16, 2])))
            vec(nc.vector.tensor_tensor(c0, col(C_MUP, AB_TILES), col(C_MUN, AB_TILES), ALU.add))
            vec(nc.vector.tensor_scalar(kam, col(C_KA, 4), -1.0, 1.0, ALU.mult, ALU.add))
            dve.wait_ge(s_vec, c[0])
            vec(nc.vector.tensor_scalar(c0, c0, -1.0, 1.0, ALU.mult, ALU.add))
            for l in range(DEPTH):
                for cc in range(NMOD):
                    m = mod[:, mod_at(l, cc):mod_at(l, cc) + DT, :]
                    if cc % 3 == 1:
                        vec(nc.vector.tensor_scalar(m, m, 1.0, None, ALU.add))
                    elif halved(cc) != 1.0:
                        vec(nc.vector.tensor_scalar(m, m, halved(cc), None, ALU.mult))
            dve.wait_ge(s_vec, c[0])
            for g in range(2):
                nc.vector.memset(gate_sums[:, g, :], 0.0).then_inc(gate_acc, 1)
            for g in range(COLUMNWISE * DT // 4):
                for k in (2 * g, 2 * g + 1):
                    dve.wait_ge(gate_full[k % 2], 16 * (k // 2) + 16)
                    for h in range(2):
                        dve.wait_ge(gate_acc, 2 * k + h + 2)
                        sm = gate_sums[:, h, :]
                        nc.vector.scalar_tensor_tensor(out=sm, in0=gate_ring[:, k % 2, :], scalar=col(C_COND + DT * h + k),
                                                       in1=sm, op0=ALU.mult, op1=ALU.add).then_inc(gate_acc, 1)
                dve.wait_ge(m_used, 4 * g + 8)
                m = mod[:, 4 * g:4 * g + 4, :]
                nc.vector.scalar_tensor_tensor(out=m, in0=pp[2 + g % 2][:, 0, 0:8].rearrange("p (a b) -> p a b", b=2),
                                               scalar=halved(g // 2), in1=m, op0=ALU.mult, op1=ALU.add).then_inc(m_taken, 1)
            dve.wait_ge(m_taken, COLUMNWISE * DT // 4 + 2)
            gain(0, 0)
            dve.wait_ge(gate_sum, 1)
            m = mod[:, mod_at(0, COLUMNWISE):mod_at(0, COLUMNWISE) + DT, :]
            fin(nc.vector.scalar_tensor_tensor(out=m, in0=pp[1][:, 0, 0:2 * DT].rearrange("p (a b) -> p a b", b=2),
                                               scalar=halved(COLUMNWISE), in1=m, op0=ALU.mult, op1=ALU.add))

            def clear_sums(q):
                for g in range(2):
                    nc.vector.memset(sec_sum[:, q % 2, g, :], 0.0).then_inc(sec_acc, 1)

            def sum_rows(q, turn2, k, e):
                dve.wait_ge(sec_full[e], 16 * turn2 + (64 * q + 16))
                for g in range(2):
                    dve.wait_ge(sec_acc, sum_steps(q, k, g))
                    sm = sec_sum[:, q % 2, g, :]
                    nc.vector.scalar_tensor_tensor(out=sm, in0=sec_ring[:, e, :], scalar=cols3[:, k + (C_COND + DT * g), :],
                                                   in1=sm, op0=ALU.mult, op1=ALU.add).then_inc(sec_acc, 1)

            def take_section(q, ps):
                l2, cc = (q + FIRST) // NMOD, (q + FIRST) % NMOD
                m = mod[:, mod_at(l2, cc):mod_at(l2, cc) + DT, :]
                fin(nc.vector.scalar_tensor_tensor(out=m, in0=ps[:, 1, HALF:HALF + 2 * DT].rearrange("p (a b) -> p a b", b=2),
                                                   scalar=halved(cc), in1=m, op0=ALU.mult, op1=ALU.add))
                if cc % 3 == 1:
                    gain(l2, cc // 3)

            def norm(k):
                l, s, u = norm_no[k]
                dve.wait_ge(n_root, k + 1)
                nc.vector.reciprocal(rt_t, rt_t).then_inc(n_recip, 1)
                dve.wait_ge(n_recip, k + 1)
                last = k == NORMS - 1
                for t in range(DT):
                    for a, b, g in SEGS:
                        sc = col(C_FINAL + t) if last else mod[:, mod_at(l, 3 * s + 1) + t, g:g + 1]
                        ins = nc.vector.scalar_tensor_tensor(out=norm_t[:, t, a:b], in0=x[:, t, a:b], scalar=sc,
                                                             in1=rt_t[:, a:b], op0=ALU.mult, op1=ALU.mult)
                    ins.then_inc(n_scaled, 1)
                if last:
                    return
                sh = mod_at(l, 3 * s)
                for t in range(DT):
                    dve.wait_ge(n_hi, DT * k + t + 1)
                    for a, b, g in SEGS:
                        ins = nc.vector.scalar_tensor_tensor(out=h_lo[:, t, a:b], in0=norm_t[:, t, a:b],
                                                             scalar=mod[:, sh + t, g:g + 1], in1=f32(h_hi[:, t, a:b]),
                                                             op0=ALU.add, op1=ALU.subtract)
                    ins.then_inc(n_lo, 1)

            def stage(i):
                kind, l, f, b, cnt = stages[i]
                key = stages[i][:4]
                n0 = start[key]
                ahead = LOOKAHEAD(i)
                q = SECTIONS.get(key)
                if key in norm_before:
                    norm(norm_before[key])
                    if q is not None:
                        dve.wait_ge(n_lo, DT * norm_before[key] + DT)
                if FRESH(i):
                    split_lo(0, n0)
                    split_lo(0, n0 + 1)
                if q is not None:
                    clear_sums(q)
                if kind == "up":
                    h0 = hid[key]

                    def turn(i, last):
                        for e in range(2):
                            early = q is not None and last and e == 1 and cnt // 2 < DT
                            if early:
                                sum_rows(q, i, 2 * i + e, e)
                            if not (last and e == 1 and not ahead):
                                for j in (2 * e + 2, 2 * e + 3):
                                    split_lo(i, n0 + j)
                            dve.wait_ge(slab_used, 4 * i + (n0 + 2 * e + 2 + RING))
                            dve.wait_ge(silu_done, 2 * i + (h0 + e + 1))
                            dve.wait_ge(g_ready, 2 * i + (h0 + e + 1))
                            nc.vector.tensor_tensor(prod_t, silu_t, pp[(n0 + 2 * e + 1) % 4][:, :, 0:HALF],
                                                    ALU.mult).then_inc(pair_free, 2)
                            dve.wait_ge(ghi_done, 2 * i + (h0 + e + 1))
                            nc.vector.tensor_tensor(halves2(g_lo, 2 * i + e), prod_t, f32(halves2(g_hi, 2 * i + e)),
                                                    ALU.subtract).then_inc(g_ready, 1)
                            if q is not None and not early:
                                sum_rows(q, i, 2 * i + e, e)

                    loop_and_last(dve, cnt // 4, turn)
                    if q is not None:
                        for k in range(cnt // 2, DT):
                            sum_rows(q, k // 2, k, k % 2)
                elif kind in ("down", "out"):
                    gate = mod_at(l, 5 if kind == "out" else (2 if f == 0 else 8))
                    for j in range(cnt):
                        if j + 2 < cnt or ahead:
                            split_lo(0, n0 + j + 2)
                        if q is not None:
                            sum_rows(q, j // 2, j, j % 2)
                        dve.wait_ge(slab_used, n0 + j + 1 + RING)
                        if j == 0:
                            dve.wait_ge(pair_free, n0 + RING)
                        ps = pp[(n0 + j) % 4]
                        if kind == "down":
                            for q2 in sections_at(key, j):
                                take_section(q2, ps)
                        for (a, b2), src, g in (((0, HALF), ps[:, 0, 0:HALF], 0),
                                                ((HALF, LAT), ps[:, 1, 0:LAT - HALF], 0),
                                                ((LAT, TOK), ps[:, 1, LAT - HALF:HALF], 1)):
                            ins = nc.vector.scalar_tensor_tensor(out=x[:, j, a:b2], in0=src,
                                                                 scalar=mod[:, gate + j, g:g + 1], in1=x[:, j, a:b2],
                                                                 op0=ALU.mult, op1=ALU.add)
                        ins.then_inc(pair_free, 1)
                elif l % 2 == 0:
                    for q in range(2):
                        for z in (0, 513, 643):
                            w = 2 if z == 513 else 1
                            ins = nc.vector.memset(praw[q][:, z:z + w], 0.0)
                    ins.then_inc(ab_pad, 1)
                    for j in range(cnt):
                        if j + 2 < cnt or ahead:
                            split_lo(0, n0 + j + 2)
                        dve.wait_ge(pair_free, n0 + j + 1 + RING)
                        src = praw[j % 2]
                        for op in range(3):
                            if op:
                                dve.wait_ge(ab_shift, 3 * j + op)
                            for a, b2, o in ((0, LAT, 1), (LAT, TOK, 3)):
                                dst = big[:, j, a:b2]
                                if op == 0:
                                    ins = nc.vector.tensor_scalar(dst, src[:, a + o:b2 + o], c0[:, j:j + 1], None, ALU.mult)
                                else:
                                    d = -1 if op == 1 else 1
                                    mu = col((C_MUP if op == 1 else C_MUN) + j)
                                    ins = nc.vector.scalar_tensor_tensor(out=dst, in0=src[:, a + o + d:b2 + o + d], scalar=mu,
                                                                         in1=dst, op0=ALU.mult, op1=ALU.add)
                            ins.then_inc(ab_shift, 1)
                else:
                    for j in range(cnt):
                        if j + 2 < cnt or ahead:
                            split_lo(0, n0 + j + 2)

            def split_out(m):
                for t in range(DT):
                    dve.wait_ge(o_hi, DT * m + t + 1)
                    nc.vector.tensor_tensor(h_lo[:, t, :], big[:, t, :], f32(h_hi[:, t, :]), ALU.subtract).then_inc(o_lo, 1)

            for i in range(len(stages)):
                if stages[i][0] == "out":
                    (dve_attn_ab if stages[i][1] % 2 == 0 else dve_attn_c)(dve)
                    if stages[i][1] % 2 == 0:
                        dve_rwkv(dve)
                    split_out(stages[i][1])
                stage(i)
            norm(NORMS - 1)

        @block.tensor
        def _(pe):
            pe.wait_ge(s_load, 16 * LOADS)
            for t in range(NCH):
                if t == 4:
                    pe.wait_ge(s_ev, 1)
                for d in range(DT):
                    ins = nc.tensor.transpose(pp[t % 4][:, d // 4, (d % 4) * P:(d % 4 + 1) * P],
                                              x_rows[:, t, d * P:(d + 1) * P], ident)
                ins.then_inc(s_tr, 1)
            pe.wait_ge(s_ev, 2)
            for r in range(3):
                ins = nc.tensor.transpose(pp[1][:, 0, r * P:(r + 1) * P], rows[r], ident)
            ins.then_inc(s_tr, 1)
            pe.wait_ge(s_cond, 1)
            pe.wait_ge(s_ev, NCH + 1)
            cond = col(C_COND, 16).rearrange("p (g k) -> p k g", g=2)
            with pe.Fori(0, COLUMNWISE * DT // 8) as i:
                for j in range(8):
                    pe.wait_ge(mraw_full[j % RING], 32 * i + (16 * (j // RING) + 16))
                    if j % 4 == 0:
                        pe.wait_ge(m_taken, 2 * i + (j // 4 + 1))
                    for k in range(DT):
                        ins = nc.tensor.matmul(pp[2 + j // 4][:, 0, 2 * (j % 4):2 * (j % 4) + 2], mod_ring[:, j % RING, k, :],
                                               cond[:, k, :], start=(k == 0), stop=(k == DT - 1))
                    ins.then_inc(m_used, 1)
            pe.wait_ge(gate_acc, 2 * DT + 3)
            for t in range(DT):
                for g in range(2):
                    ins = nc.tensor.matmul(pp[1][:, 0, 2 * t + g:2 * t + g + 1], gate_sums[:, g, t * P:(t + 1) * P], ones,
                                           start=True, stop=True)
            ins.then_inc(gate_sum, 1)

            def norm(k):
                pair = pp[norm_at[k] % 4]
                if k == 0:
                    pe.wait_ge(m_taken, COLUMNWISE * DT // 4 + 2)
                else:
                    pe.wait_ge(pair_free, norm_at[k] + 1)
                for t in range(DT):
                    pe.wait_ge(n_sq, DT * k + t + 1)
                    for c in range(2):
                        ins = nc.tensor.matmul(pair[:, c, 0:HALF], mean_d, norm_t[:, t, c * HALF:(c + 1) * HALF],
                                               start=(t == 0), stop=(t == DT - 1))
                ins.then_inc(n_sum, 1)

            def slab(i, j, kts, k0, xh, xl, wait_tile, sections=()):
                pe.wait_ge(lo_full, 4 * i + (j + 1 + RING))
                pe.wait_ge(pair_free, 4 * i + (j + 1))
                ps = pp[j % 4]
                for k in range(kts):
                    if wait_tile:
                        wait_tile(k)
                    hi, lo = w_hi[:, j % RING, k + k0, :], w_lo[:, j % RING, k + k0, :]
                    for w, v in ((hi, xh), (hi, xl), (lo, xh)):
                        for c in range(2):
                            ins = nc.tensor.matmul(ps[:, c, 0:HALF], w, v[:, k, c * HALF:(c + 1) * HALF],
                                                   start=(k == 0 and w is hi and v is xh),
                                                   stop=(k == kts - 1 and w is lo))
                for q in sections:
                    pe.wait_ge(sec_acc, sum_steps(q, DT) + 1)
                    for t in range(DT):
                        for g in range(2):
                            c = HALF + 2 * t + g
                            ins = nc.tensor.matmul(ps[:, 1, c:c + 1], sec_sum[:, q % 2, g, t * P:(t + 1) * P], ones,
                                                   start=True, stop=True)
                ins.then_inc(slab_used, 1)

            def stage(i):
                kind, l, f, b, cnt = stages[i]
                key = stages[i][:4]
                n0 = start[key]
                if key in norm_before:
                    norm(norm_before[key])
                k0, kts = 0, DT
                if kind == "down":
                    kts = BLOCKS[b][1]
                    k0 = BLOCKS[b][0] - min(BLOCKS[b][0], FT - DT)
                    xh, xl = g_hi, g_lo
                    tile_ready = lambda k: pe.wait_ge(g_ready, hid[key] - kts + k + 2)
                elif kind == "out":
                    xh, xl = h_hi, h_lo
                    tile_ready = lambda k: pe.wait_ge(o_lo, DT * l + k + 1)
                else:
                    xh, xl = h_hi, h_lo
                    kk = norm_before.get(key)
                    tile_ready = None if kk is None else (lambda k: pe.wait_ge(n_lo, DT * kk + k + 1))
                looped = 0
                if not (kind == "down" and ("up", l, f, b) in SECTIONS):
                    looped = cnt // 4 * 4
                    with pe.Fori(0, cnt // 4) as i2:
                        for j in range(4):
                            slab(i2, n0 + j, kts, k0, xh, xl, tile_ready if j == 0 else None)
                else:
                    for j in range(cnt):
                        slab(0, n0 + j, kts, k0, xh, xl, tile_ready if j == 0 else None, sections_at(key, j))
                    looped = cnt
                for j in range(looped, cnt):
                    slab(0, n0 + j, kts, k0, xh, xl, None)

            for i in range(len(stages)):
                if stages[i][0] == "out":
                    (pe_attn_ab if stages[i][1] % 2 == 0 else pe_attn_c)(pe)
                    if stages[i][1] % 2 == 0:
                        pe_rwkv(pe)
                stage(i)
            norm(NORMS - 1)
            for t in range(NCH):
                if t == 0:
                    pe.wait_ge(n_scaled, DT * NORMS)
                if t == 4:
                    pe.wait_ge(y_ev, 1)
                for d in range(DT):
                    ins = nc.tensor.transpose(pp[t % 4][:, d // 4, (d % 4) * P:(d % 4 + 1) * P],
                                              norm_t[:, d, t * P:(t + 1) * P], ident)
                ins.then_inc(y_tr, 1)


_INS = ["x_prompt", "x_sample", "c", "c_ctx", "cache_a_k", "cache_a_v", "state_b_wkv", "cache_c_k", "cache_c_v", "norms",
        "mod_w", "mod_b", "ffn_w1", "ffn_w3", "ffn_w2", "w_in_ab", "w_out_ab", "a_sink", "b_mu_prev", "b_mu_next", "b_w0",
        "b_w2", "b_a0", "b_a2", "b_k_k", "b_k_a", "b_r_k", "b_g2", "b_gn_w", "b_gn_b", "w_in_c", "w_out_c", "c_lq1",
        "c_lk1", "c_lq2", "c_lk2", "c_subln", "final_norm"]
_OUTS = [("y_prompt", (1, CTX, D)), ("y_sample", (1, LAT, D)), ("new_a_k", (1, 1, CTX, 2, HD)),
         ("new_a_v", (1, 1, CTX, 2, HD)), ("new_b_wkv", (1, 1, 2, 8, HD, HD)), ("new_c_k", (1, 1, CTX, CH, P)),
         ("new_c_v", (1, 1, CTX, CH, P))]


def kernel(**inputs):
    import concourse.bacc as _bacc
    from concourse.bass_utils import run_bass_kernel_spmd as _run

    nc = _bacc.Bacc("TRN2", target_bir_lowering=False, num_devices=1)
    arrays, T = {}, {}
    for name in _INS:
        arrays[name] = np.ascontiguousarray(inputs[name])
    for name, a in zip(("t_base", "t_attn", "t_rwkv"), tables()):
        arrays[name] = np.ascontiguousarray(a)
    for name, a in arrays.items():
        T[name] = nc.dram_tensor(name, a.shape, mybir.dt.from_np(a.dtype), kind="ExternalInput").ap()
    for name, shape in _OUTS:
        T[name] = nc.dram_tensor(name, shape, F32, kind="ExternalOutput").ap()
    build(nc, T)
    r = _run(nc, [arrays], core_ids=[0])
    return tuple(r.results[0][name] for name, _ in _OUTS)
```
